# Optimizing a Trainium2 kernel written in Bass

```python
import math
import jax, jax.numpy as jnp
from jax import lax
import numpy as np

D_MODEL = 1024
BATCH = 1
SEQ = 256
DEPTH = 2

GLA_HEADS = 4
GLA_DK = 128
GLA_DV = 256
GLA_RANK = 16
GLA_TAU = 16.0
GLA_CHUNK = 64
DIL_PATTERN = ((128, 1), (512, 4), (2048, 16))
DIL_HEADS = 8
DIL_HD = 64
ROPE_THETA = 10000.0
N_EXPERTS = 16
N_GROUPS = 4
EXPERTS_PER_GROUP = N_EXPERTS // N_GROUPS
TOP_K = 2
D_FF = 1024
LN_EPS = 1e-5
RMS_EPS = 1e-6
DN_ALPHA = (2 * DEPTH) ** 0.25
DN_BETA = (8 * DEPTH) ** -0.25
NEG_INF = -1e30

GLA_QK_W = GLA_HEADS * GLA_DK
GLA_V_W = GLA_HEADS * GLA_DV
N_DIL = len(DIL_PATTERN)
DIL_GROUP_W = DIL_HEADS * DIL_HD
N_BRANCH = 2
SPLITS = (GLA_QK_W, GLA_QK_W, GLA_V_W, GLA_V_W, GLA_RANK,
          N_DIL * DIL_GROUP_W, N_DIL * DIL_GROUP_W, N_DIL * DIL_GROUP_W, N_BRANCH * D_MODEL)
V_BLOCKS = (2, 7)
D_IN = sum(SPLITS)
SPLIT_POINTS = tuple(sum(SPLITS[:i + 1]) for i in range(len(SPLITS) - 1))

kernel_name = "hybrid_gla_dilated_gated_moe_deepnorm"

def layer_norm(x, g, b):
    xf = x.astype(jnp.float32)
    mu = jnp.mean(xf, axis=-1, keepdims=True)
    var = jnp.mean(jnp.square(xf - mu), axis=-1, keepdims=True)
    y = (xf - mu) * lax.rsqrt(var + LN_EPS) * g.astype(jnp.float32) + b.astype(jnp.float32)
    return y.astype(x.dtype)

def rotary(x, positions):
    e = x.shape[-1]
    half = e // 2
    inv_freq = jnp.power(jnp.float32(ROPE_THETA), -jnp.arange(0, e, 2, dtype=jnp.float32) / e)
    ang = positions.astype(jnp.float32)[..., None] * inv_freq
    cos = jnp.cos(ang)[:, :, None, :]
    sin = jnp.sin(ang)[:, :, None, :]
    xf = x.astype(jnp.float32)
    x1, x2 = xf[..., :half], xf[..., half:]
    return jnp.concatenate([x1 * cos - x2 * sin, x2 * cos + x1 * sin], axis=-1).astype(x.dtype)

def gla_chunked(q, k, v, log_a):
    B, S, H, DK = q.shape
    DV = v.shape[-1]
    C = GLA_CHUNK
    N = S // C

    def chunks(t):
        return t.astype(jnp.float32).reshape(B, N, C, H, t.shape[-1]).transpose(0, 3, 1, 2, 4)

    qc = chunks(q) * (DK ** -0.5)
    kc = chunks(k)
    vc = chunks(v)
    b = jnp.cumsum(chunks(log_a), axis=3)
    b_end = b[:, :, :, -1:, :]
    q_t = qc * jnp.exp(b)
    k_t = kc * jnp.exp(-b)
    k_s = kc * jnp.exp(b_end - b)
    causal = jnp.tril(jnp.ones((C, C), dtype=bool))
    att = jnp.where(causal, jnp.einsum('bhnid,bhnjd->bhnij', q_t, k_t), 0.0)
    o_intra = jnp.einsum('bhnij,bhnjv->bhniv', att, vc)
    decay = jnp.exp(b_end[:, :, :, 0, :])

    def step(state, inp):
        q_n, k_n, v_n, d_n = inp
        o_n = jnp.einsum('bhcd,bhdv->bhcv', q_n, state)
        state = d_n[..., None] * state + jnp.einsum('bhcd,bhcv->bhdv', k_n, v_n)
        return state, o_n

    init = jnp.zeros((B, H, DK, DV), jnp.float32)
    xs = (jnp.moveaxis(q_t, 2, 0), jnp.moveaxis(k_s, 2, 0), jnp.moveaxis(vc, 2, 0), jnp.moveaxis(decay, 2, 0))
    _, o_inter = lax.scan(step, init, xs)
    o = o_intra + jnp.moveaxis(o_inter, 0, 2)
    return o.transpose(0, 2, 3, 1, 4).reshape(B, S, H, DV)

def dilated_group(q, k, v, window, dilation):
    B, S, H, E = q.shape
    steps = window // dilation
    L = S // dilation
    nb = -(-L // steps)
    Lp = nb * steps

    def to_sub(t):
        t = t.reshape(B, L, dilation, H, E).transpose(0, 2, 3, 1, 4)
        t = jnp.pad(t, ((0, 0), (0, 0), (0, 0), (0, Lp - L), (0, 0)))
        return t.reshape(B, dilation, H, nb, steps, E)

    qb, kb, vb = to_sub(q), to_sub(k), to_sub(v)

    def with_prev(t):
        prev = jnp.concatenate([jnp.zeros_like(t[:, :, :, :1]), t[:, :, :, :-1]], axis=3)
        return jnp.concatenate([prev, t], axis=4)

    kw, vw = with_prev(kb), with_prev(vb)
    s = jnp.einsum('bdhnqe,bdhnke->bdhnqk', qb, kw).astype(jnp.float32) * (E ** -0.5)
    qi = jnp.arange(steps)[:, None]
    kj = jnp.arange(2 * steps)[None, :]
    rel = steps + qi - kj
    band = (rel >= 0) & (rel <= steps)
    blk = jnp.arange(nb)[:, None, None]
    key_exists = (blk * steps - steps + kj[None]) >= 0
    mask = band[None] & key_exists
    s = jnp.where(mask, s, NEG_INF)
    m = jnp.max(s, axis=-1, keepdims=True)
    p = jnp.exp(s - m)
    l = jnp.sum(p, axis=-1, keepdims=True)
    o = jnp.einsum('bdhnqk,bdhnke->bdhnqe', p, vw.astype(jnp.float32)) / l
    lse = (m + jnp.log(l))[..., 0]
    o = o.reshape(B, dilation, H, Lp, E)[:, :, :, :L].transpose(0, 3, 1, 2, 4).reshape(B, S, H, E)
    lse = lse.reshape(B, dilation, H, Lp)[..., :L].transpose(0, 3, 1, 2).reshape(B, S, H)
    return o, lse

def dilated_branch(q, k, v, positions):
    B, S, _ = q.shape
    q = rotary(q.reshape(B, S, N_DIL * DIL_HEADS, DIL_HD), positions)
    k = rotary(k.reshape(B, S, N_DIL * DIL_HEADS, DIL_HD), positions)
    v = v.reshape(B, S, N_DIL * DIL_HEADS, DIL_HD)
    outs, lses = [], []
    for g, (window, dilation) in enumerate(DIL_PATTERN):
        sl = slice(g * DIL_HEADS, (g + 1) * DIL_HEADS)
        o, lse = dilated_group(q[:, :, sl], k[:, :, sl], v[:, :, sl], window, dilation)
        outs.append(o)
        lses.append(lse)
    w = jax.nn.softmax(jnp.stack(lses, axis=0), axis=0)
    o = jnp.sum(w[..., None] * jnp.stack(outs, axis=0), axis=0)
    return o.reshape(B, S, DIL_GROUP_W)

def grouped_moe(x, w_router, b_router, w_gate, w_up, w_down):
    B, S, _ = x.shape
    logits = jnp.einsum('bsd,de->bse', x, w_router).astype(jnp.float32) + b_router.astype(jnp.float32)
    probs = jax.nn.softmax(logits, axis=-1)
    pg = probs.reshape(B, S, N_GROUPS, EXPERTS_PER_GROUP)
    group_score = lax.top_k(pg, TOP_K)[0].sum(-1)
    g_sel = jnp.argmax(group_score, axis=-1)
    in_group = jnp.arange(N_GROUPS) == g_sel[..., None]
    cand = jnp.where(in_group[..., None], pg, -1.0).reshape(B, S, N_EXPERTS)
    vals, idx = lax.top_k(cand, TOP_K)
    gates = vals / jnp.sum(vals, axis=-1, keepdims=True)
    combine = jnp.sum(jax.nn.one_hot(idx, N_EXPERTS, dtype=jnp.float32) * gates[..., None], axis=-2)
    y = jnp.zeros((B, S, x.shape[-1]), jnp.float32)
    for e in range(N_EXPERTS):
        h = jax.nn.silu(x @ w_gate[e]) * (x @ w_up[e])
        y = y + combine[..., e:e + 1] * (h @ w_down[e]).astype(jnp.float32)
    return y.astype(x.dtype)

def setup_inputs(seed: int = 0) -> dict:
    key = jax.random.key(seed)
    ks = jax.random.split(key, 20)
    f32 = jnp.float32

    def nrm(k, shape, scale):
        return jax.random.normal(k, shape, f32) * scale

    x = nrm(ks[0], (BATCH, SEQ, D_MODEL), 1.0)
    offset = jax.random.randint(ks[1], (BATCH, 1), 0, SEQ)
    positions = (offset + jnp.arange(SEQ)[None, :]).astype(jnp.int32)
    col_scale = jnp.concatenate([jnp.full((n,), DN_BETA if i in V_BLOCKS else 1.0, f32)
                                 for i, n in enumerate(SPLITS)])
    w_in = nrm(ks[2], (DEPTH, D_MODEL, D_IN), D_MODEL ** -0.5) * col_scale
    w_alpha_up = nrm(ks[3], (DEPTH, GLA_RANK, GLA_QK_W), GLA_RANK ** -0.5)
    b_alpha = nrm(ks[4], (DEPTH, GLA_QK_W), 0.1)
    gla_norm = 1.0 + nrm(ks[5], (DEPTH, GLA_V_W), 0.02)
    w_gla_o = nrm(ks[6], (DEPTH, GLA_V_W, D_MODEL), GLA_V_W ** -0.5)
    w_att_o = nrm(ks[7], (DEPTH, DIL_GROUP_W, D_MODEL), DIL_GROUP_W ** -0.5)
    w_out = nrm(ks[8], (DEPTH, D_MODEL, D_MODEL), D_MODEL ** -0.5 * DN_BETA)
    ln1_g = 1.0 + nrm(ks[9], (DEPTH, D_MODEL), 0.02)
    ln1_b = nrm(ks[10], (DEPTH, D_MODEL), 0.02)
    w_router = nrm(ks[11], (D_MODEL, N_EXPERTS), D_MODEL ** -0.5)
    b_router = nrm(ks[12], (N_EXPERTS,), 0.01)
    w_e_gate = nrm(ks[13], (DEPTH, N_EXPERTS, D_MODEL, D_FF), D_MODEL ** -0.5)
    w_e_up = nrm(ks[14], (DEPTH, N_EXPERTS, D_MODEL, D_FF), D_MODEL ** -0.5)
    w_e_down = nrm(ks[15], (DEPTH, N_EXPERTS, D_FF, D_MODEL), D_FF ** -0.5 * DN_BETA)
    ln2_g = 1.0 + nrm(ks[16], (DEPTH, D_MODEL), 0.02)
    ln2_b = nrm(ks[17], (DEPTH, D_MODEL), 0.02)
    return {"x": x, "positions": positions, "w_in": w_in, "w_alpha_up": w_alpha_up,
            "b_alpha": b_alpha, "gla_norm": gla_norm, "w_gla_o": w_gla_o, "w_att_o": w_att_o,
            "w_out": w_out, "ln1_g": ln1_g, "ln1_b": ln1_b, "w_router": w_router,
            "b_router": b_router, "w_e_gate": w_e_gate, "w_e_up": w_e_up, "w_e_down": w_e_down,
            "ln2_g": ln2_g, "ln2_b": ln2_b}

def reference(x, positions, w_in, w_alpha_up, b_alpha, gla_norm, w_gla_o, w_att_o, w_out,
              ln1_g, ln1_b, w_router, b_router, w_e_gate, w_e_up, w_e_down, ln2_g, ln2_b):
    B, S, _ = x.shape
    for i in range(DEPTH):
        h = x @ w_in[i]
        q_g, k_g, v_g, r_g, a_g, q_d, k_d, v_d, gate_in = jnp.split(h, SPLIT_POINTS, axis=-1)
        log_a = jax.nn.log_sigmoid((a_g @ w_alpha_up[i]).astype(jnp.float32)
                                   + b_alpha[i].astype(jnp.float32)) / GLA_TAU
        o = gla_chunked(q_g.reshape(B, S, GLA_HEADS, GLA_DK), k_g.reshape(B, S, GLA_HEADS, GLA_DK),
                        v_g.reshape(B, S, GLA_HEADS, GLA_DV), log_a.reshape(B, S, GLA_HEADS, GLA_DK))
        o = o * lax.rsqrt(jnp.mean(jnp.square(o), axis=-1, keepdims=True) + RMS_EPS)
        o = o * gla_norm[i].astype(jnp.float32).reshape(GLA_HEADS, GLA_DV)
        y_gla = (o.reshape(B, S, GLA_V_W).astype(x.dtype) * jax.nn.silu(r_g)) @ w_gla_o[i]
        y_att = dilated_branch(q_d, k_d, v_d, positions).astype(x.dtype) @ w_att_o[i]
        g_gla, g_att = jnp.split(jax.nn.sigmoid(gate_in), N_BRANCH, axis=-1)
        mix = (g_gla * y_gla + g_att * y_att) @ w_out[i]
        x = layer_norm(DN_ALPHA * x + mix, ln1_g[i], ln1_b[i])
        y_moe = grouped_moe(x, w_router, b_router, w_e_gate[i], w_e_up[i], w_e_down[i])
        x = layer_norm(DN_ALPHA * x + y_moe, ln2_g[i], ln2_b[i])
    return x


_drawn_inputs = setup_inputs


def setup_inputs(seed=0):
    import zlib

    import numpy as np

    out = dict(_drawn_inputs(seed))
    spreads = {}
    factors = {}
    for name, (base, spread) in spreads.items():
        noise = np.random.default_rng([zlib.crc32(name.encode()), seed]).standard_normal(out[name].shape)
        drawn = base * np.exp(spread * noise) if base else spread * noise
        out[name] = __import__('jax').numpy.asarray(drawn.astype(out[name].dtype))
    for name, factor in factors.items():
        out[name] = (out[name] * factor).astype(out[name].dtype)
    return out
```

```python
from contextlib import ExitStack

import numpy as np
import concourse.bass as bass
from concourse import mybir

F32 = mybir.dt.float32
F16 = mybir.dt.float16
I32 = mybir.dt.int32
U32 = mybir.dt.uint32
ALU = mybir.AluOpType
ACT = mybir.ActivationFunctionType
AX = mybir.AxisListType

P = 128
TOK = 256
TT = TOK // P
DM = 1024
KT = DM // P
DEPTH = 2
HEADS, DK, DV, RANK, TAU = 4, 128, 256, 16, 16.0
CHUNK = 64
NCH = TOK // CHUNK
GROUPS, AH, HD = 3, 8, 64
E, EG, SLOTS = 16, 4, 64
PAIRS = E // 2
FF = 1024
LN_EPS, RMS_EPS = 1e-5, 1e-6
ALPHA = float((2 * DEPTH) ** 0.25)
NEG = -1e30
A_COL = 2 * HEADS * DK + 2 * HEADS * DV
D_COL = A_COL + RANK
RING = 6
CW = 4096
FRONT_CHUNKS = 24
PAIR_CHUNKS = 12
FRONT_ROUNDS = FRONT_CHUNKS // RING
STAGES = 3
PAIR_ROUNDS = PAIR_CHUNKS // STAGES
W_SCALE, X_SCALE = 64.0, 16.0
UNSCALE = 1.0 / (W_SCALE * X_SCALE)
TWO_PI_A = 6.28125
TWO_PI_B = 0.0019350051879882812
TWO_PI_C = float(2 * np.pi - TWO_PI_A - TWO_PI_B)
ROUND = 12582912.0

CONST = {}
_at = 0
for _name, _n in (("ident", P), ("ones", P), ("rot", P), ("before", P), ("causal", P), ("mask", GROUPS * TOK),
                  ("keep", TOK), ("slot", SLOTS), ("lower", EG * EG), ("inv_freq", 1), ("half_pi", 1),
                  ("limits", 3)):
    CONST[_name] = (_at, _at + _n)
    _at += _n
CONST_W = _at


def constant_table():
    t = np.zeros((P, CONST_W), np.float32)
    p = np.arange(P)

    def put(name, v):
        t[:, CONST[name][0]:CONST[name][1]] = v

    put("ident", np.eye(P))
    put("ones", 1.0)
    rot = np.zeros((P, P))
    for m in range(P):
        if m % HD < HD // 2:
            rot[m + HD // 2, m] = -1.0
        else:
            rot[m - HD // 2, m] = 1.0
    put("rot", rot)
    put("before", p[:, None] < p[None, :])
    put("causal", (p[:, None] <= p[None, :]) & (p[:, None] // CHUNK == p[None, :] // CHUNK))
    dist = (P + p)[:, None] - np.arange(TOK)[None, :]
    near = [(dist >= 0) & (dist <= 128), (dist >= 0) & (dist % 4 == 0), (dist >= 0) & (dist % 16 == 0)]
    put("mask", np.concatenate([np.where(m, 0.0, NEG) for m in near], axis=1))
    put("keep", (np.arange(TOK) % CHUNK != 0)[None, :])
    put("slot", np.arange(SLOTS)[None, :])
    i = np.arange(EG)
    put("lower", (i[None, :] < i[:, None]).reshape(1, -1))
    put("inv_freq", np.power(np.float32(10000.0), -(2 * (p % (HD // 2))).astype(np.float32) / np.float32(HD))[:, None])
    put("half_pi", np.pi / 2)
    put("limits", (np.arange(1, 4) * SLOTS)[None, :])
    return t


class Plan:

    def __init__(self, steps):
        self.start, self.size, n = {}, {}, 0
        for name, k in steps:
            assert name not in self.start, name
            self.start[name], self.size[name] = n, k
            n += k
        self.total = n

    def of(self, base):
        return lambda name, k=None: base * self.total + (self.start[name] + (self.size[name] if k is None else k))


UNITS = [(qt, h) for qt in range(TT) for h in range(AH)]

PE_PLAN = Plan(
    [(f"xT{t}{c}", 1) for t in range(TT) for c in range(2)] + [("a", 1), ("z0", 1), ("z1", 1)]
    + [(f"{n}{j}", 1) for n in "qk" for j in range(2)] + [(f"v{c}{t}", 1) for c in range(2) for t in range(TT)]
    + [(f"r{j}", 1) for j in range(4)] + [("ks0", 1), ("ks1", 1), ("att0", 1), ("att1", 1)]
    + [(f"upd{n}{j}", 1) for n in range(NCH - 1) for j in range(2)] + [(f"o{h}", 1) for h in range(HEADS)]
    + [("ss0", 1), ("ss1", 1)]
    + [s for i in range(13) for s in ([(f"raw{i}", 1)] if i < 12 else []) + ([(f"rot{i - 1}", 1)] if i else [])]
    + [(f"vd{g}{t}", 1) for g in range(GROUPS) for t in range(TT)]
    + [s for i in range(18) for s in
       ([(f"S{i}", 1)] if i < 16 else [])
       + ([(f"pt{i - 1}{j}", 1) for j in range(UNITS[i - 1][0] + 1)] if 1 <= i <= 16 else [])
       + ([(f"pv{i - 2}", 1)] if i >= 2 else [])]
    + [("at0", 1), ("at1", 1)] + [(f"gt{j}", 1) for j in range(8)]
    + [(f"yg{j}", 1) for j in range(4)] + [(f"ya{j}", 1) for j in range(4)]
    + [(f"mo{c}{t}", 1) for c in range(2) for t in range(TT)]
    + [(f"x1T{t}{c}", 1) for t in range(TT) for c in range(2)] + [("logits", 1), ("rank", 1)])

ACT_PLAN = Plan(
    [("xT0", 1), ("xT1", 1), ("aT", 1), ("z0", 2), ("z1", 2), ("soft", 3), ("decay", 3)]
    + [(f"v{c}{t}", 1) for c in range(2) for t in range(TT)] + [(f"r{j}", 1) for j in range(4)]
    + [("ksn0", 1), ("ksn1", 1)] + [(f"sq{h}", 1) for h in range(HEADS)] + [("rms0", 1), ("rms1", 1)]
    + [(f"raw{i}", 1) for i in range(12)] + [(f"vd{g}{t}", 1) for g in range(GROUPS) for t in range(TT)]
    + [s for i in range(17) for s in
       ([(f"ex{i}", 1)] if i < 16 else []) + ([(f"pt{i - 1}", UNITS[i - 1][0] + 1)] if i else [])]
    + [("at0", 1), ("at1", 1)] + [(f"gt{j}", 1) for j in range(8)]
    + [("ln1", 1), ("x1T0", 1), ("x1T1", 1), ("router", 1), ("x_hi", 1), ("ln2", 1)])

DVE_PLAN = Plan(
    [("xT0", 1), ("xT1", 1), ("scan", 6), ("last", 1), ("qt0", 1), ("qt1", 1), ("kt0", 2), ("kt1", 2)]
    + [("attm0", 1), ("attm1", 1)] + [("upd00", 1), ("upd01", 1)]
    + [(f"upd{n}{j}", 2) for n in range(1, NCH - 1) for j in range(2)] + [(f"o{h}", 2) for h in range(HEADS)]
    + [("ms0", 1), ("ms1", 1), ("on0", 2), ("on1", 2)] + [(f"rope{i}", 3) for i in range(12)]
    + [s for i in range(16) for s in [(f"sc{i}", 2)] + ([("an0", 2)] if i == 10 else [])] + [("an1", 2)]
    + [(f"yg{j}", 1) for j in range(4)] + [(f"ya{j}", 2) for j in range(4)]
    + [(f"mo{c}{t}", 1) for c in range(2) for t in range(TT)]
    + [("ln1a", 7), ("ln1r", 1), ("ln1n0", 3), ("ln1n1", 3), ("x1T0", 1), ("x1T1", 1), ("xacc", 1)]
    + [("logits", 3), ("gate", 19), ("rank", 2), ("passes", 4), ("x_lo", 1), ("ln2a", 7), ("ln2r", 1), ("ln2n0", 3), ("ln2n1", 3)])

GATHER = [(h, k, part) for h in range(2) for k in range(KT) for part in range(2)]
PE_PASS = Plan([(f"xg{h}{k}{i}", 1) for h, k, i in GATHER] + [(f"g{t}{c}", 1) for t in range(TT) for c in range(2)])
ACT_PASS = Plan([(f"xg{h}{k}{i}", 1) for h, k, i in GATHER[0::2]]
                + [(f"g{t}{c}", 1) for t in range(TT) for c in range(2)])
DVE_PASS = Plan([("S0", 1), ("S1", 1), ("gated", 2)] + [(f"xg{h}{k}{i}", 1) for h, k, i in GATHER[1::2]] + [("next", 1)])
PE_PAIR = Plan([("yT0", 1), ("yT1", 1)] + [(f"y{t}{c}", 1) for t in range(TT) for c in range(2)])
ACT_PAIR = Plan([("silu0", 1), ("hh0", 1), ("silu1", 1), ("yT0", 1), ("hh1", 1), ("yT1", 1), ("yn0", 1), ("yn1", 1)])
DVE_PAIR = Plan([("x", 1), ("h0", 1), ("hl0", 1), ("h1", 1), ("hl1", 1), ("G", 1)]
                + [(f"y{t}{c}", 1) for t in range(TT) for c in range(2)])
PAIR_ORDER = [("gate", 0), ("up", 0), ("gate", 1), ("down", 0), ("up", 1), ("down", 1)]


def build(nc, x, positions, w_in, w_alpha_up, b_alpha, gla_norm, w_gla_o, w_att_o, w_out, ln1_g, ln1_b,
          w_router, b_router, w_e_gate, w_e_up, w_e_down, ln2_g, ln2_b, constants, out):
    with ExitStack() as ctx:
        def sb(name, shape, dt=F32):
            return ctx.enter_context(nc.sbuf_tensor(name, shape, dt))

        def sem(name):
            return ctx.enter_context(nc.semaphore(name))

        ctx.enter_context(nc.allow_non_contiguous_dma("small strided parameter loads"))

        ring = sb("ring", [P, RING, CW])
        x_nat = sb("x_nat", [P, TT, DM])
        xacc = sb("xacc", [P, TT, DM])
        xT = sb("xT", [P, KT, TOK])
        area = sb("area", [P, 16384])
        cst = sb("cst", [P, CONST_W])
        lnp = sb("lnp", [P, 2, DM])
        cos = sb("cos", [P, TOK])
        sin = sb("sin", [P, TOK])
        w_a = sb("w_a", [P, KT, RANK])
        w_au = sb("w_au", [RANK, HEADS * DK])
        b_al = sb("b_al", [P, HEADS])
        gnorm = sb("gnorm", [P, 8])
        w_r = sb("w_r", [P, KT, E])
        b_r = sb("b_r", [P, E])
        aT = sb("aT", [RANK, TOK])
        dec = sb("dec", [P, HEADS, NCH])
        G_pair = sb("G_pair", [P, TOK])
        stats = sb("stats", [P, TT, 2, 6])
        mv = sb("mv", [P, TT, 2])
        rstd = sb("rstd", [P, TT])
        top = sb("top", [P, 16])
        ntop = sb("ntop", [P, 16])
        psum_l = sb("psum_l", [P, 16])
        rl = sb("rl", [P, 16])
        e_t = sb("e_t", [P, TT, E])
        sel = sb("sel", [P, TT, E])
        comb = sb("comb", [P, TT, E])
        rk = sb("rk", [P, TT, E])
        pm = sb("pm", [P, TT, E])
        g_s = sb("g_s", [P, 8])
        g_r = sb("g_r", [P, 8])
        two = sb("two", [P, 4])
        lim = sb("lim", [1, 4])
        passes_sb = sb("passes_sb", [1, 1], I32)
        bank = ctx.enter_context(nc.psum_tensor("bank", [P, 8, 512], F32))

        def part(a, width, pattern=None, **kw):
            v = area[:, a:a + width]
            return v.rearrange(pattern, **kw) if pattern else v

        zb = part(0, 1024, "p (h t) -> p h t", h=HEADS)
        lb = part(1024, 1024, "p (h t) -> p h t", h=HEADS)
        q_t = part(2048, 1024, "p (h t) -> p h t", h=HEADS)
        k_t = part(3072, 1024, "p (h t) -> p h t", h=HEADS)
        v_g = part(4096, 2048, "p (t c) -> p t c", t=TT)
        ks_n = part(6144, 1024, "p (t h d) -> p t h d", t=TT, h=HEADS)
        attm = part(7168, 1024, "p (t h i) -> p t h i", t=TT, h=HEADS)
        state = part(8192, 3072, "p (n h v) -> p n h v", n=3, h=HEADS)
        sq = part(11264, 2048, "p (m t) -> p m t", m=8)
        rms = part(13312, 1024, "p (h t) -> p h t", h=HEADS)
        oT = part(14336, 2048, "p (m t) -> p m t", m=8)
        qk = part(0, 6144, "p (c t) -> p c t", c=24)
        v_d = part(6144, 3072, "p (t c) -> p t c", t=TT)
        raw = part(9216, 1024, "p (b c t) -> p b c t", b=2, c=2)
        rtmp = part(10240, 512, "p (c t) -> p c t", c=2)
        prob = part(9216, 1536, "p (b c) -> p b c", b=2)
        probT = part(10752, 1536, "p (b c q) -> p b c q", b=2, c=6)
        att_n = part(12288, 1024, "p (t c) -> p t c", t=TT)
        attT = part(13312, 1024, "p (k t) -> p k t", k=4)
        gateT = part(0, 4096, "p (c t) -> p c t", c=16)
        mixT = part(4096, 2048, "p (c t) -> p c t", c=8)
        mtmp = part(6144, 512, "p (c t) -> p c t", c=2)
        cmp_a, cmp_b = part(12288, 128), part(12416, 128)
        xg = part(0, 8192).bitcast(F16).rearrange("p (k i s) -> p k i s", k=KT, i=2)
        S = part(8192, 1024).bitcast(F16).rearrange("p (t e s) -> p t e s", t=TT, e=E)
        x_pair = part(9216, 1024).bitcast(F16).rearrange("p (k i s) -> p k i s", k=KT, i=2)
        G = part(10240, 2048, "p (r t) -> p r t", r=PAIRS)
        hid = part(12288, 1024, "p (j c) -> p j c", j=2)
        h16 = part(13312, 1024).bitcast(F16).rearrange("p (j i c) -> p j i c", j=2, i=2)
        S_gated = part(14336, 2048, "p (t e s) -> p t e s", t=TT, e=E)
        yT = part(14336, 1024, "p (m j s) -> p m j s", m=8, j=2)
        yn = part(15360, 1024)

        def const(name, rows=P):
            a, b = CONST[name]
            return cst[0:rows, a:b]

        ident, ones = const("ident"), const("ones")
        x16 = xT[:, :, :].rearrange("p k t -> p (k t)").bitcast(F16).rearrange("p (i t d) -> p i t d", i=2, t=TT)
        parts16 = [ring[:, STAGES + i, :].bitcast(F16).rearrange("p (i k c) -> p i k c", i=2, k=KT)
                   for i in range(STAGES)]

        def halves(b):
            return bank[:, b, :].rearrange("p (c t) -> p c t", c=2)

        setup_landed = sem("setup_landed")
        router_landed = sem("router_landed")
        small_landed = sem("small_landed")
        ln1_landed = sem("ln1_landed")
        ln2_landed = sem("ln2_landed")
        landed = [sem(f"chunk_landed{s}") for s in range(RING)]
        chunk_done = sem("chunk_done")
        hi_done = sem("hi_done")
        split_done = sem("split_done")
        expert_done = sem("expert_done")
        x_ready = sem("x_ready")
        zeroed = sem("zeroed")
        rope_done = sem("rope_tables")
        rope_act = sem("rope_tables_act")
        pe_done, act_done, dve_done = sem("pe_done"), sem("act_done"), sem("dve_done")
        pe_pass, act_pass, dve_pass = sem("pe_pass"), sem("act_pass"), sem("dve_pass")
        pe_pair, act_pair, dve_pair = sem("pe_pair"), sem("act_pair"), sem("dve_pair")
        out_done = sem("out_done")
        apart_sem = sem("apart")

        block = ctx.enter_context(nc.Block())

        def apart(eng):
            eng.sem_inc(apart_sem, 1)

        def pass_loop(eng, layer, body, passes_reg):
            before = eng.snap(passes_reg)
            eng.wait_ge(dve_done, DVE_PLAN.of(layer)("passes"))
            apart(eng)
            n = eng.value_load(passes_sb[0:1, 0:1], min_val=1, max_val=TOK // SLOTS)
            with eng.Fori(0, n) as p:
                body(before + p)
            eng.reg_add(passes_reg, passes_reg, n)

        w_in_v = w_in.rearrange("l (k p) c -> p l k c", p=P)
        gla_o_v = w_gla_o.rearrange("l (k p) c -> p l k c", p=P)
        att_o_v = w_att_o.rearrange("l (k p) c -> p l k c", p=P)
        out_v = w_out.rearrange("l (k p) c -> p l k c", p=P)
        expert_v = {"gate": w_e_gate.rearrange("l e (k p) c -> p (l e) k c", p=P),
                    "up": w_e_up.rearrange("l e (k p) c -> p (l e) k c", p=P),
                    "down": w_e_down.rearrange("l e (k p) c -> p (l e) k c", p=P)}
        starts = [c * 512 for c in range(A_COL // 512)] + [D_COL + c * 512 for c in range(13)]
        front = [(w_in_v, s, 512) for s in starts] + [(gla_o_v, 0, 512), (gla_o_v, 512, 512), (att_o_v, 0, 1024),
                                                      (out_v, 0, 512), (out_v, 512, 512)]
        assert len(front) == FRONT_CHUNKS

        @block.sync
        def _(sp):
            passes_reg = sp.alloc_register("sp_passes")
            sp.reg_mov(passes_reg, 0)
            sp.dma_start(x_nat[:, :, :], x[0, :, :].rearrange("(t p) d -> p t d", p=P)).then_inc(setup_landed, 16)
            sp.dma_start(cst[:, :], constants).then_inc(setup_landed, 16)
            with sp.Fori(0, DEPTH) as layer:
                used = sp.snap(passes_reg) * (PAIRS * PAIR_CHUNKS)
                for c, (w, col, width) in enumerate(front):
                    if c < STAGES:
                        sp.wait_ge(split_done, used + (c + 1))
                    elif c < RING:
                        sp.wait_ge(expert_done, used + (c - STAGES + 1))
                    else:
                        sp.wait_ge(chunk_done, layer * FRONT_CHUNKS + (c - RING + 1))
                    src = w[:, bass.ds(layer, 1), :, col:col + width].rearrange("p o k c -> p (o k) c")
                    dst = ring[:, c % RING, :].rearrange("p (k c) -> p k c", c=width)
                    sp.dma_start(dst, src).then_inc(landed[c % RING], 16)
                sp.wait_ge(chunk_done, layer * FRONT_CHUNKS + (FRONT_CHUNKS - STAGES))

                def experts(q):
                    with sp.Fori(0, PAIRS) as pair:
                        n1 = (q * PAIRS + pair) * PAIR_CHUNKS
                        for c in range(PAIR_CHUNKS):
                            kind, j = PAIR_ORDER[c // 2]
                            sp.wait_ge(split_done, n1 + (c + 1))
                            src = expert_v[kind][:, bass.ds(layer * E + pair * 2 + j, 1), :,
                                                 (c % 2) * 512:(c % 2) * 512 + 512].rearrange("p o k c -> p (o k) c")
                            sp.dma_start(ring[:, c % STAGES, :].rearrange("p (k c) -> p k c", c=512), src)\
                              .then_inc(landed[c % STAGES], 16)

                pass_loop(sp, layer, experts, passes_reg)
            sp.wait_ge(x_ready, DEPTH + 1)
            sp.dma_start(out[0, :, :].rearrange("(t p) d -> p t d", p=P), x_nat[:, :, :]).then_inc(out_done, 16)
            sp.wait_ge(out_done, 16)

        @block.gpsimd
        def _(pool):
            pool.dma_start(w_r[:, :, :], w_router.rearrange("(k p) e -> p k e", p=P)).then_inc(router_landed, 16)
            pool.dma_start(b_r[:, :], b_router.rearrange("(o e) -> o e", o=1).partition_broadcast(P)
                           .rearrange("a o e -> a (o e)")).then_inc(router_landed, 16)
            pool.dma_start(cos[:, :].bitcast(I32), positions[0:1, :].partition_broadcast(P)
                           .rearrange("a o e -> a (o e)")).then_inc(router_landed, 16)
            with pool.Fori(0, DEPTH) as layer:
                pool.wait_ge(x_ready, layer + 1)
                apart(pool)
                pool.dma_start(w_a[:, :, :], w_in_v[:, bass.ds(layer, 1), :, A_COL:A_COL + RANK]
                               .rearrange("p o k c -> p (o k) c")).then_inc(small_landed, 16)
                pool.dma_start(w_au[:, :], w_alpha_up[bass.ds(layer, 1), :, :].rearrange("o r c -> (o r) c"))\
                    .then_inc(small_landed, 16)
                pool.dma_start(b_al[:, :], b_alpha[bass.ds(layer, 1), :].rearrange("o (h p) -> p (o h)", p=P))\
                    .then_inc(small_landed, 16)
                pool.dma_start(gnorm[:, :], gla_norm[bass.ds(layer, 1), :].rearrange("o (h p) -> p (o h)", p=P))\
                    .then_inc(small_landed, 16)
                nc.gpsimd.memset(attm, 0.0).then_inc(zeroed, 1)
                pool.dma_start(lnp[:, 0, :], ln1_g[bass.ds(layer, 1), :].partition_broadcast(P)
                               .rearrange("a o e -> a (o e)")).then_inc(ln1_landed, 16)
                pool.dma_start(lnp[:, 1, :], ln1_b[bass.ds(layer, 1), :].partition_broadcast(P)
                               .rearrange("a o e -> a (o e)")).then_inc(ln1_landed, 16)
                pool.wait_ge(dve_done, DVE_PLAN.of(layer)("ln1n1"))
                apart(pool)
                pool.dma_start(lnp[:, 0, :], ln2_g[bass.ds(layer, 1), :].partition_broadcast(P)
                               .rearrange("a o e -> a (o e)")).then_inc(ln2_landed, 16)
                pool.dma_start(lnp[:, 1, :], ln2_b[bass.ds(layer, 1), :].partition_broadcast(P)
                               .rearrange("a o e -> a (o e)")).then_inc(ln2_landed, 16)

        @block.tensor
        def _(pe):
            passes_reg = pe.alloc_register("pe_passes")
            pe.reg_mov(passes_reg, 0)
            pe.sem_inc(split_done, STAGES)
            pe.sem_inc(expert_done, STAGES)
            pe.wait_ge(setup_landed, 32)
            pe.wait_ge(router_landed, 48)

            def transposes(b, sources):
                for i, s in enumerate(sources):
                    mm = pe.transpose(bank[:, b, i * P:(i + 1) * P], s, ident)
                return mm

            with pe.Fori(0, DEPTH) as layer:
                Pn, A, D = PE_PLAN.of(layer), ACT_PLAN.of(layer), DVE_PLAN.of(layer)
                expert_rounds = pe.snap(passes_reg) * (PAIRS * PAIR_ROUNDS)

                def arrived(c):
                    n = layer * FRONT_ROUNDS + (c // RING + 1)
                    if c % RING < STAGES:
                        n = n + expert_rounds
                    pe.wait_ge(landed[c % RING], n * 16)

                def wide(c, width=512):
                    return ring[:, c % RING, :].rearrange("p (k c) -> p k c", c=width)

                def features(b, half, w, col, rhs, kt=KT):
                    for k in range(kt):
                        mm = pe.matmul(bank[:, b, half * TOK:(half + 1) * TOK], w[:, k, col:col + P], rhs[:, k, :],
                                       start=(k == 0), stop=(k == kt - 1))
                    return mm

                def tokens(b, t, w, lhs):
                    for k in range(KT):
                        mm = pe.matmul(bank[:, b, :], lhs[:, k, t * P:(t + 1) * P], w[:, k, :],
                                       start=(k == 0), stop=(k == KT - 1))
                    return mm

                pe.wait_ge(x_ready, layer + 1)
                for t in range(TT):
                    for c in range(2):
                        transposes(4 * c + t, [x_nat[:, t, k * P:(k + 1) * P] for k in range(4 * c, 4 * c + 4)])\
                            .then_inc(pe_done, 1)
                pe.wait_ge(small_landed, (layer + 1) * 64)
                pe.wait_ge(act_done, A("xT1"))
                pe.wait_ge(dve_done, D("xT1"))
                for k in range(KT):
                    mm = pe.matmul(bank[0:RANK, 2, 0:TOK], w_a[:, k, :], xT[:, k, :], start=(k == 0), stop=(k == KT - 1))
                mm.then_inc(pe_done, 1)
                pe.wait_ge(act_done, A("aT"))
                for j in range(2):
                    for i in range(2):
                        h = 2 * j + i
                        mm = pe.matmul(bank[:, j, i * TOK:(i + 1) * TOK], w_au[:, h * DK:(h + 1) * DK], aT[:, :],
                                       start=True, stop=True)
                    mm.then_inc(pe_done, 1)
                for c in range(2):
                    arrived(c)
                    for j in range(2):
                        features(4 + 2 * c + j, 0, wide(c), 2 * j * P, xT)
                        mm = features(4 + 2 * c + j, 1, wide(c), (2 * j + 1) * P, xT)
                        mm.then_inc(pe_done, 1)
                    pe.drain().then_inc(chunk_done, 1)
                users = ["z0", "z1", "aT"]
                n = 0
                for c in range(2, 4):
                    arrived(c)
                    for t in range(TT):
                        pe.wait_ge(act_done, A(users[n % 3]))
                        tokens(n % 3, t, wide(c), xT).then_inc(pe_done, 1)
                        users[n % 3] = f"v{c - 2}{t}"
                        n += 1
                    pe.drain().then_inc(chunk_done, 1)
                for c in range(4, 6):
                    arrived(c)
                    for j in range(2):
                        pe.wait_ge(act_done, A(users[n % 3]))
                        features(n % 3, 0, wide(c), 2 * j * P, xT)
                        features(n % 3, 1, wide(c), (2 * j + 1) * P, xT).then_inc(pe_done, 1)
                        users[n % 3] = f"r{2 * (c - 4) + j}"
                        n += 1
                    pe.drain().then_inc(chunk_done, 1)
                pe.wait_ge(dve_done, D("kt1"))
                for t in range(TT):
                    pe.wait_ge(act_done, A(users[n % 3]))
                    transposes(n % 3, [zb[:, h, t * P:(t + 1) * P] for h in range(HEADS)]).then_inc(pe_done, 1)
                    users[n % 3] = f"ksn{t}"
                    n += 1
                for t in range(TT):
                    for h in range(HEADS):
                        mm = pe.matmul(bank[:, 4 + t, h * P:(h + 1) * P], k_t[:, h, t * P:(t + 1) * P],
                                       q_t[:, h, t * P:(t + 1) * P], start=True, stop=True)
                    mm.then_inc(pe_done, 1)
                pe.wait_ge(act_done, A("ksn1"))
                for c in range(NCH - 1):
                    t, rows = c // 2, slice((c % 2) * CHUNK, (c % 2 + 1) * CHUNK)
                    for j in range(2):
                        if c:
                            pe.wait_ge(dve_done, D(f"upd{c - 1}{j}"))
                        for i in range(2):
                            h = 2 * j + i
                            mm = pe.matmul(bank[:, 6 + j, i * DV:(i + 1) * DV], ks_n[rows, t, h, :],
                                           v_g[rows, t, h * DV:(h + 1) * DV], start=True, stop=True)
                        mm.then_inc(pe_done, 1)
                free = ["attm0", "attm1", "upd20", "upd21"]
                pe.wait_ge(dve_done, D("upd21"))
                for h in range(HEADS):
                    for m in range(2):
                        cols = slice(h * DV + m * P, h * DV + (m + 1) * P)
                        for t in range(TT):
                            pe.matmul(bank[:, 4 + h, m * TOK + t * P:m * TOK + (t + 1) * P], v_g[:, t, cols],
                                      attm[:, t, h, :], start=True, stop=False)
                            for c in range(max(2 * t, 1), 2 * t + 2):
                                mm = pe.matmul(bank[:, 4 + h, m * TOK + c * CHUNK:m * TOK + (c + 1) * CHUNK],
                                               state[:, c - 1, h, m * P:(m + 1) * P],
                                               q_t[:, h, c * CHUNK:(c + 1) * CHUNK], start=False, stop=(c == 2 * t + 1))
                    mm.then_inc(pe_done, 1)
                for j in range(2):
                    pe.wait_ge(act_done, A(f"sq{2 * j + 1}"))
                    for i in range(2):
                        for m in range(2):
                            mm = pe.matmul(bank[:, 3 if j == 0 else 2, i * TOK:(i + 1) * TOK], ones, sq[:, 4 * j + 2 * i + m, :],
                                           start=(m == 0), stop=(m == 1))
                    mm.then_inc(pe_done, 1)

                rope_free = [f"o{h}" for h in range(HEADS)]
                for i in range(13):
                    if i < 12:
                        c = 6 + i // 2
                        if i % 2 == 0:
                            arrived(c)
                        if i >= 2:
                            pe.wait_ge(act_done, A(f"raw{i - 2}"))
                        features(i % 2, 0, wide(c), (2 * (i % 2)) * P, xT)
                        features(i % 2, 1, wide(c), (2 * (i % 2) + 1) * P, xT).then_inc(pe_done, 1)
                        if i % 2 == 1:
                            pe.drain().then_inc(chunk_done, 1)
                    if i >= 1:
                        pe.wait_ge(act_done, A(f"raw{i - 1}"))
                        pe.wait_ge(dve_done, D(rope_free[(i - 1) % 4]))
                        pe.matmul(bank[:, 4 + (i - 1) % 4, :], const("rot"),
                                  raw[:, (i - 1) % 2, :, :].rearrange("p c t -> p (c t)"), start=True, stop=True)\
                            .then_inc(pe_done, 1)
                        rope_free[(i - 1) % 4] = f"rope{i - 1}"
                pe.wait_ge(dve_done, D("ms1"))
                users = ["raw10", "raw11", "rms1"]
                n = 0
                for g in range(GROUPS):
                    arrived(12 + g)
                    for t in range(TT):
                        pe.wait_ge(act_done, A(users[n % 3]))
                        tokens(n % 3, t, wide(12 + g), xT).then_inc(pe_done, 1)
                        users[n % 3] = f"vd{g}{t}"
                        n += 1
                    pe.drain().then_inc(chunk_done, 1)
                pe.wait_ge(dve_done, D("rope11"))
                for i in range(18):
                    if i < 16:
                        qt, h = UNITS[i]
                        if i >= 2:
                            pe.wait_ge(dve_done, D(f"sc{i - 2}"))
                        for g in range(GROUPS):
                            hh = g * AH + h
                            rows = slice((hh % 2) * HD, (hh % 2 + 1) * HD)
                            nk = (qt + 1) * P
                            b = 4 + 2 * (i % 2) + g // 2
                            mm = pe.matmul(bank[:, b, (g % 2) * TOK:(g % 2) * TOK + nk],
                                           qk[rows, hh // 2, qt * P:(qt + 1) * P], qk[rows, 12 + hh // 2, 0:nk],
                                           start=True, stop=True)
                        mm.then_inc(pe_done, 1)
                    if 1 <= i <= 16:
                        u = i - 1
                        pe.wait_ge(act_done, A(f"ex{u}"))
                        for j in range(UNITS[u][0] + 1):
                            pe.wait_ge(act_done, A(users[n % 3]))
                            transposes(n % 3, [prob[:, u % 2, (3 * j + s) * P:(3 * j + s + 1) * P] for s in range(3)])\
                                .then_inc(pe_done, 1)
                            users[n % 3] = f"pt{u}"
                            n += 1
                    if i >= 2:
                        u = i - 2
                        qt, h = UNITS[u]
                        pe.wait_ge(act_done, A(f"pt{u}"))
                        if u == 0:
                            pe.wait_ge(act_done, A("vd21"))
                        if u == 8:
                            pe.wait_ge(dve_done, D("an0"))
                        parts = [(g, kt) for g in range(GROUPS) for kt in range(qt + 1)]
                        for s, (g, kt) in enumerate(parts):
                            mm = pe.matmul(bank[:, 3, h * HD:(h + 1) * HD], probT[:, u % 2, s, :],
                                           v_d[:, kt, g * 512 + h * HD:g * 512 + (h + 1) * HD],
                                           start=(s == 0), stop=(s == len(parts) - 1))
                        mm.then_inc(pe_done, 1)
                for qt in range(TT):
                    pe.wait_ge(dve_done, D(f"an{qt}"))
                    pe.wait_ge(act_done, A(users[n % 3]))
                    transposes(n % 3, [att_n[:, qt, k * P:(k + 1) * P] for k in range(4)]).then_inc(pe_done, 1)
                    users[n % 3] = f"at{qt}"
                    n += 1
                for j in range(8):
                    c = 15 + j // 2
                    if j % 2 == 0:
                        arrived(c)
                    pe.wait_ge(act_done, A(users[n % 3]))
                    features(n % 3, 0, wide(c), (2 * (j % 2)) * P, xT)
                    features(n % 3, 1, wide(c), (2 * (j % 2) + 1) * P, xT).then_inc(pe_done, 1)
                    users[n % 3] = f"gt{j}"
                    n += 1
                    if j % 2 == 1:
                        pe.drain().then_inc(chunk_done, 1)
                for j in range(4):
                    if j % 2 == 0:
                        arrived(19 + j // 2)
                    w = wide(19 + j // 2)
                    features(4 + j, 0, w, (2 * (j % 2)) * P, oT)
                    features(4 + j, 1, w, (2 * (j % 2) + 1) * P, oT).then_inc(pe_done, 1)
                    if j % 2 == 1:
                        pe.drain().then_inc(chunk_done, 1)
                arrived(21)
                pe.wait_ge(act_done, A("at1"))
                for j in range(4):
                    pe.wait_ge(dve_done, D(f"yg{j}"))
                    features(4 + j, 0, wide(21, 1024), 2 * j * P, attT, 4)
                    features(4 + j, 1, wide(21, 1024), (2 * j + 1) * P, attT, 4).then_inc(pe_done, 1)
                pe.drain().then_inc(chunk_done, 1)
                pe.wait_ge(dve_done, D("ya3"))
                for c in range(2):
                    arrived(22 + c)
                    for t in range(TT):
                        tokens(4 + 2 * c + t, t, wide(22 + c), mixT).then_inc(pe_done, 1)
                    pe.drain().then_inc(chunk_done, 1)
                pe.wait_ge(act_done, A("gt7"))
                for t in range(TT):
                    pe.wait_ge(dve_done, D(f"ln1n{t}"))
                    for c in range(2):
                        transposes(4 * c + t, [x_nat[:, t, k * P:(k + 1) * P] for k in range(4 * c, 4 * c + 4)])\
                            .then_inc(pe_done, 1)
                pe.wait_ge(act_done, A("x1T1"))
                pe.wait_ge(dve_done, D("x1T1"))
                for t in range(TT):
                    for k in range(KT):
                        mm = pe.matmul(bank[:, 6, t * E:(t + 1) * E], xT[:, k, t * P:(t + 1) * P], w_r[:, k, :],
                                       start=(k == 0), stop=(k == KT - 1))
                mm.then_inc(pe_done, 1)
                pe.wait_ge(dve_done, D("gate", 15))
                pe.matmul(bank[:, 7, 0:E], const("before"), sel[:, 0, :], start=True, stop=True)
                pe.matmul(bank[:, 7, E:2 * E], ones, sel[:, 0, :], start=True, stop=False)
                pe.matmul(bank[:, 7, E:2 * E], const("before"), sel[:, 1, :], start=False, stop=True)
                pe.matmul(bank[:, 7, 2 * E:3 * E], ones, sel[:, 0, :], start=True, stop=False)
                pe.matmul(bank[:, 7, 2 * E:3 * E], ones, sel[:, 1, :], start=False, stop=True).then_inc(pe_done, 1)

                def experts(q):
                    AP_, DP = ACT_PASS.of(q), DVE_PASS.of(q)
                    pe.wait_ge(dve_done, D("x_lo"))
                    pe.wait_ge(dve_pass, DP("S1"))
                    last_a, last_d = [None] * 3, [None] * 4
                    na = nd = 0
                    for n, (hf, k, i) in enumerate(GATHER):
                        step = f"xg{hf}{k}{i}"
                        if n % 2 == 0:
                            if last_a[na % 3]:
                                pe.wait_ge(act_pass, AP_(last_a[na % 3]))
                            b, last_a[na % 3] = na % 3, step
                            na += 1
                        else:
                            if last_d[nd % 4]:
                                pe.wait_ge(dve_pass, DP(last_d[nd % 4]))
                            b, last_d[nd % 4] = 4 + nd % 4, step
                            nd += 1
                        for t in range(TT):
                            mm = pe.matmul(bank[:, b, :], x16[:, i, t, k * P:(k + 1) * P],
                                           S[:, t, hf * 8:(hf + 1) * 8, :].rearrange("p e s -> p (e s)"),
                                           start=(t == 0), stop=(t == TT - 1))
                        mm.then_inc(pe_pass, 1)
                    pe.wait_ge(dve_pass, DP("gated"))
                    for t in range(TT):
                        for c in range(2):
                            pe.wait_ge(act_pass, AP_(last_a[na % 3]))
                            transposes(na % 3, [S_gated[:, t, 2 * r:2 * r + 2, :].rearrange("p e s -> p (e s)")
                                                for r in range(4 * c, 4 * c + 4)]).then_inc(pe_pass, 1)
                            last_a[na % 3] = f"g{t}{c}"
                            na += 1
                    pe.wait_ge(act_pass, AP_("g11"))
                    pe.wait_ge(dve_pass, DP("next"))
                    apart(pe)

                    with pe.Fori(0, PAIRS) as pair:
                        r = q * PAIRS + pair
                        AR, DR = ACT_PAIR.of(r), DVE_PAIR.of(r)
                        pe.wait_ge(dve_pair, DR("x"))
                        for c in range(PAIR_CHUNKS):
                            kind, j = PAIR_ORDER[c // 2]
                            b = {"gate": 4, "up": 5, "down": 6}[kind]
                            if c % 2 == 0:
                                if kind == "gate" and j == 1:
                                    pe.wait_ge(act_pair, AR("silu0"))
                                if kind == "down":
                                    pe.wait_ge(dve_pair, DR(f"hl{j}"))
                                    if j == 1:
                                        pe.wait_ge(act_pair, AR("yT0"))
                                if kind == "up" and j == 1:
                                    pe.wait_ge(dve_pair, DR("h0"))
                            pe.wait_ge(split_done, r * PAIR_CHUNKS + (c + 1 + STAGES))
                            w = parts16[c % STAGES]
                            for m in range(4):
                                mo = (c % 2) * 4 + m
                                for k in range(KT):
                                    for n, (wi, xi) in enumerate(((0, 0), (0, 1), (1, 0))):
                                        if kind == "down":
                                            rhs = h16[:, j, xi, k * SLOTS:(k + 1) * SLOTS]
                                        else:
                                            rhs = x_pair[:, k, xi, j * SLOTS:(j + 1) * SLOTS]
                                        mm = pe.matmul(bank[:, b, mo * SLOTS:(mo + 1) * SLOTS],
                                                       w[:, wi, k, m * P:(m + 1) * P], rhs,
                                                       start=(k == 0 and n == 0), stop=(k == KT - 1 and n == 2))
                            mm.then_inc(expert_done, 1)
                        pe.wait_ge(act_pair, AR("yT1"))
                        for c in range(2):
                            transposes([7, 0][c], [yT[:, m, :, :].rearrange("p j s -> p (j s)")
                                                   for m in range(4 * c, 4 * c + 4)]).then_inc(pe_pair, 1)
                        pe.wait_ge(act_pair, AR("yn1"))
                        pe.wait_ge(dve_pair, DR("G"))
                        for t in range(TT):
                            for c in range(2):
                                pe.matmul(bank[:, [1, 2, 3, 7][2 * t + c], :], G_pair[:, t * P:(t + 1) * P],
                                          yn[:, c * 512:(c + 1) * 512], start=True, stop=True).then_inc(pe_pair, 1)

                pass_loop(pe, layer, experts, passes_reg)

        @block.scalar
        def _(act):
            passes_reg = act.alloc_register("act_passes")
            act.reg_mov(passes_reg, 0)
            act.wait_ge(rope_done, 8)
            act.activation(sin[:, :], area[:, 0:TOK], ACT.Sin).then_inc(rope_act, 1)
            act.activation(area[:, 256:512], area[:, 0:TOK], ACT.Abs).then_inc(rope_act, 1)
            act.wait_ge(rope_act, 2)
            act.activation(cos[:, :], area[:, 256:512], ACT.Sin, bias=const("half_pi"), scale=-1.0).then_inc(rope_act, 1)

            with act.Fori(0, DEPTH) as layer:
                Pn, A, D = PE_PLAN.of(layer), ACT_PLAN.of(layer), DVE_PLAN.of(layer)

                def quads(b):
                    return bank[:, b, :].rearrange("p (k t) -> p k t", k=4)

                act.wait_ge(x_ready, layer + 1)
                for t in range(TT):
                    act.wait_ge(pe_done, Pn(f"xT{t}0"))
                    act.activation(xT[:, 0:4, t * P:(t + 1) * P], quads(t), ACT.Copy).then_inc(act_done, 1)
                act.wait_ge(pe_done, Pn("a"))
                act.activation(aT[:, :], bank[0:RANK, 2, 0:TOK], ACT.Copy).then_inc(act_done, 1)
                for h in range(HEADS):
                    act.wait_ge(pe_done, Pn(f"z{h // 2}"))
                    act.activation(zb[:, h, :], bank[:, h // 2, (h % 2) * TOK:(h % 2 + 1) * TOK], ACT.Identity,
                                   bias=b_al[:, h:h + 1]).then_inc(act_done, 1)
                act.wait_ge(act_done, A("z1"))
                act.activation(lb, zb, ACT.Abs).then_inc(act_done, 1)
                act.wait_ge(act_done, A("soft", 1))
                act.activation(lb, lb, ACT.Exp, scale=-1.0).then_inc(act_done, 1)
                act.wait_ge(act_done, A("soft", 2))
                act.activation(lb, lb, ACT.Ln, bias=ones[:, 0:1]).then_inc(act_done, 1)
                act.wait_ge(dve_done, D("scan"))
                act.activation(q_t, lb, ACT.Exp, scale=1.0 / TAU).then_inc(act_done, 1)
                act.activation(k_t, lb, ACT.Exp, scale=-1.0 / TAU).then_inc(act_done, 1)
                act.activation(zb, zb, ACT.Exp, scale=1.0 / TAU).then_inc(act_done, 1)
                n = 0
                for c in range(2):
                    for t in range(TT):
                        act.wait_ge(pe_done, Pn(f"v{c}{t}"))
                        act.activation(v_g[:, t, c * 512:(c + 1) * 512], bank[:, n % 3, :], ACT.Copy).then_inc(act_done, 1)
                        n += 1
                for j in range(4):
                    act.wait_ge(pe_done, Pn(f"r{j}"))
                    act.activation(oT[:, 2 * j:2 * j + 2, :], halves(n % 3), ACT.Silu).then_inc(act_done, 1)
                    n += 1
                for t in range(TT):
                    act.wait_ge(pe_done, Pn(f"ks{t}"))
                    act.activation(ks_n[:, t, :, :], quads(n % 3), ACT.Copy).then_inc(act_done, 1)
                    n += 1
                for h in range(HEADS):
                    act.wait_ge(pe_done, Pn(f"o{h}"))
                    act.activation(sq[:, 2 * h:2 * h + 2, :], halves(4 + h), ACT.Square).then_inc(act_done, 1)
                for j in range(2):
                    act.wait_ge(dve_done, D(f"ms{j}"))
                    act.activation(rms[:, 2 * j:2 * j + 2, :], rms[:, 2 * j:2 * j + 2, :], ACT.Sqrt).then_inc(act_done, 1)
                for i in range(12):
                    act.wait_ge(pe_done, Pn(f"raw{i}"))
                    if i >= 2:
                        act.wait_ge(dve_done, D(f"rope{i - 2}"))
                    act.activation(raw[:, i % 2, :, :], halves(i % 2), ACT.Copy).then_inc(act_done, 1)
                n = 0
                for g in range(GROUPS):
                    for t in range(TT):
                        act.wait_ge(pe_done, Pn(f"vd{g}{t}"))
                        act.activation(v_d[:, t, g * 512:(g + 1) * 512], bank[:, n % 3, :], ACT.Copy).then_inc(act_done, 1)
                        n += 1
                for i in range(17):
                    if i < 16:
                        w = 3 * (UNITS[i][0] + 1) * P
                        act.wait_ge(dve_done, D(f"sc{i}"))
                        act.activation(prob[:, i % 2, 0:w], prob[:, i % 2, 0:w], ACT.Exp, bias=ntop[:, i:i + 1],
                                       scale=HD ** -0.5, accum_out=psum_l[:, i:i + 1]).then_inc(act_done, 1)
                    if i >= 1:
                        u = i - 1
                        for j in range(UNITS[u][0] + 1):
                            act.wait_ge(pe_done, Pn(f"pt{u}{j}"))
                            if j == 0 and u >= 2:
                                act.wait_ge(pe_done, Pn(f"pv{u - 2}"))
                            act.activation(probT[:, u % 2, 3 * j:3 * j + 3, :], quads(n % 3)[:, 0:3, :], ACT.Copy)\
                                .then_inc(act_done, 1)
                            n += 1
                for qt in range(TT):
                    act.wait_ge(pe_done, Pn(f"at{qt}"))
                    act.activation(attT[:, :, qt * P:(qt + 1) * P], quads(n % 3), ACT.Copy).then_inc(act_done, 1)
                    n += 1
                for j in range(8):
                    act.wait_ge(pe_done, Pn(f"gt{j}"))
                    act.activation(gateT[:, 2 * j:2 * j + 2, :], halves(n % 3), ACT.Sigmoid).then_inc(act_done, 1)
                    n += 1
                act.wait_ge(dve_done, D("ln1a"))
                act.activation(rstd[:, :], rstd[:, :], ACT.Sqrt).then_inc(act_done, 1)
                for t in range(TT):
                    act.wait_ge(pe_done, Pn(f"x1T{t}0"))
                    act.activation(xT[:, 0:4, t * P:(t + 1) * P], quads(t), ACT.Copy).then_inc(act_done, 1)
                act.wait_ge(dve_done, D("logits"))
                act.activation(e_t[:, :, :], e_t[:, :, :], ACT.Exp).then_inc(act_done, 1)
                act.activation(x16[:, 0, :, :], x_nat[:, :, :], ACT.Copy, scale=X_SCALE).then_inc(act_done, 1)

                def experts(q):
                    PP = PE_PASS.of(q)
                    for n, (hf, k, i) in enumerate(GATHER[0::2]):
                        act.wait_ge(pe_pass, PP(f"xg{hf}{k}{i}"))
                        act.activation(xg[:, k, i, hf * 512:(hf + 1) * 512], bank[:, n % 3, :], ACT.Copy)\
                            .then_inc(act_pass, 1)
                    n = len(GATHER) // 2
                    for t in range(TT):
                        for c in range(2):
                            act.wait_ge(pe_pass, PP(f"g{t}{c}"))
                            act.activation(G[:, 4 * c:4 * c + 4, t * P:(t + 1) * P], quads(n % 3), ACT.Copy)\
                                .then_inc(act_pass, 1)
                            n += 1
                    with act.Fori(0, PAIRS) as pair:
                        r = q * PAIRS + pair
                        n0 = r * PAIR_CHUNKS
                        PR, DR = PE_PAIR.of(r), DVE_PAIR.of(r)

                        def high(c):
                            act.wait_ge(landed[c % STAGES],
                                        ((layer + 1) * FRONT_ROUNDS + r * PAIR_ROUNDS + (c // STAGES + 1)) * 16)
                            act.wait_ge(expert_done, n0 + (c + 1))
                            act.activation(parts16[c % STAGES][:, 0, :, :],
                                           ring[:, c % STAGES, :].rearrange("p (k c) -> p k c", c=512), ACT.Copy,
                                           scale=W_SCALE).then_inc(hi_done, 1)

                        def used(kind, j):
                            act.wait_ge(expert_done, n0 + (2 * PAIR_ORDER.index((kind, j)) + 2 + STAGES))

                        def silu(j):
                            used("gate", j)
                            act.activation(hid[:, j, :], bank[:, 4, :], ACT.Silu, scale=UNSCALE).then_inc(act_pair, 1)

                        def high_h(j):
                            act.wait_ge(dve_pair, DR(f"h{j}"))
                            act.activation(h16[:, j, 0, :], hid[:, j, :], ACT.Copy).then_inc(act_pair, 1)

                        def y_out(j):
                            used("down", j)
                            act.activation(yT[:, :, j, :], bank[:, 6, :].rearrange("p (m s) -> p m s", m=8), ACT.Copy,
                                           scale=UNSCALE).then_inc(act_pair, 1)

                        for c in range(4):
                            high(c)
                        silu(0)
                        high(4)
                        high(5)
                        high_h(0)
                        high(6)
                        high(7)
                        silu(1)
                        high(8)
                        high(9)
                        y_out(0)
                        high(10)
                        high(11)
                        high_h(1)
                        y_out(1)
                        for c in range(2):
                            act.wait_ge(pe_pair, PR(f"yT{c}"))
                            act.activation(yn[:, c * 512:(c + 1) * 512], bank[:, [7, 0][c], :], ACT.Copy)\
                                .then_inc(act_pair, 1)

                pass_loop(act, layer, experts, passes_reg)
                act.wait_ge(dve_done, D("ln2a"))
                act.activation(rstd[:, :], rstd[:, :], ACT.Sqrt).then_inc(act_done, 1)

        @block.vector
        def _(dve):
            V = nc.vector
            passes_reg = dve.alloc_register("dve_passes")
            dve.reg_mov(passes_reg, 0)
            dve.wait_ge(setup_landed, 32)
            dve.wait_ge(router_landed, 48)
            ang, turns = area[:, 0:TOK], area[:, 256:512]
            V.tensor_copy(turns, cos[:, :].bitcast(I32)).then_inc(rope_done, 1)
            dve.wait_ge(rope_done, 1)
            V.tensor_scalar(ang, turns, const("inv_freq"), None, ALU.mult).then_inc(rope_done, 1)
            dve.wait_ge(rope_done, 2)
            V.tensor_scalar(turns, ang, float(1 / (2 * np.pi)), ROUND, ALU.mult, ALU.add).then_inc(rope_done, 1)
            dve.wait_ge(rope_done, 3)
            V.tensor_scalar(turns, turns, -ROUND, None, ALU.add).then_inc(rope_done, 1)
            for i, c in enumerate((TWO_PI_A, TWO_PI_B, TWO_PI_C)):
                dve.wait_ge(rope_done, 4 + i)
                V.scalar_tensor_tensor(out=ang, in0=turns, scalar=-c, in1=ang, op0=ALU.mult, op1=ALU.add)\
                    .then_inc(rope_done, 1)
            dve.wait_ge(rope_done, 7)
            V.tensor_scalar(ang, ang, 3.1415925, -3.1415925, ALU.min, ALU.max).then_inc(rope_done, 1)
            dve.wait_ge(rope_act, 3)
            V.memset(stats[:, :, :, :], 0.0).then_inc(x_ready, 1)

            with dve.Fori(0, DEPTH) as layer:
                Pn, A, D = PE_PLAN.of(layer), ACT_PLAN.of(layer), DVE_PLAN.of(layer)

                def quads(b):
                    return bank[:, b, :].rearrange("p (k t) -> p k t", k=4)

                def own(step, n=None):
                    dve.wait_ge(dve_done, D(step, n))

                dve.wait_ge(x_ready, layer + 1)
                for t in range(TT):
                    dve.wait_ge(pe_done, Pn(f"xT{t}1"))
                    V.tensor_copy(xT[:, 4:8, t * P:(t + 1) * P], quads(4 + t)).then_inc(dve_done, 1)
                dve.wait_ge(act_done, A("soft"))
                V.scalar_tensor_tensor(out=zb, in0=zb, scalar=0.0, in1=lb, op0=ALU.min, op1=ALU.subtract)\
                    .then_inc(dve_done, 1)
                own("scan", 1)
                for h in range(HEADS):
                    V.tensor_tensor_scan(lb[:, h, :], const("keep"), zb[:, h, :], 0.0, ALU.mult, ALU.add)\
                        .then_inc(dve_done, 1)
                own("scan", 5)
                lb_c = lb.rearrange("p h (n c) -> p (h n) c", c=CHUNK)
                V.tensor_tensor(zb.rearrange("p h (n c) -> p (h n) c", c=CHUNK),
                                lb_c[:, :, CHUNK - 1:CHUNK].to_broadcast([P, HEADS * NCH, CHUNK]), lb_c, ALU.subtract)\
                    .then_inc(dve_done, 1)
                dve.wait_ge(act_done, A("decay"))
                V.tensor_copy(dec[:, :, :], q_t.rearrange("p h (n c) -> p h n c", c=CHUNK)[:, :, :, CHUNK - 1])\
                    .then_inc(dve_done, 1)
                own("last")
                for j in range(2):
                    dve.wait_ge(pe_done, Pn(f"q{j}"))
                    qv = q_t[:, 2 * j:2 * j + 2, :]
                    V.scalar_tensor_tensor(out=qv, in0=halves(4 + j), scalar=DK ** -0.5, in1=qv, op0=ALU.mult,
                                           op1=ALU.mult).then_inc(dve_done, 1)
                for j in range(2):
                    dve.wait_ge(pe_done, Pn(f"k{j}"))
                    for dst in (k_t, zb):
                        kv = dst[:, 2 * j:2 * j + 2, :]
                        V.tensor_tensor(kv, halves(6 + j), kv, ALU.mult).then_inc(dve_done, 1)
                dve.wait_ge(zeroed, layer + 1)
                for t in range(TT):
                    dve.wait_ge(pe_done, Pn(f"att{t}"))
                    apart(dve)
                    V.copy_predicated(attm[:, t, :, :], const("causal").bitcast(U32).unsqueeze(1)
                                      .to_broadcast([P, HEADS, P]), quads(4 + t)).then_inc(dve_done, 1)
                for c in range(NCH - 1):
                    for j in range(2):
                        dve.wait_ge(pe_done, Pn(f"upd{c}{j}"))
                        if c == 0:
                            V.tensor_copy(state[:, 0, 2 * j:2 * j + 2, :], halves(6 + j)).then_inc(dve_done, 1)
                        else:
                            own(f"upd{c - 1}{j}")
                            for i in range(2):
                                h = 2 * j + i
                                V.scalar_tensor_tensor(out=state[:, c, h, :], in0=state[:, c - 1, h, :],
                                                       scalar=dec[:, h, c:c + 1], in1=bank[:, 6 + j, i * DV:(i + 1) * DV],
                                                       op0=ALU.mult, op1=ALU.add).then_inc(dve_done, 1)
                dve.wait_ge(act_done, A("r3"))
                dve.wait_ge(small_landed, (layer + 1) * 64)
                for h in range(HEADS):
                    dve.wait_ge(act_done, A(f"sq{h}"))
                    for m in range(2):
                        V.scalar_tensor_tensor(out=oT[:, 2 * h + m, :], in0=bank[:, 4 + h, m * TOK:(m + 1) * TOK],
                                               scalar=gnorm[:, 2 * h + m:2 * h + m + 1], in1=oT[:, 2 * h + m, :],
                                               op0=ALU.mult, op1=ALU.mult).then_inc(dve_done, 1)
                for j in range(2):
                    dve.wait_ge(pe_done, Pn(f"ss{j}"))
                    V.tensor_scalar(rms[:, 2 * j:2 * j + 2, :], halves(3 if j == 0 else 2), 1.0 / DV, RMS_EPS,
                                    ALU.mult, ALU.add).then_inc(dve_done, 1)
                for j in range(2):
                    dve.wait_ge(act_done, A(f"rms{j}"))
                    rj = rms[:, 2 * j:2 * j + 2, :]
                    V.reciprocal(rj, rj).then_inc(dve_done, 1)
                    own(f"on{j}", 1)
                    ov = oT[:, 4 * j:4 * j + 4, :].rearrange("p (h m) t -> p h m t", m=2)
                    V.tensor_tensor(ov, ov, rj.unsqueeze(2).to_broadcast([P, 2, 2, TOK]), ALU.mult).then_inc(dve_done, 1)
                cosb = cos[:, :].unsqueeze(1).to_broadcast([P, 2, TOK])
                sinb = sin[:, :].unsqueeze(1).to_broadcast([P, 2, TOK])
                for i in range(12):
                    dst = qk[:, 2 * i:2 * i + 2, :]
                    dve.wait_ge(pe_done, Pn(f"rot{i}"))
                    if i:
                        own(f"rope{i - 1}")
                    V.tensor_tensor(dst, raw[:, i % 2, :, :], cosb, ALU.mult).then_inc(dve_done, 1)
                    V.tensor_tensor(rtmp, halves(4 + i % 4), sinb, ALU.mult).then_inc(dve_done, 1)
                    own(f"rope{i}", 2)
                    V.tensor_tensor(dst, dst, rtmp, ALU.add).then_inc(dve_done, 1)
                own("rope11")

                def attention_out(qt):
                    dve.wait_ge(act_done, A(f"ex{8 * qt + 7}"))
                    V.reciprocal(rl[:, 8 * qt:8 * qt + 8], psum_l[:, 8 * qt:8 * qt + 8]).then_inc(dve_done, 1)
                    dve.wait_ge(pe_done, Pn(f"pv{8 * qt + 7}"))
                    own(f"an{qt}", 1)
                    V.tensor_tensor(att_n[:, qt, :].rearrange("p (h e) -> p h e", h=AH),
                                    bank[:, 3, :].rearrange("p (h e) -> p h e", h=AH),
                                    rl[:, 8 * qt:8 * qt + 8].unsqueeze(2).to_broadcast([P, AH, HD]), ALU.mult)\
                        .then_inc(dve_done, 1)

                for i, (qt, h) in enumerate(UNITS):
                    nk = (qt + 1) * P
                    b = 4 + 2 * (i % 2)
                    dve.wait_ge(pe_done, Pn(f"S{i}"))
                    if i >= 2:
                        dve.wait_ge(pe_done, Pn(f"pt{i - 2}{UNITS[i - 2][0]}"))
                    apart(dve)
                    scores = bank[:, b:b + 2, :].rearrange("p b (g k) -> p (b g) k", g=2)[:, 0:3, 0:nk]
                    mask = const("mask").rearrange("p (g k) -> p g k", g=3)[:, :, TOK - nk:TOK]
                    V.tensor_tensor_reduce(prob[:, i % 2, 0:3 * nk].rearrange("p (g k) -> p g k", g=3), scores, mask,
                                           1.0, -3e38, ALU.add, ALU.max, top[:, i:i + 1]).then_inc(dve_done, 1)
                    own(f"sc{i}", 1)
                    V.tensor_scalar(ntop[:, i:i + 1], top[:, i:i + 1], -(HD ** -0.5), None, ALU.mult)\
                        .then_inc(dve_done, 1)
                    if i == 10:
                        attention_out(0)
                attention_out(1)
                for j in range(4):
                    dve.wait_ge(pe_done, Pn(f"yg{j}"))
                    dve.wait_ge(act_done, A(f"gt{j}"))
                    V.tensor_tensor(mixT[:, 2 * j:2 * j + 2, :], halves(4 + j), gateT[:, 2 * j:2 * j + 2, :], ALU.mult)\
                        .then_inc(dve_done, 1)
                for j in range(4):
                    dve.wait_ge(pe_done, Pn(f"ya{j}"))
                    dve.wait_ge(act_done, A(f"gt{4 + j}"))
                    own("yg3") if j == 0 else own(f"ya{j - 1}")
                    V.tensor_tensor(mtmp, halves(4 + j), gateT[:, 8 + 2 * j:10 + 2 * j, :], ALU.mult)\
                        .then_inc(dve_done, 1)
                    own(f"ya{j}", 1)
                    V.tensor_tensor(mixT[:, 2 * j:2 * j + 2, :], mixT[:, 2 * j:2 * j + 2, :], mtmp, ALU.add)\
                        .then_inc(dve_done, 1)
                for c in range(2):
                    for t in range(TT):
                        dve.wait_ge(pe_done, Pn(f"mo{c}{t}"))
                        xv = x_nat[:, t, c * 512:(c + 1) * 512]
                        V.scalar_tensor_tensor(out=xv, in0=xv, scalar=ALPHA, in1=bank[:, 4 + 2 * c + t, :],
                                               op0=ALU.mult, op1=ALU.add).then_inc(dve_done, 1)

                def layer_norm(w, src, params_landed, last_sem):
                    for t in range(TT):
                        for c in range(2):
                            V.bn_stats(stats[:, t, c, :], src[:, t, c * 512:(c + 1) * 512]).then_inc(dve_done, 1)
                    own(w + "a", 4)
                    apart(dve)
                    for t in range(TT):
                        V.bn_aggr(mv[:, t, :], stats[:, t, :, :].rearrange("p c s -> p (c s)")).then_inc(dve_done, 1)
                    own(w + "a", 6)
                    V.tensor_scalar(rstd[:, :], mv[:, :, 1], LN_EPS, None, ALU.add).then_inc(dve_done, 1)
                    dve.wait_ge(act_done, A(w))
                    V.reciprocal(rstd[:, :], rstd[:, :]).then_inc(dve_done, 1)
                    own(w + "r")
                    dve.wait_ge(params_landed, (layer + 1) * 32)
                    for t in range(TT):
                        xv = x_nat[:, t, :]
                        V.tensor_scalar(xv, src[:, t, :], mv[:, t, 0:1], rstd[:, t:t + 1], ALU.subtract, ALU.mult)\
                            .then_inc(dve_done, 1)
                        own(f"{w}n{t}", 1)
                        V.tensor_tensor(xv, xv, lnp[:, 0, :], ALU.mult).then_inc(dve_done, 1)
                        own(f"{w}n{t}", 2)
                        V.tensor_tensor(xv, xv, lnp[:, 1, :], ALU.add).then_inc(dve_done, 1)

                own("mo11")
                layer_norm("ln1", x_nat, ln1_landed, None)
                for t in range(TT):
                    dve.wait_ge(pe_done, Pn(f"x1T{t}1"))
                    V.tensor_copy(xT[:, 4:8, t * P:(t + 1) * P], quads(4 + t)).then_inc(dve_done, 1)
                V.tensor_scalar(xacc[:, :, :], x_nat[:, :, :], ALPHA, None, ALU.mult).then_inc(dve_done, 1)

                two_b = two[:, 0:2].unsqueeze(2).to_broadcast([P, TT, E])
                dve.wait_ge(pe_done, Pn("logits"))
                V.tensor_tensor(e_t[:, :, :], bank[:, 6, 0:TT * E].rearrange("p (t e) -> p t e", t=TT),
                                b_r[:, :].unsqueeze(1).to_broadcast([P, TT, E]), ALU.add).then_inc(dve_done, 1)
                own("logits", 1)
                V.tensor_reduce(two[:, 0:2], e_t[:, :, :], AX.X, ALU.max).then_inc(dve_done, 1)
                own("logits", 2)
                V.tensor_tensor(e_t[:, :, :], e_t[:, :, :], two_b, ALU.subtract).then_inc(dve_done, 1)
                dve.wait_ge(act_done, A("router"))
                e_f = e_t[:, :, :].rearrange("p t e -> p (t e)")
                n = 0

                def gate_step(ins):
                    ins.then_inc(dve_done, 1)

                def places(v, groups):
                    v4 = v.rearrange("p (g i) -> p g i", i=EG)
                    first = v4.unsqueeze(3).to_broadcast([P, groups, EG, EG])
                    other = v4.unsqueeze(2).to_broadcast([P, groups, EG, EG])
                    a = cmp_a[:, 0:groups * 16].rearrange("p (g i j) -> p g i j", i=EG, j=EG)
                    b = cmp_b[:, 0:groups * 16].rearrange("p (g i j) -> p g i j", i=EG, j=EG)
                    return first, other, a, b

                sel_f = sel[:, :, :].rearrange("p t e -> p (t e)")
                rk_f = rk[:, :, :].rearrange("p t e -> p (t e)")
                for v, groups, dst, limit, base in ((e_f, 8, rk_f, 1.5, 0), (g_s[:, :], 2, g_r[:, :], 0.5, 8)):
                    first, other, a, b = places(v, groups)
                    if base:
                        own("gate", base)
                    V.tensor_tensor(a, other, first, ALU.is_gt).then_inc(dve_done, 1)
                    V.tensor_tensor(b, other, first, ALU.is_equal).then_inc(dve_done, 1)
                    own("gate", base + 2)
                    bf = cmp_b[:, 0:groups * 16].rearrange("p (g c) -> p g c", g=groups)
                    V.tensor_tensor(bf, bf, const("lower").unsqueeze(1).to_broadcast([P, groups, 16]), ALU.mult)\
                        .then_inc(dve_done, 1)
                    own("gate", base + 3)
                    af = cmp_a[:, 0:groups * 16]
                    V.tensor_tensor(af, af, cmp_b[:, 0:groups * 16], ALU.add).then_inc(dve_done, 1)
                    own("gate", base + 4)
                    V.tensor_reduce(dst, af.rearrange("p (c j) -> p c j", j=EG), AX.X, ALU.add).then_inc(dve_done, 1)
                    own("gate", base + 5)
                    V.tensor_scalar(dst, dst, limit, None, ALU.is_lt).then_inc(dve_done, 1)
                    own("gate", base + 6)
                    if base == 0:
                        V.tensor_tensor(e_f, e_f, rk_f, ALU.mult).then_inc(dve_done, 1)
                        own("gate", 7)
                        V.tensor_reduce(g_s[:, :], e_f.rearrange("p (g i) -> p g i", i=EG), AX.X, ALU.add)\
                            .then_inc(dve_done, 1)
                in_group = g_r[:, :].unsqueeze(2).to_broadcast([P, 8, EG])
                g4 = dict(i=EG)
                V.tensor_tensor(sel_f.rearrange("p (g i) -> p g i", **g4), rk_f.rearrange("p (g i) -> p g i", **g4),
                                in_group, ALU.mult).then_inc(dve_done, 1)
                V.tensor_tensor(e_f.rearrange("p (g i) -> p g i", **g4), e_f.rearrange("p (g i) -> p g i", **g4),
                                in_group, ALU.mult).then_inc(dve_done, 1)
                own("gate", 16)
                V.tensor_reduce(two[:, 2:4], e_t[:, :, :], AX.X, ALU.add).then_inc(dve_done, 1)
                own("gate", 17)
                V.reciprocal(two[:, 0:2], two[:, 2:4]).then_inc(dve_done, 1)
                own("gate", 18)
                V.tensor_tensor(comb[:, :, :], e_t[:, :, :], two_b, ALU.mult).then_inc(dve_done, 1)
                dve.wait_ge(pe_done, Pn("rank"))
                V.scalar_tensor_tensor(out=pm[:, :, :], in0=bank[:, 7, 0:TT * E].rearrange("p (t e) -> p t e", t=TT),
                                       scalar=1.0, in1=sel[:, :, :], op0=ALU.add, op1=ALU.mult).then_inc(dve_done, 1)
                own("rank", 1)
                V.tensor_scalar(pm[:, :, :], pm[:, :, :], -1.0, None, ALU.add).then_inc(dve_done, 1)
                V.tensor_reduce(lim[:, 0:1], bank[0:1, 7, 2 * E:3 * E], AX.X, ALU.max).then_inc(dve_done, 1)
                own("passes", 1)
                V.tensor_scalar(lim[:, 1:4], const("limits", 1), lim[:, 0:1], None, ALU.is_lt).then_inc(dve_done, 1)
                own("passes", 2)
                V.tensor_reduce(lim[:, 0:1], lim[:, 1:4], AX.X, ALU.add).then_inc(dve_done, 1)
                own("passes", 3)
                V.tensor_scalar(passes_sb[:, :], lim[:, 0:1], 1.0, None, ALU.add).then_inc(dve_done, 1)
                dve.wait_ge(act_done, A("x_hi"))
                V.scalar_tensor_tensor(out=x16[:, 1, :, :], in0=x_nat[:, :, :], scalar=X_SCALE, in1=x16[:, 0, :, :],
                                       op0=ALU.mult, op1=ALU.subtract).then_inc(dve_done, 1)

                def experts(q):
                    PP, DP = PE_PASS.of(q), DVE_PASS.of(q)
                    for t in range(TT):
                        V.tensor_tensor(S[:, t, :, :], const("slot").unsqueeze(1).to_broadcast([P, E, SLOTS]),
                                        pm[:, t, :].unsqueeze(2).to_broadcast([P, E, SLOTS]), ALU.is_equal)\
                            .then_inc(dve_pass, 1)
                    dve.wait_ge(dve_pass, DP("S1"))
                    for t in range(TT):
                        V.tensor_tensor(S_gated[:, t, :, :], S[:, t, :, :],
                                        comb[:, t, :].unsqueeze(2).to_broadcast([P, E, SLOTS]), ALU.mult)\
                            .then_inc(dve_pass, 1)
                    for n, (hf, k, i) in enumerate(GATHER[1::2]):
                        dve.wait_ge(pe_pass, PP(f"xg{hf}{k}{i}"))
                        V.tensor_copy(xg[:, k, i, hf * 512:(hf + 1) * 512], bank[:, 4 + n % 4, :]).then_inc(dve_pass, 1)
                    V.tensor_scalar(pm[:, :, :], pm[:, :, :], float(-SLOTS), None, ALU.add).then_inc(dve_pass, 1)
                    dve.wait_ge(act_pass, ACT_PASS.of(q)("g11"))
                    dve.wait_ge(dve_pass, DP("next"))
                    apart(dve)
                    with dve.Fori(0, PAIRS) as pair:
                        r = q * PAIRS + pair
                        n0 = r * PAIR_CHUNKS
                        PR, AR, DR = PE_PAIR.of(r), ACT_PAIR.of(r), DVE_PAIR.of(r)

                        def low(c):
                            dve.wait_ge(hi_done, n0 + (c + 1))
                            w = parts16[c % STAGES]
                            V.scalar_tensor_tensor(out=w[:, 1, :, :],
                                                   in0=ring[:, c % STAGES, :].rearrange("p (k c) -> p k c", c=512),
                                                   scalar=W_SCALE, in1=w[:, 0, :, :], op0=ALU.mult,
                                                   op1=ALU.subtract).then_inc(split_done, 1)

                        def hidden(j):
                            dve.wait_ge(expert_done, n0 + (2 * PAIR_ORDER.index(("up", j)) + 2 + STAGES))
                            dve.wait_ge(act_pair, AR(f"silu{j}"))
                            V.scalar_tensor_tensor(out=hid[:, j, :], in0=bank[:, 5, :], scalar=UNSCALE * X_SCALE,
                                                   in1=hid[:, j, :], op0=ALU.mult, op1=ALU.mult).then_inc(dve_pair, 1)

                        def low_h(j):
                            dve.wait_ge(act_pair, AR(f"hh{j}"))
                            V.tensor_tensor(h16[:, j, 1, :], hid[:, j, :], h16[:, j, 0, :], ALU.subtract)\
                                .then_inc(dve_pair, 1)

                        V.tensor_copy(x_pair.rearrange("p k i s -> p (k i) s"),
                                      xg.rearrange("p k i s -> p (k i) s")[:, :, bass.ds(pair * (2 * SLOTS), 2 * SLOTS)])\
                            .then_inc(dve_pair, 1)
                        for c in range(5):
                            low(c)
                        hidden(0)
                        low(5)
                        low_h(0)
                        for c in range(6, 11):
                            low(c)
                        hidden(1)
                        low(11)
                        low_h(1)
                        V.tensor_copy(G_pair[:, :], G[:, bass.ds(pair, 1), :].rearrange("p o t -> p (o t)"))\
                            .then_inc(dve_pair, 1)
                        dve.wait_ge(dve_pair, DR("G"))
                        for t in range(TT):
                            for c in range(2):
                                dve.wait_ge(pe_pair, PR(f"y{t}{c}"))
                                xv = xacc[:, t, c * 512:(c + 1) * 512]
                                V.tensor_tensor(xv, xv, bank[:, [1, 2, 3, 7][2 * t + c], :], ALU.add)\
                                    .then_inc(dve_pair, 1)
                    dve.wait_ge(dve_pair, DVE_PAIR.of(q * PAIRS + (PAIRS - 1))("y11"))
                    apart(dve)

                pass_loop(dve, layer, experts, passes_reg)
                layer_norm("ln2", xacc, ln2_landed, None)
                own("ln2n1")
                V.memset(stats[:, :, :, :], 0.0).then_inc(x_ready, 1)


_INS = ["x", "positions", "w_in", "w_alpha_up", "b_alpha", "gla_norm", "w_gla_o", "w_att_o", "w_out", "ln1_g", "ln1_b",
        "w_router", "b_router", "w_e_gate", "w_e_up", "w_e_down", "ln2_g", "ln2_b"]


def kernel(**inputs):
    import concourse.bacc as bacc
    from concourse.bass_utils import run_bass_kernel_spmd as run

    nc = bacc.Bacc("TRN2", target_bir_lowering=False, num_devices=1)
    arrays, args = {}, []
    for name in _INS + ["constants"]:
        a = constant_table() if name == "constants" else np.ascontiguousarray(inputs[name])
        arrays[f"in_{name}"] = a
        args.append(nc.dram_tensor(f"in_{name}", a.shape, mybir.dt.from_np(a.dtype), kind="ExternalInput").ap())
    out = nc.dram_tensor("out_0", (1, TOK, DM), F32, kind="ExternalOutput").ap()
    build(nc, *args, out)
    r = run(nc, [arrays], core_ids=[0])
    return r.results[0]["out_0"]
```

```python
from contextlib import ExitStack

import numpy as np
import concourse.bass as bass
from concourse import mybir

F32 = mybir.dt.float32
F16 = mybir.dt.float16
I32 = mybir.dt.int32
U32 = mybir.dt.uint32
ALU = mybir.AluOpType
ACT = mybir.ActivationFunctionType
AX = mybir.AxisListType

P = 128
TOK = 256
TT = TOK // P
DM = 1024
KT = DM // P
DEPTH = 2
HEADS, DK, DV, RANK, TAU = 4, 128, 256, 16, 16.0
CHUNK = 64
NCH = TOK // CHUNK
GROUPS, AH, HD = 3, 8, 64
E, EG, SLOTS = 16, 4, 64
PAIRS = E // 2
FF = 1024
LN_EPS, RMS_EPS = 1e-5, 1e-6
ALPHA = float((2 * DEPTH) ** 0.25)
NEG = -1e30
A_COL = 2 * HEADS * DK + 2 * HEADS * DV
D_COL = A_COL + RANK
STAGES = 3
CW = 4096
FRONT_CHUNKS = 24
PAIR_CHUNKS = 12
assert FRONT_CHUNKS % STAGES == 0 and PAIR_CHUNKS % STAGES == 0
W_SCALE, X_SCALE = 64.0, 16.0
UNSCALE = 1.0 / (W_SCALE * X_SCALE)
TWO_PI_A = 6.28125
TWO_PI_B = 0.0019350051879882812
TWO_PI_C = float(2 * np.pi - TWO_PI_A - TWO_PI_B)
ROUND = 12582912.0

CONST = {}
_at = 0
for _name, _n in (("ident", P), ("ones", P), ("rot", P), ("before", P), ("causal", P), ("mask", GROUPS * TOK),
                  ("keep", TOK), ("slot", SLOTS), ("lower", EG * EG), ("inv_freq", 1), ("half_pi", 1),
                  ("limits", 3)):
    CONST[_name] = (_at, _at + _n)
    _at += _n
CONST_W = _at


def constant_table():
    t = np.zeros((P, CONST_W), np.float32)
    p = np.arange(P)

    def put(name, v):
        t[:, CONST[name][0]:CONST[name][1]] = v

    put("ident", np.eye(P))
    put("ones", 1.0)
    rot = np.zeros((P, P))
    for m in range(P):
        if m % HD < HD // 2:
            rot[m + HD // 2, m] = -1.0
        else:
            rot[m - HD // 2, m] = 1.0
    put("rot", rot)
    put("before", p[:, None] < p[None, :])
    put("causal", (p[:, None] <= p[None, :]) & (p[:, None] // CHUNK == p[None, :] // CHUNK))
    dist = (P + p)[:, None] - np.arange(TOK)[None, :]
    near = [(dist >= 0) & (dist <= 128), (dist >= 0) & (dist % 4 == 0), (dist >= 0) & (dist % 16 == 0)]
    put("mask", np.concatenate([np.where(m, 0.0, NEG) for m in near], axis=1))
    put("keep", (np.arange(TOK) % CHUNK != 0)[None, :])
    put("slot", np.arange(SLOTS)[None, :])
    i = np.arange(EG)
    put("lower", (i[None, :] < i[:, None]).reshape(1, -1))
    put("inv_freq", np.power(np.float32(10000.0), -(2 * (p % (HD // 2))).astype(np.float32) / np.float32(HD))[:, None])
    put("half_pi", np.pi / 2)
    put("limits", (np.arange(1, 4) * SLOTS)[None, :])
    return t


class Plan:

    def __init__(self, steps):
        self.start, self.size, n = {}, {}, 0
        for name, k in steps:
            assert name not in self.start, name
            self.start[name], self.size[name] = n, k
            n += k
        self.total = n

    def of(self, base):
        return lambda name, k=None: base * self.total + (self.start[name] + (self.size[name] if k is None else k))


UNITS = [(qt, h) for qt in range(TT) for h in range(AH)]

LAST_JOB = {"q1": 0, "k1": 1, "v01": 2, "v11": 3, "r1": 4, "r3": 5}
LAST_JOB.update({f"raw{2 * j + 1}": 6 + j for j in range(6)})
LAST_JOB.update({f"vd{g}1": 12 + g for g in range(GROUPS)})
LAST_JOB.update({f"gt{2 * j + 1}": 15 + j for j in range(4)})
LAST_JOB.update({"yg1": 19, "yg3": 20, "ya3": 21, "mo01": 22, "mo11": 23})

TURN_1 = (["z0", "z1", "a"] + [f"v{c}{t}" for c in range(2) for t in range(TT)] + [f"r{j}" for j in range(4)]
          + ["ks0", "ks1"])
TURN_2 = (["raw10", "raw11", "ss1"] + [f"vd{g}{t}" for g in range(GROUPS) for t in range(TT)]
          + [f"pt{u}{j}" for u in range(16) for j in range(UNITS[u][0] + 1)]
          + ["gt0", "gt1", "at0", "at1"] + [f"gt{j}" for j in range(2, 8)])
BANK, BEFORE = {}, {}
for _turn in (TURN_1, TURN_2):
    for _i, _name in enumerate(_turn):
        BANK[_name] = _i % 3
        BEFORE[_name] = _turn[_i - 3] if _i >= 3 else None

PE_PLAN = Plan([(name, 0 if name in LAST_JOB else 1) for name in
    [f"xT{t}{c}" for t in range(TT) for c in range(2)] + ["a", "z0", "z1"]
    + [f"{n}{j}" for n in "qk" for j in range(2)] + [f"v{c}{t}" for c in range(2) for t in range(TT)]
    + [f"r{j}" for j in range(4)] + ["ks0", "ks1", "att0", "att1"]
    + [f"upd{n}{j}" for n in range(NCH - 1) for j in range(2)] + [f"o{h}" for h in range(HEADS)] + ["ss0", "ss1"]
    + [s for i in range(13) for s in ([f"raw{i}"] if i < 12 else []) + ([f"rot{i - 1}"] if i else [])]
    + [f"vd{g}{t}" for g in range(GROUPS) for t in range(TT)]
    + [s for i in range(19) for s in
       ([f"S{i}"] if i < 16 else [])
       + ([f"pt{i - 1}{j}" for j in range(UNITS[i - 1][0] + 1)] if 1 <= i <= 16 else [])
       + ([f"pv{i - 3}"] if i >= 3 else [])]
    + ["gt0", "gt1", "at0", "at1"] + [f"gt{j}" for j in range(2, 8)]
    + [f"yg{j}" for j in range(4)] + [f"ya{j}" for j in range(4)]
    + [f"mo{c}{t}" for c in range(2) for t in range(TT)]
    + [f"x1T{t}{c}" for t in range(TT) for c in range(2)] + ["logits", "rank"]])

ACT_PLAN = Plan(
    [(f"xT{t}{c}", 1) for t in range(TT) for c in range(2)]
    + [("aT", 1), ("z0", 2), ("z1", 2), ("soft", 3), ("decay", 3)]
    + [(f"v{c}{t}", 1) for c in range(2) for t in range(TT)] + [(f"r{j}", 1) for j in range(4)]
    + [("ksn0", 1), ("ksn1", 1)] + [(f"sq{h}", 1) for h in range(HEADS)] + [("rms0", 1), ("rms1", 1), ("alpha_x", 1)]
    + [(f"raw{i}", 1) for i in range(12)] + [(f"vd{g}{t}", 1) for g in range(GROUPS) for t in range(TT)]
    + [s for i in range(17) for s in
       ([(f"pt{i - 1}", UNITS[i - 1][0] + 1)] if i else []) + ([(f"ex{i}", 1)] if i < 16 else [])]
    + [("gt0", 1), ("gt1", 1), ("at0", 1), ("at1", 1), ("o_hi", 1)] + [(f"gt{j}", 1) for j in range(2, 8)]
    + [(f"mix{j}", 1) for j in range(4)] + [("ln1", 1)] + [(f"x1T{t}{c}", 1) for t in range(TT) for c in range(2)]
    + [("router", 1), ("x_hi", 1), ("xacc", 1), ("ln2", 1)])

DVE_PLAN = Plan(
    [("wa", 2)] + [(f"xT{t}{c}", 1) for t in range(TT) for c in range(2)]
    + [("scan", 6), ("last", 1), ("qt0", 1), ("qt1", 1), ("kt0", 2), ("kt1", 2)]
    + [("attm0", 1), ("attm1", 1)] + [("upd00", 1), ("upd01", 1)]
    + [(f"upd{n}{j}", 2) for n in range(1, NCH - 1) for j in range(2)] + [(f"o{h}", 2) for h in range(HEADS)]
    + [("ms0", 1), ("ms1", 1), ("on0", 2), ("on1", 2)] + [(f"rope{i}", 3) for i in range(12)]
    + [(f"vd{g}{t}", 1) for g in range(GROUPS) for t in range(TT)]
    + [s for i in range(18) for s in ([(f"pt{i - 2}", UNITS[i - 2][0] + 1)] if i >= 2 else [])
       + ([(f"sc{i}", 2)] if i < 16 else []) + ([("an0", 2)] if i == 10 else [])]
    + [("an1", 2), ("at0", 1), ("at1", 1), ("o_lo", 1)]
    + [(f"yg{j}", 1) for j in range(4)] + [("ya0", 2), ("ya1", 2), ("mix0", 1), ("ya2", 2), ("mix1", 1), ("ya3", 2)]
    + [("mix2", 1), ("mix3", 1)] + [(f"mo{c}{t}", 1) for c in range(2) for t in range(TT)]
    + [("ln1a", 7), ("ln1r", 1), ("ln1n0", 2), ("ln1n1", 2)] + [(f"x1T{t}{c}", 1) for t in range(TT) for c in range(2)]
    + [("logits", 3), ("gate", 19), ("rank", 2), ("passes", 4), ("x_lo", 1)]
    + [("ln2a", 7), ("ln2r", 1), ("ln2n0", 2), ("ln2n1", 2)])

GATHER = [(h, k, part) for h in range(2) for k in range(KT) for part in range(2)]
PE_PASS = Plan([(f"xg{h}{k}{i}", 1) for h, k, i in GATHER] + [(f"g{t}{c}", 1) for t in range(TT) for c in range(2)])
ACT_PASS = Plan([(f"xg{h}{k}{i}", 1) for h, k, i in GATHER[0::2]]
                + [(f"g{t}{c}", 1) for t in range(TT) for c in range(2)])
DVE_PASS = Plan([("S0", 1), ("S1", 1)] + [(f"xg{h}{k}{i}", 1) for h, k, i in GATHER[1::2]]
                + [("gated", 2), ("next", 1)])
ACT_PAIR = Plan([("silu0", 1), ("hh0", 1), ("silu1", 1), ("yT0", 1), ("hh1", 1)])
DVE_PAIR = Plan([("x", 1), ("h0", 1), ("hl0", 1), ("h1", 1), ("hl1", 1)])
PE_TAIL = Plan([("yT0", 1), ("yT1", 1)] + [(f"y{t}{c}", 1) for t in range(TT) for c in range(2)])
ACT_TAIL = Plan([("yT1", 1), ("yn0", 1), ("yn1", 1)])
DVE_TAIL = Plan([("G", 1)] + [(f"y{t}{c}", 1) for t in range(TT) for c in range(2)])
PRODUCTS = ((0, 0), (0, 1), (1, 0))
PAIR_ORDER = [("gate", 0), ("up", 0), ("gate", 1), ("down", 0), ("up", 1), ("down", 1)]


def build(nc, x, positions, w_in, w_alpha_up, b_alpha, gla_norm, w_gla_o, w_att_o, w_out, ln1_g, ln1_b,
          w_router, b_router, w_e_gate, w_e_up, w_e_down, ln2_g, ln2_b, constants, out):
    with ExitStack() as ctx:
        def sb(name, shape, dt=F32):
            return ctx.enter_context(nc.sbuf_tensor(name, shape, dt))

        def sem(name):
            return ctx.enter_context(nc.semaphore(name))

        ctx.enter_context(nc.allow_non_contiguous_dma("small strided parameter loads"))

        ring = sb("ring", [P, 2 * STAGES, CW])
        x_nat = sb("x_nat", [P, TT, DM])
        xacc = sb("xacc", [P, TT, DM])
        xT = sb("xT", [P, KT, 2, TOK], F16)
        area = sb("area", [P, 16384])
        cst = sb("cst", [P, CONST_W])
        lnp = sb("lnp", [P, 2, DM])
        cos = sb("cos", [P, TOK])
        sin = sb("sin", [P, TOK])
        w_a = sb("w_a", [P, KT, RANK])
        w_a16 = sb("w_a16", [P, 2, KT, RANK], F16)
        w_au = sb("w_au", [RANK, HEADS * DK])
        b_al = sb("b_al", [P, HEADS])
        gnorm = sb("gnorm", [P, 8])
        w_r16 = sb("w_r16", [P, 2, KT, E], F16)
        b_r = sb("b_r", [P, E])
        dec = sb("dec", [P, HEADS, NCH])
        G_pair = sb("G_pair", [P, TOK])
        stats = sb("stats", [P, TT, 2, 6])
        mv = sb("mv", [P, TT, 2])
        rstd = sb("rstd", [P, TT])
        top = sb("top", [P, 16])
        ntop = sb("ntop", [P, 16])
        psum_l = sb("psum_l", [P, 16])
        rl = sb("rl", [P, 16])
        e_t = sb("e_t", [P, TT, E])
        sel = sb("sel", [P, TT, E])
        comb = sb("comb", [P, TT, E])
        rk = sb("rk", [P, TT, E])
        pm = sb("pm", [P, TT, E])
        g_s = sb("g_s", [P, 8])
        g_r = sb("g_r", [P, 8])
        two = sb("two", [P, 4])
        lim = sb("lim", [1, 4])
        passes_sb = sb("passes_sb", [1, 1], I32)
        bank = ctx.enter_context(nc.psum_tensor("bank", [P, 8, 512], F32))

        def part(a, width, pattern=None, **kw):
            v = area[:, a:a + width]
            return v.rearrange(pattern, **kw) if pattern else v

        zb = part(0, 1024, "p (h t) -> p h t", h=HEADS)
        lb = part(1024, 1024, "p (h t) -> p h t", h=HEADS)
        q_t = part(2048, 1024, "p (h t) -> p h t", h=HEADS)
        k_t = part(3072, 1024, "p (h t) -> p h t", h=HEADS)
        v_g = part(4096, 2048, "p (t c) -> p t c", t=TT)
        ks_n = part(6144, 1024, "p (t h d) -> p t h d", t=TT, h=HEADS)
        attm = part(7168, 1024, "p (t h i) -> p t h i", t=TT, h=HEADS)
        state = part(8192, 3072, "p (n h v) -> p n h v", n=3, h=HEADS)
        sq = part(11264, 2048, "p (m t) -> p m t", m=8)
        rms = part(13312, 1024, "p (h t) -> p h t", h=HEADS)
        oT = part(14336, 2048, "p (m t) -> p m t", m=8)
        aT = area[0:RANK, 11264:11264 + TOK]
        w_r = part(512, KT * E, "p (k e) -> p k e", k=KT)
        qk = part(0, 6144, "p (c t) -> p c t", c=24)
        v_d = part(6144, 3072).bitcast(F16).rearrange("p (t i c) -> p t i c", t=TT, i=2)
        raw = part(9216, 1024, "p (b c t) -> p b c t", b=2, c=2)
        rtmp = part(10240, 512, "p (c t) -> p c t", c=2)
        prob = part(9216, 1536, "p (b c) -> p b c", b=2)
        probT = part(10752, 1536).bitcast(F16).rearrange("p (b c i q) -> p b c i q", b=2, c=6, i=2)
        att_n = part(12288, 1024, "p (t c) -> p t c", t=TT)
        gateT = part(0, 4096, "p (c t) -> p c t", c=16)
        mixT = part(4096, 2048, "p (c t) -> p c t", c=8)
        mtmp = part(6144, 512, "p (c t) -> p c t", c=2)
        o16 = part(7168, 2048).bitcast(F16).rearrange("p (k i t) -> p k i t", k=8, i=2)
        att16 = part(9216, 1024).bitcast(F16).rearrange("p (k i t) -> p k i t", k=4, i=2)
        mix16 = part(10240, 2048).bitcast(F16).rearrange("p (k i t) -> p k i t", k=8, i=2)
        cmp_a, cmp_b = part(12288, 128), part(12416, 128)
        xg = part(0, 8192).bitcast(F16).rearrange("p (k i s) -> p k i s", k=KT, i=2)
        S = part(8192, 1024).bitcast(F16).rearrange("p (t e s) -> p t e s", t=TT, e=E)
        x_pair = part(9216, 1024).bitcast(F16).rearrange("p (k i s) -> p k i s", k=KT, i=2)
        G = part(10240, 2048, "p (r t) -> p r t", r=PAIRS)
        hid = part(12288, 1024, "p (j c) -> p j c", j=2)
        h16 = part(13312, 1024).bitcast(F16).rearrange("p (j i c) -> p j i c", j=2, i=2)
        S_gated = part(14336, 2048, "p (t e s) -> p t e s", t=TT, e=E)
        yT = part(14336, 1024, "p (m j s) -> p m j s", m=8, j=2)
        yn = part(15360, 1024)

        def const(name, rows=P):
            a, b = CONST[name]
            return cst[0:rows, a:b]

        ident, ones = const("ident"), const("ones")
        x16 = xT[:, :, :, :].rearrange("p k i t -> p (k i t)").rearrange("p (i t d) -> p i t d", i=2, t=TT)

        def staged(c, width=512):
            return ring[:, c % STAGES, :].rearrange("p (k c) -> p k c", c=width)

        def parts(c, width=512):
            return ring[:, STAGES + c % STAGES, :].bitcast(F16).rearrange("p (i k c) -> p i k c", i=2, c=width)

        def halves(b):
            return bank[:, b, :].rearrange("p (c t) -> p c t", c=2)

        setup_landed = sem("setup_landed")
        small_landed = sem("small_landed")
        small_ready = sem("small_ready")
        ln1_landed = sem("ln1_landed")
        ln2_landed = sem("ln2_landed")
        landed = [sem(f"chunk_landed{s}") for s in range(STAGES)]
        hi_done = sem("hi_done")
        split_done = sem("split_done")
        chunk_done = sem("chunk_done")
        x_ready = sem("x_ready")
        zeroed = sem("zeroed")
        rope_done = sem("rope_tables")
        rope_act = sem("rope_tables_act")
        pe_done, act_done, dve_done = sem("pe_done"), sem("act_done"), sem("dve_done")
        pe_pass, act_pass, dve_pass = sem("pe_pass"), sem("act_pass"), sem("dve_pass")
        act_pair, dve_pair = sem("act_pair"), sem("dve_pair")
        pe_tail, act_tail, dve_tail = sem("pe_tail"), sem("act_tail"), sem("dve_tail")
        w_r_split = sem("w_r_split")
        out_done = sem("out_done")
        apart_sem = sem("apart")

        block = ctx.enter_context(nc.Block())

        def apart(eng):
            eng.sem_inc(apart_sem, 1)

        def pass_loop(eng, layer, body, passes_reg):
            before = eng.snap(passes_reg)
            eng.wait_ge(dve_done, DVE_PLAN.of(layer)("passes"))
            apart(eng)
            n = eng.value_load(passes_sb[0:1, 0:1], min_val=1, max_val=TOK // SLOTS)
            with eng.Fori(0, n) as p:
                body(before + p)
            eng.reg_add(passes_reg, passes_reg, n)

        def stream_place(layer, passes):
            return layer * FRONT_CHUNKS + passes * (PAIRS * PAIR_CHUNKS)

        def pe_steps(layer, before):
            count = PE_PLAN.of(layer)
            return lambda name: ((chunk_done, before + (LAST_JOB[name] + 1 + STAGES)) if name in LAST_JOB
                                 else (pe_done, count(name)))

        def slot_loads(before, c):
            return (before // STAGES + (c // STAGES + 1)) * 16

        def high(act, before, c):
            act.wait_ge(landed[c % STAGES], slot_loads(before, c))
            act.wait_ge(chunk_done, before + (c + 1))
            nc.scalar.activation(parts(c)[:, 0, :, :], staged(c), ACT.Copy, scale=W_SCALE).then_inc(hi_done, 1)

        def low(dve, before, c):
            dve.wait_ge(hi_done, before + (c + 1))
            nc.vector.scalar_tensor_tensor(out=parts(c)[:, 1, :, :], in0=staged(c), scalar=W_SCALE,
                                           in1=parts(c)[:, 0, :, :], op0=ALU.mult, op1=ALU.subtract)\
                .then_inc(split_done, 1)

        w_in_v = w_in.rearrange("l (k p) c -> p l k c", p=P)
        gla_o_v = w_gla_o.rearrange("l (k p) c -> p l k c", p=P)
        att_o_v = w_att_o.rearrange("l (k p) c -> p l k c", p=P)
        out_v = w_out.rearrange("l (k p) c -> p l k c", p=P)
        expert_v = {"gate": w_e_gate.rearrange("l e (k p) c -> p (l e) k c", p=P),
                    "up": w_e_up.rearrange("l e (k p) c -> p (l e) k c", p=P),
                    "down": w_e_down.rearrange("l e (k p) c -> p (l e) k c", p=P)}
        starts = [c * 512 for c in range(A_COL // 512)] + [D_COL + c * 512 for c in range(13)]
        front = [(w_in_v, s, 512) for s in starts] + [(gla_o_v, 0, 512), (gla_o_v, 512, 512), (att_o_v, 0, 1024),
                                                      (out_v, 0, 512), (out_v, 512, 512)]
        assert len(front) == FRONT_CHUNKS

        def small_params(layer):
            return [(w_a[:, :, :], w_in_v[:, bass.ds(layer, 1), :, A_COL:A_COL + RANK]
                     .rearrange("p o k c -> p (o k) c")),
                    (w_au[:, :], w_alpha_up[bass.ds(layer, 1), :, :].rearrange("o r c -> (o r) c")),
                    (b_al[:, :], b_alpha[bass.ds(layer, 1), :].rearrange("o (h p) -> p (o h)", p=P)),
                    (gnorm[:, :], gla_norm[bass.ds(layer, 1), :].rearrange("o (h p) -> p (o h)", p=P))]

        SETUP_LOADS = 5 + len(small_params(0))

        @block.sync
        def _(sp):
            passes_reg = sp.alloc_register("sp_passes")
            sp.reg_mov(passes_reg, 0)
            sp.dma_start(x_nat[:, :, :], x[0, :, :].rearrange("(t p) d -> p t d", p=P)).then_inc(setup_landed, 16)
            sp.dma_start(cst[:, :], constants).then_inc(setup_landed, 16)
            sp.dma_start(cos[:, :].bitcast(I32), positions[0:1, :].partition_broadcast(P)
                         .rearrange("a o e -> a (o e)")).then_inc(setup_landed, 16)
            sp.dma_start(w_r, w_router.rearrange("(k p) e -> p k e", p=P)).then_inc(setup_landed, 16)
            sp.dma_start(b_r[:, :], b_router.rearrange("(o e) -> o e", o=1).partition_broadcast(P)
                         .rearrange("a o e -> a (o e)")).then_inc(setup_landed, 16)
            for dst, src in small_params(0):
                sp.dma_start(dst, src).then_inc(setup_landed, 16)
            with sp.Fori(0, DEPTH) as layer:
                before = sp.snap(stream_place(layer, sp.snap(passes_reg)))
                for c, (w, col, width) in enumerate(front):
                    sp.wait_ge(split_done, before + (c + 1))
                    src = w[:, bass.ds(layer, 1), :, col:col + width].rearrange("p o k c -> p (o k) c")
                    sp.dma_start(staged(c, width), src).then_inc(landed[c % STAGES], 16)

                def experts(q):
                    with sp.Fori(0, PAIRS) as pair:
                        before = sp.snap((layer + 1) * FRONT_CHUNKS + (q * PAIRS + pair) * PAIR_CHUNKS)
                        for c in range(PAIR_CHUNKS):
                            kind, j = PAIR_ORDER[c // 2]
                            sp.wait_ge(split_done, before + (c + 1))
                            src = expert_v[kind][:, bass.ds(layer * E + pair * 2 + j, 1), :,
                                                 (c % 2) * 512:(c % 2) * 512 + 512].rearrange("p o k c -> p (o k) c")
                            sp.dma_start(staged(c), src).then_inc(landed[c % STAGES], 16)

                pass_loop(sp, layer, experts, passes_reg)
            for t in range(TT):
                sp.wait_ge(dve_done, DVE_PLAN.of(DEPTH - 1)(f"ln2n{t}"))
                sp.dma_start(out[0, t * P:(t + 1) * P, :], x_nat[:, t, :]).then_inc(out_done, 16)
            sp.wait_ge(out_done, TT * 16)

        @block.gpsimd
        def _(pool):
            pool.wait_ge(setup_landed, SETUP_LOADS * 16)
            pool.sem_inc(small_ready, 1)

            def norm_params(layer, gain, bias, signal):
                for i, w in enumerate((gain, bias)):
                    pool.dma_start(lnp[:, i, :], w[bass.ds(layer, 1), :].partition_broadcast(P)
                                   .rearrange("a o e -> a (o e)")).then_inc(signal, 16)

            def parameters(layer, more):
                pool.wait_ge(x_ready, layer + 1)
                apart(pool)
                norm_params(layer, ln1_g, ln1_b, ln1_landed)
                nc.gpsimd.memset(attm, 0.0).then_inc(zeroed, 1)
                if more:
                    pool.wait_ge(dve_done, DVE_PLAN.of(layer)("on1"))
                    apart(pool)
                    for dst, src in small_params(layer + 1):
                        pool.dma_start(dst, src).then_inc(small_landed, 16)
                    pool.wait_ge(small_landed, (layer + 1) * (16 * len(small_params(0))))
                    pool.sem_inc(small_ready, 1)
                pool.wait_ge(dve_done, DVE_PLAN.of(layer)("ln1n1"))
                apart(pool)
                norm_params(layer, ln2_g, ln2_b, ln2_landed)

            with pool.Fori(0, DEPTH - 1) as layer:
                parameters(layer, True)
            parameters(DEPTH - 1, False)

        @block.tensor
        def _(pe):
            passes_reg = pe.alloc_register("pe_passes")
            pe.reg_mov(passes_reg, 0)
            pe.sem_inc(split_done, STAGES)
            pe.sem_inc(chunk_done, STAGES)
            pe.wait_ge(setup_landed, SETUP_LOADS * 16)

            def transposes(b, sources):
                for i, s in enumerate(sources):
                    mm = pe.transpose(bank[:, b, i * P:(i + 1) * P], s, ident)
                return mm

            with pe.Fori(0, DEPTH) as layer:
                before = pe.snap(stream_place(layer, pe.snap(passes_reg)))
                count, A, D = PE_PLAN.of(layer), ACT_PLAN.of(layer), DVE_PLAN.of(layer)

                def ended(name, mm):
                    mm.then_inc(chunk_done if name in LAST_JOB else pe_done, 1)

                def arrived(c):
                    pe.wait_ge(split_done, before + (c + 1 + STAGES))

                def bank_free(name):
                    user = BEFORE[name]
                    if user is None:
                        return
                    if user.startswith(("vd", "at")):
                        pe.wait_ge(dve_done, D(user))
                    elif user.startswith("pt"):
                        pe.wait_ge(dve_done, D(user[:-1], int(user[-1]) + 1))
                    elif user == "ss1":
                        pe.wait_ge(dve_done, D("ms1"))
                    else:
                        pe.wait_ge(act_done, A({"a": "aT", "ks0": "ksn0", "ks1": "ksn1"}.get(user, user)))

                def features(b, half, w, col, rhs, kt=KT):
                    for k in range(kt):
                        for n, (wi, xi) in enumerate(PRODUCTS):
                            mm = pe.matmul(bank[:, b, half * TOK:(half + 1) * TOK], w[:, wi, k, col:col + P],
                                           rhs[:, k, xi, :], start=(k == 0 and n == 0),
                                           stop=(k == kt - 1 and n == 2))
                    return mm

                def two_tiles(b, w, j, rhs, kt=KT):
                    features(b, 0, w, 2 * j * P, rhs, kt)
                    return features(b, 1, w, (2 * j + 1) * P, rhs, kt)

                def tokens(b, t, w, lhs):
                    for k in range(KT):
                        for n, (wi, xi) in enumerate(PRODUCTS):
                            mm = pe.matmul(bank[:, b, :], lhs[:, k, xi, t * P:(t + 1) * P], w[:, wi, k, :],
                                           start=(k == 0 and n == 0), stop=(k == KT - 1 and n == 2))
                    return mm

                def x_transposed(step):
                    for t in range(TT):
                        if step == "x1T":
                            pe.wait_ge(dve_done, D(f"ln1n{t}"))
                        for c in range(2):
                            ended(f"{step}{t}{c}", transposes(4 * c + t, [x_nat[:, t, k * P:(k + 1) * P]
                                                                          for k in range(4 * c, 4 * c + 4)]))
                    pe.wait_ge(dve_done, D(f"{step}11"))

                pe.wait_ge(x_ready, layer + 1)
                x_transposed("xT")
                pe.wait_ge(dve_done, D("wa"))
                for k in range(KT):
                    for n, (wi, xi) in enumerate(PRODUCTS):
                        mm = pe.matmul(bank[0:RANK, 2, 0:TOK], w_a16[:, wi, k, :], xT[:, k, xi, :],
                                       start=(k == 0 and n == 0), stop=(k == KT - 1 and n == 2))
                ended("a", mm)
                pe.wait_ge(act_done, A("aT"))
                for j in range(2):
                    for i in range(2):
                        h = 2 * j + i
                        mm = pe.matmul(bank[:, j, i * TOK:(i + 1) * TOK], w_au[:, h * DK:(h + 1) * DK], aT,
                                       start=True, stop=True)
                    ended(f"z{j}", mm)
                for c in range(2):
                    arrived(c)
                    for j in range(2):
                        ended(f"{'qk'[c]}{j}", two_tiles(4 + 2 * c + j, parts(c), j, xT))
                for c in range(2, 4):
                    arrived(c)
                    for t in range(TT):
                        name = f"v{c - 2}{t}"
                        bank_free(name)
                        ended(name, tokens(BANK[name], t, parts(c), xT))
                for c in range(4, 6):
                    arrived(c)
                    for j in range(2):
                        name = f"r{2 * (c - 4) + j}"
                        bank_free(name)
                        ended(name, two_tiles(BANK[name], parts(c), j, xT))
                pe.wait_ge(dve_done, D("kt1"))
                for t in range(TT):
                    name = f"ks{t}"
                    bank_free(name)
                    ended(name, transposes(BANK[name], [zb[:, h, t * P:(t + 1) * P] for h in range(HEADS)]))
                for t in range(TT):
                    for h in range(HEADS):
                        mm = pe.matmul(bank[:, 4 + t, h * P:(h + 1) * P], k_t[:, h, t * P:(t + 1) * P],
                                       q_t[:, h, t * P:(t + 1) * P], start=True, stop=True)
                    ended(f"att{t}", mm)
                pe.wait_ge(act_done, A("ksn1"))
                for c in range(NCH - 1):
                    t, rows = c // 2, slice((c % 2) * CHUNK, (c % 2 + 1) * CHUNK)
                    for j in range(2):
                        if c:
                            pe.wait_ge(dve_done, D(f"upd{c - 1}{j}"))
                        for i in range(2):
                            h = 2 * j + i
                            mm = pe.matmul(bank[:, 6 + j, i * DV:(i + 1) * DV], ks_n[rows, t, h, :],
                                           v_g[rows, t, h * DV:(h + 1) * DV], start=True, stop=True)
                        ended(f"upd{c}{j}", mm)
                pe.wait_ge(dve_done, D("upd21"))
                for h in range(HEADS):
                    for m in range(2):
                        cols = slice(h * DV + m * P, h * DV + (m + 1) * P)
                        for t in range(TT):
                            pe.matmul(bank[:, 4 + h, m * TOK + t * P:m * TOK + (t + 1) * P], v_g[:, t, cols],
                                      attm[:, t, h, :], start=True, stop=False)
                            for c in range(max(2 * t, 1), 2 * t + 2):
                                mm = pe.matmul(bank[:, 4 + h, m * TOK + c * CHUNK:m * TOK + (c + 1) * CHUNK],
                                               state[:, c - 1, h, m * P:(m + 1) * P],
                                               q_t[:, h, c * CHUNK:(c + 1) * CHUNK], start=False, stop=(c == 2 * t + 1))
                    ended(f"o{h}", mm)
                for j in range(2):
                    pe.wait_ge(act_done, A(f"sq{2 * j + 1}"))
                    for i in range(2):
                        for m in range(2):
                            mm = pe.matmul(bank[:, 3 - j, i * TOK:(i + 1) * TOK], ones, sq[:, 4 * j + 2 * i + m, :],
                                           start=(m == 0), stop=(m == 1))
                    ended(f"ss{j}", mm)

                rope_free = [f"o{h}" for h in range(HEADS)]
                for i in range(13):
                    if i < 12:
                        c = 6 + i // 2
                        if i % 2 == 0:
                            arrived(c)
                        if i >= 2:
                            pe.wait_ge(act_done, A(f"raw{i - 2}"))
                        ended(f"raw{i}", two_tiles(i % 2, parts(c), i % 2, xT))
                    if i >= 1:
                        pe.wait_ge(act_done, A(f"raw{i - 1}"))
                        pe.wait_ge(dve_done, D(rope_free[(i - 1) % 4]))
                        mm = pe.matmul(bank[:, 4 + (i - 1) % 4, :], const("rot"),
                                       raw[:, (i - 1) % 2, :, :].rearrange("p c t -> p (c t)"), start=True, stop=True)
                        ended(f"rot{i - 1}", mm)
                        rope_free[(i - 1) % 4] = f"rope{i - 1}"
                for g in range(GROUPS):
                    arrived(12 + g)
                    for t in range(TT):
                        name = f"vd{g}{t}"
                        bank_free(name)
                        ended(name, tokens(BANK[name], t, parts(12 + g), xT))
                pe.wait_ge(dve_done, D("rope11"))
                for i in range(19):
                    if i < 16:
                        qt, h = UNITS[i]
                        if i >= 2:
                            pe.wait_ge(dve_done, D(f"sc{i - 2}"))
                        for g in range(GROUPS):
                            hh = g * AH + h
                            rows = slice((hh % 2) * HD, (hh % 2 + 1) * HD)
                            nk = (qt + 1) * P
                            b = 4 + 2 * (i % 2) + g // 2
                            mm = pe.matmul(bank[:, b, (g % 2) * TOK:(g % 2) * TOK + nk],
                                           qk[rows, hh // 2, qt * P:(qt + 1) * P], qk[rows, 12 + hh // 2, 0:nk],
                                           start=True, stop=True)
                        ended(f"S{i}", mm)
                    if 1 <= i <= 16:
                        u = i - 1
                        pe.wait_ge(act_done, A(f"ex{u}"))
                        for j in range(UNITS[u][0] + 1):
                            name = f"pt{u}{j}"
                            bank_free(name)
                            ended(name, transposes(BANK[name], [prob[:, u % 2, (3 * j + s) * P:(3 * j + s + 1) * P]
                                                                for s in range(3)]))
                    if i >= 3:
                        u = i - 3
                        qt, h = UNITS[u]
                        pe.wait_ge(dve_done, D(f"pt{u}"))
                        if u == 8:
                            pe.wait_ge(dve_done, D("an0"))
                        tiles = [(g, kt) for g in range(GROUPS) for kt in range(qt + 1)]
                        for s, (g, kt) in enumerate(tiles):
                            for n, (vi, pi) in enumerate(PRODUCTS):
                                mm = pe.matmul(bank[:, 3, h * HD:(h + 1) * HD], probT[:, u % 2, s, pi, :],
                                               v_d[:, kt, vi, g * 512 + h * HD:g * 512 + (h + 1) * HD],
                                               start=(s == 0 and n == 0), stop=(s == len(tiles) - 1 and n == 2))
                        ended(f"pv{u}", mm)
                for j in range(8):
                    c = 15 + j // 2
                    if j == 2:
                        for qt in range(TT):
                            pe.wait_ge(dve_done, D(f"an{qt}"))
                            name = f"at{qt}"
                            bank_free(name)
                            ended(name, transposes(BANK[name], [att_n[:, qt, k * P:(k + 1) * P] for k in range(4)]))
                    if j % 2 == 0:
                        arrived(c)
                    name = f"gt{j}"
                    bank_free(name)
                    ended(name, two_tiles(BANK[name], parts(c), j % 2, xT))
                pe.wait_ge(dve_done, D("o_lo"))
                for j in range(4):
                    if j % 2 == 0:
                        arrived(19 + j // 2)
                    ended(f"yg{j}", two_tiles(4 + j, parts(19 + j // 2), j % 2, o16))
                arrived(21)
                for j in range(4):
                    pe.wait_ge(dve_done, D(f"yg{j}"))
                    ended(f"ya{j}", two_tiles(4 + j, parts(21, 1024), j, att16, 4))
                pe.wait_ge(dve_done, D("mix3"))
                for c in range(2):
                    arrived(22 + c)
                    for t in range(TT):
                        ended(f"mo{c}{t}", tokens(4 + 2 * c + t, t, parts(22 + c), mix16))
                pe.wait_ge(act_done, A("gt7"))
                x_transposed("x1T")
                for t in range(TT):
                    for k in range(KT):
                        for n, (wi, xi) in enumerate(PRODUCTS):
                            mm = pe.matmul(bank[:, 6, t * E:(t + 1) * E], xT[:, k, xi, t * P:(t + 1) * P],
                                           w_r16[:, wi, k, :], start=(k == 0 and n == 0), stop=(k == KT - 1 and n == 2))
                ended("logits", mm)
                pe.wait_ge(dve_done, D("gate", 15))
                pe.matmul(bank[:, 7, 0:E], const("before"), sel[:, 0, :], start=True, stop=True)
                pe.matmul(bank[:, 7, E:2 * E], ones, sel[:, 0, :], start=True, stop=False)
                pe.matmul(bank[:, 7, E:2 * E], const("before"), sel[:, 1, :], start=False, stop=True)
                pe.matmul(bank[:, 7, 2 * E:3 * E], ones, sel[:, 0, :], start=True, stop=False)
                mm = pe.matmul(bank[:, 7, 2 * E:3 * E], ones, sel[:, 1, :], start=False, stop=True)
                ended("rank", mm)

                def experts(q):
                    AP_, DP = ACT_PASS.of(q), DVE_PASS.of(q)
                    pe.wait_ge(dve_done, D("x_lo"))
                    pe.wait_ge(dve_pass, DP("S1"))
                    last_a, last_d = [None] * 3, [None] * 4
                    na = nd = 0
                    for n, (hf, k, i) in enumerate(GATHER):
                        step = f"xg{hf}{k}{i}"
                        if n % 2 == 0:
                            if last_a[na % 3]:
                                pe.wait_ge(act_pass, AP_(last_a[na % 3]))
                            b, last_a[na % 3] = na % 3, step
                            na += 1
                        else:
                            if last_d[nd % 4]:
                                pe.wait_ge(dve_pass, DP(last_d[nd % 4]))
                            b, last_d[nd % 4] = 4 + nd % 4, step
                            nd += 1
                        for t in range(TT):
                            mm = pe.matmul(bank[:, b, :], x16[:, i, t, k * P:(k + 1) * P],
                                           S[:, t, hf * 8:(hf + 1) * 8, :].rearrange("p e s -> p (e s)"),
                                           start=(t == 0), stop=(t == TT - 1))
                        mm.then_inc(pe_pass, 1)
                    pe.wait_ge(dve_pass, DP("gated"))
                    for t in range(TT):
                        for c in range(2):
                            pe.wait_ge(act_pass, AP_(last_a[na % 3]))
                            transposes(na % 3, [S_gated[:, t, 2 * r:2 * r + 2, :].rearrange("p e s -> p (e s)")
                                                for r in range(4 * c, 4 * c + 4)]).then_inc(pe_pass, 1)
                            last_a[na % 3] = f"g{t}{c}"
                            na += 1
                    pe.wait_ge(act_pass, AP_("g11"))
                    pe.wait_ge(dve_pass, DP("next"))
                    apart(pe)

                    def y_to_slots(tail):
                        pe.wait_ge(act_tail, ACT_TAIL.of(tail)("yT1"))
                        for c in range(2):
                            transposes([7, 0][c], [yT[:, m, :, :].rearrange("p j s -> p (j s)")
                                                   for m in range(4 * c, 4 * c + 4)]).then_inc(pe_tail, 1)

                    def scatter(tail):
                        pe.wait_ge(act_tail, ACT_TAIL.of(tail)("yn1"))
                        pe.wait_ge(dve_tail, DVE_TAIL.of(tail)("G"))
                        for t in range(TT):
                            for c in range(2):
                                pe.matmul(bank[:, [1, 2, 3, 7][2 * t + c], :], G_pair[:, t * P:(t + 1) * P],
                                          yn[:, c * 512:(c + 1) * 512], start=True, stop=True).then_inc(pe_tail, 1)

                    with pe.Fori(0, PAIRS) as pair:
                        r = q * PAIRS + pair
                        tail = q * (PAIRS + 1) + pair
                        before = pe.snap((layer + 1) * FRONT_CHUNKS + r * PAIR_CHUNKS)
                        AR, DR = ACT_PAIR.of(r), DVE_PAIR.of(r)
                        pe.wait_ge(dve_pair, DR("x"))
                        for c in range(PAIR_CHUNKS):
                            kind, j = PAIR_ORDER[c // 2]
                            b = {"gate": 4, "up": 5, "down": 6}[kind]
                            if c % 2 == 0:
                                if kind == "gate" and j == 1:
                                    pe.wait_ge(act_pair, AR("silu0"))
                                if kind == "down":
                                    pe.wait_ge(dve_pair, DR(f"hl{j}"))
                                    if j == 1:
                                        pe.wait_ge(act_pair, AR("yT0"))
                                if kind == "up" and j == 1:
                                    pe.wait_ge(dve_pair, DR("h0"))
                            pe.wait_ge(split_done, before + (c + 1 + STAGES))
                            w = parts(c)
                            for m in range(4):
                                mo = (c % 2) * 4 + m
                                for k in range(KT):
                                    for n, (wi, xi) in enumerate(PRODUCTS):
                                        if kind == "down":
                                            rhs = h16[:, j, xi, k * SLOTS:(k + 1) * SLOTS]
                                        else:
                                            rhs = x_pair[:, k, xi, j * SLOTS:(j + 1) * SLOTS]
                                        mm = pe.matmul(bank[:, b, mo * SLOTS:(mo + 1) * SLOTS],
                                                       w[:, wi, k, m * P:(m + 1) * P], rhs,
                                                       start=(k == 0 and n == 0), stop=(k == KT - 1 and n == 2))
                            mm.then_inc(chunk_done, 1)
                            if c == 1:
                                y_to_slots(tail)
                            if c == 2:
                                scatter(tail)
                    last = q * (PAIRS + 1) + PAIRS
                    y_to_slots(last)
                    scatter(last)

                pass_loop(pe, layer, experts, passes_reg)

        @block.scalar
        def _(act):
            passes_reg = act.alloc_register("act_passes")
            act.reg_mov(passes_reg, 0)
            turns_left, scratch = xacc[:, 0, 0:TOK], xacc[:, 0, TOK:2 * TOK]
            act.wait_ge(rope_done, 8)
            act.activation(sin[:, :], turns_left, ACT.Sin).then_inc(rope_act, 1)
            act.activation(scratch, turns_left, ACT.Abs).then_inc(rope_act, 1)
            act.wait_ge(rope_act, 2)
            act.activation(cos[:, :], scratch, ACT.Sin, bias=const("half_pi"), scale=-1.0).then_inc(rope_act, 1)

            with act.Fori(0, DEPTH) as layer:
                before = act.snap(stream_place(layer, act.snap(passes_reg)))
                Pn, A, D = pe_steps(layer, before), ACT_PLAN.of(layer), DVE_PLAN.of(layer)

                def quads(b):
                    return bank[:, b, :].rearrange("p (k t) -> p k t", k=4)

                def x_high(step):
                    for t in range(TT):
                        for c in range(2):
                            act.wait_ge(*Pn(f"{step}{t}{c}"))
                            act.activation(xT[:, 4 * c:4 * c + 4, 0, t * P:(t + 1) * P], quads(4 * c + t), ACT.Copy,
                                           scale=X_SCALE).then_inc(act_done, 1)

                for c in range(3):
                    high(act, before, c)
                act.wait_ge(x_ready, layer + 1)
                x_high("xT")
                act.wait_ge(*Pn("a"))
                act.activation(aT, bank[0:RANK, 2, 0:TOK], ACT.Copy, scale=UNSCALE).then_inc(act_done, 1)
                for h in range(HEADS):
                    act.wait_ge(*Pn(f"z{h // 2}"))
                    act.activation(zb[:, h, :], bank[:, h // 2, (h % 2) * TOK:(h % 2 + 1) * TOK], ACT.Identity,
                                   bias=b_al[:, h:h + 1]).then_inc(act_done, 1)
                act.wait_ge(act_done, A("z1"))
                act.activation(lb, zb, ACT.Abs).then_inc(act_done, 1)
                act.wait_ge(act_done, A("soft", 1))
                act.activation(lb, lb, ACT.Exp, scale=-1.0).then_inc(act_done, 1)
                act.wait_ge(act_done, A("soft", 2))
                act.activation(lb, lb, ACT.Ln, bias=ones[:, 0:1]).then_inc(act_done, 1)
                act.wait_ge(dve_done, D("scan"))
                act.activation(q_t, lb, ACT.Exp, scale=1.0 / TAU).then_inc(act_done, 1)
                act.activation(k_t, lb, ACT.Exp, scale=-1.0 / TAU).then_inc(act_done, 1)
                act.activation(zb, zb, ACT.Exp, scale=1.0 / TAU).then_inc(act_done, 1)
                high(act, before, 3)
                high(act, before, 4)
                for c in range(2):
                    for t in range(TT):
                        name = f"v{c}{t}"
                        act.wait_ge(*Pn(name))
                        act.activation(v_g[:, t, c * 512:(c + 1) * 512], bank[:, BANK[name], :], ACT.Copy,
                                       scale=UNSCALE).then_inc(act_done, 1)
                    high(act, before, 5 + c)
                for j in range(4):
                    act.wait_ge(*Pn(f"r{j}"))
                    act.activation(oT[:, 2 * j:2 * j + 2, :], halves(BANK[f"r{j}"]), ACT.Silu, scale=UNSCALE)\
                        .then_inc(act_done, 1)
                    if j == 1:
                        high(act, before, 7)
                for t in range(TT):
                    act.wait_ge(*Pn(f"ks{t}"))
                    act.activation(ks_n[:, t, :, :], quads(BANK[f"ks{t}"]), ACT.Copy).then_inc(act_done, 1)
                high(act, before, 8)
                for h in range(HEADS):
                    act.wait_ge(*Pn(f"o{h}"))
                    act.activation(sq[:, 2 * h:2 * h + 2, :], halves(4 + h), ACT.Square).then_inc(act_done, 1)
                for j in range(2):
                    act.wait_ge(dve_done, D(f"ms{j}"))
                    act.activation(rms[:, 2 * j:2 * j + 2, :], rms[:, 2 * j:2 * j + 2, :], ACT.Sqrt).then_inc(act_done, 1)
                act.activation(x_nat[:, :, :], x_nat[:, :, :], ACT.Copy, scale=ALPHA).then_inc(act_done, 1)
                for i in range(12):
                    act.wait_ge(*Pn(f"raw{i}"))
                    if i >= 2:
                        act.wait_ge(dve_done, D(f"rope{i - 2}"))
                    act.activation(raw[:, i % 2, :, :], halves(i % 2), ACT.Copy, scale=UNSCALE).then_inc(act_done, 1)
                    if i % 2 == 1:
                        high(act, before, 9 + i // 2)
                for g in range(GROUPS):
                    for t in range(TT):
                        name = f"vd{g}{t}"
                        act.wait_ge(*Pn(name))
                        act.activation(v_d[:, t, 0, g * 512:(g + 1) * 512], bank[:, BANK[name], :], ACT.Copy,
                                       scale=X_SCALE * UNSCALE).then_inc(act_done, 1)
                    if g < 2:
                        high(act, before, 15 + g)
                for i in range(17):
                    if i >= 1:
                        u = i - 1
                        for j in range(UNITS[u][0] + 1):
                            act.wait_ge(*Pn(f"pt{u}{j}"))
                            if j == 0 and u >= 2:
                                act.wait_ge(*Pn(f"pv{u - 2}"))
                            act.activation(probT[:, u % 2, 3 * j:3 * j + 3, 0, :], quads(BANK[f"pt{u}{j}"])[:, 0:3, :],
                                           ACT.Copy, scale=X_SCALE).then_inc(act_done, 1)
                    if i < 16:
                        w = 3 * (UNITS[i][0] + 1) * P
                        act.wait_ge(dve_done, D(f"sc{i}"))
                        act.activation(prob[:, i % 2, 0:w], prob[:, i % 2, 0:w], ACT.Exp, bias=ntop[:, i:i + 1],
                                       scale=HD ** -0.5, accum_out=psum_l[:, i:i + 1]).then_inc(act_done, 1)
                    if i == 2:
                        high(act, before, 17)

                def gate(j):
                    act.wait_ge(*Pn(f"gt{j}"))
                    act.activation(gateT[:, 2 * j:2 * j + 2, :], halves(BANK[f"gt{j}"]), ACT.Sigmoid, scale=UNSCALE)\
                        .then_inc(act_done, 1)

                gate(0)
                gate(1)
                for qt in range(TT):
                    act.wait_ge(*Pn(f"at{qt}"))
                    act.activation(att16[:, :, 0, qt * P:(qt + 1) * P], quads(BANK[f"at{qt}"]), ACT.Copy,
                                   scale=1.0 / X_SCALE).then_inc(act_done, 1)
                high(act, before, 18)
                act.wait_ge(*Pn("pv15"))
                act.wait_ge(dve_done, D("on1"))
                act.activation(o16[:, :, 0, :], oT, ACT.Copy, scale=X_SCALE).then_inc(act_done, 1)
                for j in range(2, 8):
                    gate(j)
                    if j % 2 == 1:
                        high(act, before, 18 + j // 2)
                high(act, before, 22)
                high(act, before, 23)
                for j in range(4):
                    act.wait_ge(dve_done, D(f"ya{j}"))
                    act.activation(mix16[:, 2 * j:2 * j + 2, 0, :], mixT[:, 2 * j:2 * j + 2, :], ACT.Copy,
                                   scale=X_SCALE).then_inc(act_done, 1)
                act.wait_ge(dve_done, D("ln1a"))
                act.activation(rstd[:, :], rstd[:, :], ACT.Sqrt).then_inc(act_done, 1)
                x_high("x1T")
                act.wait_ge(dve_done, D("logits"))
                act.activation(e_t[:, :, :], e_t[:, :, :], ACT.Exp).then_inc(act_done, 1)
                act.activation(x16[:, 0, :, :], x_nat[:, :, :], ACT.Copy, scale=X_SCALE).then_inc(act_done, 1)
                act.activation(xacc[:, :, :], x_nat[:, :, :], ACT.Copy, scale=ALPHA).then_inc(act_done, 1)

                def experts(q):
                    PP = PE_PASS.of(q)
                    first = act.snap((layer + 1) * FRONT_CHUNKS + q * (PAIRS * PAIR_CHUNKS))
                    for c in range(3):
                        high(act, first, c)
                    for n, (hf, k, i) in enumerate(GATHER[0::2]):
                        act.wait_ge(pe_pass, PP(f"xg{hf}{k}{i}"))
                        act.activation(xg[:, k, i, hf * 512:(hf + 1) * 512], bank[:, n % 3, :], ACT.Copy)\
                            .then_inc(act_pass, 1)
                    n = len(GATHER) // 2
                    for t in range(TT):
                        for c in range(2):
                            act.wait_ge(pe_pass, PP(f"g{t}{c}"))
                            act.activation(G[:, 4 * c:4 * c + 4, t * P:(t + 1) * P], quads(n % 3), ACT.Copy)\
                                .then_inc(act_pass, 1)
                            n += 1

                    def y_out(done, j, signal):
                        act.wait_ge(chunk_done, done)
                        act.activation(yT[:, :, j, :], bank[:, 6, :].rearrange("p (m s) -> p m s", m=8), ACT.Copy,
                                       scale=UNSCALE).then_inc(signal, 1)

                    def slots_out(tail):
                        for c in range(2):
                            act.wait_ge(pe_tail, PE_TAIL.of(tail)(f"yT{c}"))
                            act.activation(yn[:, c * 512:(c + 1) * 512], bank[:, [7, 0][c], :], ACT.Copy)\
                                .then_inc(act_tail, 1)

                    def pair_steps(pair, last):
                        r = q * PAIRS + pair
                        before = act.snap((layer + 1) * FRONT_CHUNKS + r * PAIR_CHUNKS)
                        tail = q * (PAIRS + 1) + pair
                        DR = DVE_PAIR.of(r)

                        def used(kind, j):
                            return before + (2 * PAIR_ORDER.index((kind, j)) + 2 + STAGES)

                        def silu(j):
                            act.wait_ge(chunk_done, used("gate", j))
                            act.activation(hid[:, j, :], bank[:, 4, :], ACT.Silu, scale=UNSCALE).then_inc(act_pair, 1)

                        def high_h(j):
                            act.wait_ge(dve_pair, DR(f"h{j}"))
                            act.activation(h16[:, j, 0, :], hid[:, j, :], ACT.Copy).then_inc(act_pair, 1)

                        y_out(before + STAGES, 1, act_tail)
                        high(act, before, 3)
                        slots_out(tail)
                        silu(0)
                        high(act, before, 4)
                        high(act, before, 5)
                        high_h(0)
                        high(act, before, 6)
                        high(act, before, 7)
                        silu(1)
                        high(act, before, 8)
                        high(act, before, 9)
                        y_out(used("down", 0), 0, act_pair)
                        high(act, before, 10)
                        high(act, before, 11)
                        high_h(1)
                        if not last:
                            for c in range(PAIR_CHUNKS, PAIR_CHUNKS + 3):
                                high(act, before, c)

                    act.wait_ge(dve_pass, DVE_PASS.of(q)("next"))
                    apart(act)
                    with act.Fori(0, PAIRS - 1) as pair:
                        pair_steps(pair, False)
                    pair_steps(PAIRS - 1, True)
                    y_out((layer + 1) * FRONT_CHUNKS + (q * PAIRS + PAIRS) * PAIR_CHUNKS + STAGES, 1, act_tail)
                    slots_out(q * (PAIRS + 1) + PAIRS)

                pass_loop(act, layer, experts, passes_reg)
                act.wait_ge(dve_done, D("ln2a"))
                act.activation(rstd[:, :], rstd[:, :], ACT.Sqrt).then_inc(act_done, 1)

        @block.vector
        def _(dve):
            V = nc.vector
            passes_reg = dve.alloc_register("dve_passes")
            dve.reg_mov(passes_reg, 0)
            dve.wait_ge(setup_landed, SETUP_LOADS * 16)
            V.memset(stats[:, :, :, :], 0.0).then_inc(x_ready, 1)
            ang, turns = xacc[:, 0, 0:TOK], xacc[:, 0, TOK:2 * TOK]
            V.tensor_copy(turns, cos[:, :].bitcast(I32)).then_inc(rope_done, 1)
            dve.wait_ge(rope_done, 1)
            V.tensor_scalar(ang, turns, const("inv_freq"), None, ALU.mult).then_inc(rope_done, 1)
            dve.wait_ge(rope_done, 2)
            V.tensor_scalar(turns, ang, float(1 / (2 * np.pi)), ROUND, ALU.mult, ALU.add).then_inc(rope_done, 1)
            dve.wait_ge(rope_done, 3)
            V.tensor_scalar(turns, turns, -ROUND, None, ALU.add).then_inc(rope_done, 1)
            for i, c in enumerate((TWO_PI_A, TWO_PI_B, TWO_PI_C)):
                dve.wait_ge(rope_done, 4 + i)
                V.scalar_tensor_tensor(out=ang, in0=turns, scalar=-c, in1=ang, op0=ALU.mult, op1=ALU.add)\
                    .then_inc(rope_done, 1)
            dve.wait_ge(rope_done, 7)
            V.tensor_scalar(ang, ang, 3.1415925, -3.1415925, ALU.min, ALU.max).then_inc(rope_done, 1)
            V.tensor_scalar(w_r16[:, 0, :, :], w_r, W_SCALE, None, ALU.mult).then_inc(w_r_split, 1)
            dve.wait_ge(w_r_split, 1)
            V.scalar_tensor_tensor(out=w_r16[:, 1, :, :], in0=w_r, scalar=W_SCALE, in1=w_r16[:, 0, :, :],
                                   op0=ALU.mult, op1=ALU.subtract).then_inc(w_r_split, 1)

            with dve.Fori(0, DEPTH) as layer:
                before = dve.snap(stream_place(layer, dve.snap(passes_reg)))
                Pn, A, D = pe_steps(layer, before), ACT_PLAN.of(layer), DVE_PLAN.of(layer)

                def quads(b):
                    return bank[:, b, :].rearrange("p (k t) -> p k t", k=4)

                def own(step, n=None):
                    dve.wait_ge(dve_done, D(step, n))

                def low_part(out, src, scale):
                    hi, lo = out
                    V.scalar_tensor_tensor(out=lo, in0=src, scalar=scale, in1=hi, op0=ALU.mult, op1=ALU.subtract)\
                        .then_inc(dve_done, 1)

                def x_low(step):
                    for t in range(TT):
                        for c in range(2):
                            dve.wait_ge(act_done, A(f"{step}{t}{c}"))
                            xv = xT[:, 4 * c:4 * c + 4, :, t * P:(t + 1) * P]
                            low_part((xv[:, :, 0, :], xv[:, :, 1, :]), quads(4 * c + t), X_SCALE)

                dve.wait_ge(small_ready, layer + 1)
                V.tensor_scalar(w_a16[:, 0, :, :], w_a[:, :, :], W_SCALE, None, ALU.mult).then_inc(dve_done, 1)
                own("wa", 1)
                low_part((w_a16[:, 0, :, :], w_a16[:, 1, :, :]), w_a[:, :, :], W_SCALE)
                x_low("xT")
                low(dve, before, 0)
                low(dve, before, 1)
                dve.wait_ge(act_done, A("soft"))
                V.scalar_tensor_tensor(out=zb, in0=zb, scalar=0.0, in1=lb, op0=ALU.min, op1=ALU.subtract)\
                    .then_inc(dve_done, 1)
                own("scan", 1)
                for h in range(HEADS):
                    V.tensor_tensor_scan(lb[:, h, :], const("keep"), zb[:, h, :], 0.0, ALU.mult, ALU.add)\
                        .then_inc(dve_done, 1)
                own("scan", 5)
                lb_c = lb.rearrange("p h (n c) -> p (h n) c", c=CHUNK)
                V.tensor_tensor(zb.rearrange("p h (n c) -> p (h n) c", c=CHUNK),
                                lb_c[:, :, CHUNK - 1:CHUNK].to_broadcast([P, HEADS * NCH, CHUNK]), lb_c, ALU.subtract)\
                    .then_inc(dve_done, 1)
                dve.wait_ge(act_done, A("decay"))
                V.tensor_copy(dec[:, :, :], q_t.rearrange("p h (n c) -> p h n c", c=CHUNK)[:, :, :, CHUNK - 1])\
                    .then_inc(dve_done, 1)
                low(dve, before, 2)
                own("last")
                for j in range(2):
                    dve.wait_ge(*Pn(f"q{j}"))
                    qv = q_t[:, 2 * j:2 * j + 2, :]
                    V.scalar_tensor_tensor(out=qv, in0=halves(4 + j), scalar=DK ** -0.5 * UNSCALE, in1=qv, op0=ALU.mult,
                                           op1=ALU.mult).then_inc(dve_done, 1)
                low(dve, before, 3)
                for j in range(2):
                    dve.wait_ge(*Pn(f"k{j}"))
                    for dst in (k_t, zb):
                        kv = dst[:, 2 * j:2 * j + 2, :]
                        V.scalar_tensor_tensor(out=kv, in0=halves(6 + j), scalar=UNSCALE, in1=kv, op0=ALU.mult,
                                               op1=ALU.mult).then_inc(dve_done, 1)
                for c in range(4, 8):
                    low(dve, before, c)
                dve.wait_ge(zeroed, layer + 1)
                for t in range(TT):
                    dve.wait_ge(*Pn(f"att{t}"))
                    apart(dve)
                    V.copy_predicated(attm[:, t, :, :], const("causal").bitcast(U32).unsqueeze(1)
                                      .to_broadcast([P, HEADS, P]), quads(4 + t)).then_inc(dve_done, 1)
                for c in range(NCH - 1):
                    for j in range(2):
                        dve.wait_ge(*Pn(f"upd{c}{j}"))
                        if c == 0:
                            V.tensor_copy(state[:, 0, 2 * j:2 * j + 2, :], halves(6 + j)).then_inc(dve_done, 1)
                        else:
                            own(f"upd{c - 1}{j}")
                            for i in range(2):
                                h = 2 * j + i
                                V.scalar_tensor_tensor(out=state[:, c, h, :], in0=state[:, c - 1, h, :],
                                                       scalar=dec[:, h, c:c + 1], in1=bank[:, 6 + j, i * DV:(i + 1) * DV],
                                                       op0=ALU.mult, op1=ALU.add).then_inc(dve_done, 1)
                dve.wait_ge(act_done, A("r3"))
                for h in range(HEADS):
                    dve.wait_ge(act_done, A(f"sq{h}"))
                    for m in range(2):
                        V.scalar_tensor_tensor(out=oT[:, 2 * h + m, :], in0=bank[:, 4 + h, m * TOK:(m + 1) * TOK],
                                               scalar=gnorm[:, 2 * h + m:2 * h + m + 1], in1=oT[:, 2 * h + m, :],
                                               op0=ALU.mult, op1=ALU.mult).then_inc(dve_done, 1)
                for j in range(2):
                    dve.wait_ge(*Pn(f"ss{j}"))
                    V.tensor_scalar(rms[:, 2 * j:2 * j + 2, :], halves(3 if j == 0 else 2), 1.0 / DV, RMS_EPS,
                                    ALU.mult, ALU.add).then_inc(dve_done, 1)
                low(dve, before, 8)
                for j in range(2):
                    dve.wait_ge(act_done, A(f"rms{j}"))
                    rj = rms[:, 2 * j:2 * j + 2, :]
                    V.reciprocal(rj, rj).then_inc(dve_done, 1)
                    own(f"on{j}", 1)
                    ov = oT[:, 4 * j:4 * j + 4, :].rearrange("p (h m) t -> p h m t", m=2)
                    V.tensor_tensor(ov, ov, rj.unsqueeze(2).to_broadcast([P, 2, 2, TOK]), ALU.mult).then_inc(dve_done, 1)
                cosb = cos[:, :].unsqueeze(1).to_broadcast([P, 2, TOK])
                sinb = sin[:, :].unsqueeze(1).to_broadcast([P, 2, TOK])
                for i in range(12):
                    dst = qk[:, 2 * i:2 * i + 2, :]
                    dve.wait_ge(*Pn(f"rot{i}"))
                    if i:
                        own(f"rope{i - 1}")
                    V.tensor_tensor(dst, raw[:, i % 2, :, :], cosb, ALU.mult).then_inc(dve_done, 1)
                    V.tensor_tensor(rtmp, halves(4 + i % 4), sinb, ALU.mult).then_inc(dve_done, 1)
                    own(f"rope{i}", 2)
                    V.tensor_tensor(dst, dst, rtmp, ALU.add).then_inc(dve_done, 1)
                    if i % 2 == 0:
                        low(dve, before, 9 + i // 2)
                for g in range(GROUPS):
                    for t in range(TT):
                        name = f"vd{g}{t}"
                        dve.wait_ge(act_done, A(name))
                        vv = v_d[:, t, :, g * 512:(g + 1) * 512]
                        low_part((vv[:, 0, :], vv[:, 1, :]), bank[:, BANK[name], :], X_SCALE * UNSCALE)
                    if g < 2:
                        low(dve, before, 15 + g)
                own("rope11")

                def attention_out(qt):
                    dve.wait_ge(act_done, A(f"ex{8 * qt + 7}"))
                    V.reciprocal(rl[:, 8 * qt:8 * qt + 8], psum_l[:, 8 * qt:8 * qt + 8]).then_inc(dve_done, 1)
                    dve.wait_ge(*Pn(f"pv{8 * qt + 7}"))
                    own(f"an{qt}", 1)
                    V.tensor_tensor(att_n[:, qt, :].rearrange("p (h e) -> p h e", h=AH),
                                    bank[:, 3, :].rearrange("p (h e) -> p h e", h=AH),
                                    rl[:, 8 * qt:8 * qt + 8].unsqueeze(2).to_broadcast([P, AH, HD]), ALU.mult)\
                        .then_inc(dve_done, 1)

                def probabilities_low(u):
                    for j in range(UNITS[u][0] + 1):
                        dve.wait_ge(act_done, A(f"pt{u}", j + 1))
                        pv = probT[:, u % 2, 3 * j:3 * j + 3, :, :]
                        low_part((pv[:, :, 0, :], pv[:, :, 1, :]), quads(BANK[f"pt{u}{j}"])[:, 0:3, :], X_SCALE)

                for i, (qt, h) in enumerate(UNITS):
                    if i >= 2:
                        probabilities_low(i - 2)
                    nk = (qt + 1) * P
                    b = 4 + 2 * (i % 2)
                    dve.wait_ge(*Pn(f"S{i}"))
                    if i >= 2:
                        dve.wait_ge(*Pn(f"pt{i - 2}{UNITS[i - 2][0]}"))
                    apart(dve)
                    scores = bank[:, b:b + 2, :].rearrange("p b (g k) -> p (b g) k", g=2)[:, 0:3, 0:nk]
                    mask = const("mask").rearrange("p (g k) -> p g k", g=3)[:, :, TOK - nk:TOK]
                    V.tensor_tensor_reduce(prob[:, i % 2, 0:3 * nk].rearrange("p (g k) -> p g k", g=3), scores, mask,
                                           1.0, -3e38, ALU.add, ALU.max, top[:, i:i + 1]).then_inc(dve_done, 1)
                    own(f"sc{i}", 1)
                    V.tensor_scalar(ntop[:, i:i + 1], top[:, i:i + 1], -(HD ** -0.5), None, ALU.mult)\
                        .then_inc(dve_done, 1)
                    if i == 4:
                        low(dve, before, 17)
                    if i == 10:
                        attention_out(0)
                probabilities_low(14)
                probabilities_low(15)
                attention_out(1)
                for qt in range(TT):
                    dve.wait_ge(act_done, A(f"at{qt}"))
                    av = att16[:, :, :, qt * P:(qt + 1) * P]
                    low_part((av[:, :, 0, :], av[:, :, 1, :]), quads(BANK[f"at{qt}"]), 1.0 / X_SCALE)
                low(dve, before, 18)
                dve.wait_ge(act_done, A("o_hi"))
                low_part((o16[:, :, 0, :], o16[:, :, 1, :]), oT, X_SCALE)
                for c in range(19, 22):
                    low(dve, before, c)
                for j in range(4):
                    dve.wait_ge(*Pn(f"yg{j}"))
                    dve.wait_ge(act_done, A(f"gt{j}"))
                    V.scalar_tensor_tensor(out=mixT[:, 2 * j:2 * j + 2, :], in0=halves(4 + j), scalar=UNSCALE,
                                           in1=gateT[:, 2 * j:2 * j + 2, :], op0=ALU.mult, op1=ALU.mult)\
                        .then_inc(dve_done, 1)
                    if j % 2 == 1:
                        low(dve, before, 22 + j // 2)

                def attention_branch(j):
                    dve.wait_ge(*Pn(f"ya{j}"))
                    dve.wait_ge(act_done, A(f"gt{4 + j}"))
                    own("yg3") if j == 0 else own(f"ya{j - 1}")
                    V.scalar_tensor_tensor(out=mtmp, in0=halves(4 + j), scalar=UNSCALE,
                                           in1=gateT[:, 8 + 2 * j:10 + 2 * j, :], op0=ALU.mult, op1=ALU.mult)\
                        .then_inc(dve_done, 1)
                    own(f"ya{j}", 1)
                    V.tensor_tensor(mixT[:, 2 * j:2 * j + 2, :], mixT[:, 2 * j:2 * j + 2, :], mtmp, ALU.add)\
                        .then_inc(dve_done, 1)

                def mix_low(j):
                    dve.wait_ge(act_done, A(f"mix{j}"))
                    mv_ = mix16[:, 2 * j:2 * j + 2, :, :]
                    low_part((mv_[:, :, 0, :], mv_[:, :, 1, :]), mixT[:, 2 * j:2 * j + 2, :], X_SCALE)

                attention_branch(0)
                attention_branch(1)
                mix_low(0)
                attention_branch(2)
                mix_low(1)
                attention_branch(3)
                mix_low(2)
                mix_low(3)
                dve.wait_ge(act_done, A("alpha_x"))
                for c in range(2):
                    for t in range(TT):
                        dve.wait_ge(*Pn(f"mo{c}{t}"))
                        xv = x_nat[:, t, c * 512:(c + 1) * 512]
                        V.scalar_tensor_tensor(out=xv, in0=bank[:, 4 + 2 * c + t, :], scalar=UNSCALE, in1=xv,
                                               op0=ALU.mult, op1=ALU.add).then_inc(dve_done, 1)

                def layer_norm(w, src, params_landed, last_sem):
                    for t in range(TT):
                        for c in range(2):
                            V.bn_stats(stats[:, t, c, :], src[:, t, c * 512:(c + 1) * 512]).then_inc(dve_done, 1)
                    own(w + "a", 4)
                    apart(dve)
                    for t in range(TT):
                        V.bn_aggr(mv[:, t, :], stats[:, t, :, :].rearrange("p c s -> p (c s)")).then_inc(dve_done, 1)
                    own(w + "a", 6)
                    V.tensor_scalar(rstd[:, :], mv[:, :, 1], LN_EPS, None, ALU.add).then_inc(dve_done, 1)
                    dve.wait_ge(act_done, A(w))
                    V.reciprocal(rstd[:, :], rstd[:, :]).then_inc(dve_done, 1)
                    own(w + "r")
                    dve.wait_ge(params_landed, (layer + 1) * 32)
                    for t in range(TT):
                        xv = x_nat[:, t, :]
                        V.scalar_tensor_tensor(out=xv, in0=src[:, t, :], scalar=mv[:, t, 0:1], in1=lnp[:, 0, :],
                                               op0=ALU.subtract, op1=ALU.mult).then_inc(dve_done, 1)
                        own(f"{w}n{t}", 1)
                        V.scalar_tensor_tensor(out=xv, in0=xv, scalar=rstd[:, t:t + 1], in1=lnp[:, 1, :],
                                               op0=ALU.mult, op1=ALU.add).then_inc(dve_done, 1)

                own("mo11")
                layer_norm("ln1", x_nat, ln1_landed, None)
                x_low("x1T")

                two_b = two[:, 0:2].unsqueeze(2).to_broadcast([P, TT, E])
                dve.wait_ge(*Pn("logits"))
                V.scalar_tensor_tensor(out=e_t[:, :, :], in0=bank[:, 6, 0:TT * E].rearrange("p (t e) -> p t e", t=TT),
                                       scalar=UNSCALE, in1=b_r[:, :].unsqueeze(1).to_broadcast([P, TT, E]),
                                       op0=ALU.mult, op1=ALU.add).then_inc(dve_done, 1)
                own("logits", 1)
                V.tensor_reduce(two[:, 0:2], e_t[:, :, :], AX.X, ALU.max).then_inc(dve_done, 1)
                own("logits", 2)
                V.tensor_tensor(e_t[:, :, :], e_t[:, :, :], two_b, ALU.subtract).then_inc(dve_done, 1)
                dve.wait_ge(act_done, A("router"))
                e_f = e_t[:, :, :].rearrange("p t e -> p (t e)")
                n = 0

                def gate_step(ins):
                    ins.then_inc(dve_done, 1)

                def places(v, groups):
                    v4 = v.rearrange("p (g i) -> p g i", i=EG)
                    first = v4.unsqueeze(3).to_broadcast([P, groups, EG, EG])
                    other = v4.unsqueeze(2).to_broadcast([P, groups, EG, EG])
                    a = cmp_a[:, 0:groups * 16].rearrange("p (g i j) -> p g i j", i=EG, j=EG)
                    b = cmp_b[:, 0:groups * 16].rearrange("p (g i j) -> p g i j", i=EG, j=EG)
                    return first, other, a, b

                sel_f = sel[:, :, :].rearrange("p t e -> p (t e)")
                rk_f = rk[:, :, :].rearrange("p t e -> p (t e)")
                for v, groups, dst, limit, base in ((e_f, 8, rk_f, 1.5, 0), (g_s[:, :], 2, g_r[:, :], 0.5, 8)):
                    first, other, a, b = places(v, groups)
                    if base:
                        own("gate", base)
                    V.tensor_tensor(a, other, first, ALU.is_gt).then_inc(dve_done, 1)
                    V.tensor_tensor(b, other, first, ALU.is_equal).then_inc(dve_done, 1)
                    own("gate", base + 2)
                    bf = cmp_b[:, 0:groups * 16].rearrange("p (g c) -> p g c", g=groups)
                    V.tensor_tensor(bf, bf, const("lower").unsqueeze(1).to_broadcast([P, groups, 16]), ALU.mult)\
                        .then_inc(dve_done, 1)
                    own("gate", base + 3)
                    af = cmp_a[:, 0:groups * 16]
                    V.tensor_tensor(af, af, cmp_b[:, 0:groups * 16], ALU.add).then_inc(dve_done, 1)
                    own("gate", base + 4)
                    V.tensor_reduce(dst, af.rearrange("p (c j) -> p c j", j=EG), AX.X, ALU.add).then_inc(dve_done, 1)
                    own("gate", base + 5)
                    V.tensor_scalar(dst, dst, limit, None, ALU.is_lt).then_inc(dve_done, 1)
                    own("gate", base + 6)
                    if base == 0:
                        V.tensor_tensor(e_f, e_f, rk_f, ALU.mult).then_inc(dve_done, 1)
                        own("gate", 7)
                        V.tensor_reduce(g_s[:, :], e_f.rearrange("p (g i) -> p g i", i=EG), AX.X, ALU.add)\
                            .then_inc(dve_done, 1)
                in_group = g_r[:, :].unsqueeze(2).to_broadcast([P, 8, EG])
                g4 = dict(i=EG)
                V.tensor_tensor(sel_f.rearrange("p (g i) -> p g i", **g4), rk_f.rearrange("p (g i) -> p g i", **g4),
                                in_group, ALU.mult).then_inc(dve_done, 1)
                V.tensor_tensor(e_f.rearrange("p (g i) -> p g i", **g4), e_f.rearrange("p (g i) -> p g i", **g4),
                                in_group, ALU.mult).then_inc(dve_done, 1)
                own("gate", 16)
                V.tensor_reduce(two[:, 2:4], e_t[:, :, :], AX.X, ALU.add).then_inc(dve_done, 1)
                own("gate", 17)
                V.reciprocal(two[:, 0:2], two[:, 2:4]).then_inc(dve_done, 1)
                own("gate", 18)
                V.tensor_tensor(comb[:, :, :], e_t[:, :, :], two_b, ALU.mult).then_inc(dve_done, 1)
                dve.wait_ge(*Pn("rank"))
                V.scalar_tensor_tensor(out=pm[:, :, :], in0=bank[:, 7, 0:TT * E].rearrange("p (t e) -> p t e", t=TT),
                                       scalar=1.0, in1=sel[:, :, :], op0=ALU.add, op1=ALU.mult).then_inc(dve_done, 1)
                own("rank", 1)
                V.tensor_scalar(pm[:, :, :], pm[:, :, :], -1.0, None, ALU.add).then_inc(dve_done, 1)
                V.tensor_reduce(lim[:, 0:1], bank[0:1, 7, 2 * E:3 * E], AX.X, ALU.max).then_inc(dve_done, 1)
                own("passes", 1)
                V.tensor_scalar(lim[:, 1:4], const("limits", 1), lim[:, 0:1], None, ALU.is_lt).then_inc(dve_done, 1)
                own("passes", 2)
                V.tensor_reduce(lim[:, 0:1], lim[:, 1:4], AX.X, ALU.add).then_inc(dve_done, 1)
                own("passes", 3)
                V.tensor_scalar(passes_sb[:, :], lim[:, 0:1], 1.0, None, ALU.add).then_inc(dve_done, 1)
                dve.wait_ge(act_done, A("x_hi"))
                V.scalar_tensor_tensor(out=x16[:, 1, :, :], in0=x_nat[:, :, :], scalar=X_SCALE, in1=x16[:, 0, :, :],
                                       op0=ALU.mult, op1=ALU.subtract).then_inc(dve_done, 1)

                def experts(q):
                    PP, DP = PE_PASS.of(q), DVE_PASS.of(q)
                    first = dve.snap((layer + 1) * FRONT_CHUNKS + q * (PAIRS * PAIR_CHUNKS))
                    for t in range(TT):
                        V.tensor_tensor(S[:, t, :, :], const("slot").unsqueeze(1).to_broadcast([P, E, SLOTS]),
                                        pm[:, t, :].unsqueeze(2).to_broadcast([P, E, SLOTS]), ALU.is_equal)\
                            .then_inc(dve_pass, 1)
                    for n, (hf, k, i) in enumerate(GATHER[1::2]):
                        dve.wait_ge(pe_pass, PP(f"xg{hf}{k}{i}"))
                        V.tensor_copy(xg[:, k, i, hf * 512:(hf + 1) * 512], bank[:, 4 + n % 4, :]).then_inc(dve_pass, 1)
                        if n in (3, 7, 11):
                            low(dve, first, n // 4)
                    dve.wait_ge(dve_pass, DP("S1"))
                    for t in range(TT):
                        V.tensor_tensor(S_gated[:, t, :, :], S[:, t, :, :],
                                        comb[:, t, :].unsqueeze(2).to_broadcast([P, E, SLOTS]), ALU.mult)\
                            .then_inc(dve_pass, 1)
                    V.tensor_scalar(pm[:, :, :], pm[:, :, :], float(-SLOTS), None, ALU.add).then_inc(dve_pass, 1)
                    V.memset(G_pair[:, :], 0.0).then_inc(dve_tail, 1)

                    def add_y(tail):
                        for t in range(TT):
                            for c in range(2):
                                dve.wait_ge(pe_tail, PE_TAIL.of(tail)(f"y{t}{c}"))
                                xv = xacc[:, t, c * 512:(c + 1) * 512]
                                V.tensor_tensor(xv, xv, bank[:, [1, 2, 3, 7][2 * t + c], :], ALU.add)\
                                    .then_inc(dve_tail, 1)

                    def x_of(pair):
                        V.tensor_copy(x_pair.rearrange("p k i s -> p (k i) s"),
                                      xg.rearrange("p k i s -> p (k i) s")[:, :, bass.ds(pair * (2 * SLOTS), 2 * SLOTS)])\
                            .then_inc(dve_pair, 1)

                    def pair_steps(pair, last):
                        r = q * PAIRS + pair
                        before = dve.snap((layer + 1) * FRONT_CHUNKS + r * PAIR_CHUNKS)
                        AR = ACT_PAIR.of(r)

                        def hidden(j):
                            dve.wait_ge(chunk_done, before + (2 * PAIR_ORDER.index(("up", j)) + 2 + STAGES))
                            dve.wait_ge(act_pair, AR(f"silu{j}"))
                            V.scalar_tensor_tensor(out=hid[:, j, :], in0=bank[:, 5, :], scalar=UNSCALE * X_SCALE,
                                                   in1=hid[:, j, :], op0=ALU.mult, op1=ALU.mult).then_inc(dve_pair, 1)

                        def low_h(j):
                            dve.wait_ge(act_pair, AR(f"hh{j}"))
                            V.tensor_tensor(h16[:, j, 1, :], hid[:, j, :], h16[:, j, 0, :], ALU.subtract)\
                                .then_inc(dve_pair, 1)

                        low(dve, before, 3)
                        low(dve, before, 4)
                        hidden(0)
                        low(dve, before, 5)
                        low_h(0)
                        add_y(q * (PAIRS + 1) + pair)
                        V.tensor_copy(G_pair[:, :], G[:, bass.ds(pair, 1), :].rearrange("p o t -> p (o t)"))\
                            .then_inc(dve_tail, 1)
                        for c in range(6, 11):
                            low(dve, before, c)
                        hidden(1)
                        low(dve, before, 11)
                        low_h(1)
                        if not last:
                            x_of(pair + 1)
                            for c in range(PAIR_CHUNKS, PAIR_CHUNKS + 3):
                                low(dve, before, c)

                    dve.wait_ge(act_pass, ACT_PASS.of(q)("g11"))
                    dve.wait_ge(dve_pass, DP("next"))
                    dve.wait_ge(act_done, A("xacc"))
                    x_of(0)
                    with dve.Fori(0, PAIRS - 1) as pair:
                        pair_steps(pair, False)
                    pair_steps(PAIRS - 1, True)
                    last = q * (PAIRS + 1) + PAIRS
                    add_y(last)
                    dve.wait_ge(dve_tail, DVE_TAIL.of(last)("y11"))
                    apart(dve)

                pass_loop(dve, layer, experts, passes_reg)
                layer_norm("ln2", xacc, ln2_landed, None)
                own("ln2n1")
                V.memset(stats[:, :, :, :], 0.0).then_inc(x_ready, 1)


_INS = ["x", "positions", "w_in", "w_alpha_up", "b_alpha", "gla_norm", "w_gla_o", "w_att_o", "w_out", "ln1_g", "ln1_b",
        "w_router", "b_router", "w_e_gate", "w_e_up", "w_e_down", "ln2_g", "ln2_b"]


def kernel(**inputs):
    import concourse.bacc as bacc
    from concourse.bass_utils import run_bass_kernel_spmd as run

    nc = bacc.Bacc("TRN2", target_bir_lowering=False, num_devices=1)
    arrays, args = {}, []
    for name in _INS + ["constants"]:
        a = constant_table() if name == "constants" else np.ascontiguousarray(inputs[name])
        arrays[f"in_{name}"] = a
        args.append(nc.dram_tensor(f"in_{name}", a.shape, mybir.dt.from_np(a.dtype), kind="ExternalInput").ap())
    out = nc.dram_tensor("out_0", (1, TOK, DM), F32, kind="ExternalOutput").ap()
    build(nc, *args, out)
    r = run(nc, [arrays], core_ids=[0])
    return r.results[0]["out_0"]
```

```python
from contextlib import ExitStack

import numpy as np
import concourse.bass as bass
from concourse import mybir

F32 = mybir.dt.float32
F16 = mybir.dt.float16
I32 = mybir.dt.int32
U32 = mybir.dt.uint32
ALU = mybir.AluOpType
ACT = mybir.ActivationFunctionType
AX = mybir.AxisListType

P = 128
TOK = 256
TT = TOK // P
DM = 1024
KT = DM // P
DEPTH = 2
HEADS, DK, DV, RANK, TAU = 4, 128, 256, 16, 16.0
CHUNK = 64
NCH = TOK // CHUNK
GROUPS, AH, HD = 3, 8, 64
E, EG, SLOTS = 16, 4, 64
PAIRS = E // 2
FF = 1024
LN_EPS, RMS_EPS = 1e-5, 1e-6
ALPHA = float((2 * DEPTH) ** 0.25)
NEG = -1e30
A_COL = 2 * HEADS * DK + 2 * HEADS * DV
D_COL = A_COL + RANK
STAGES = 3
DEEP = 4
CW = 4096
FRONT_CHUNKS = 24
PAIR_CHUNKS = 12
assert FRONT_CHUNKS % STAGES == 0 and PAIR_CHUNKS % DEEP == 0
W_SCALE, X_SCALE = 64.0, 16.0
UNSCALE = 1.0 / (W_SCALE * X_SCALE)
TWO_PI_A = 6.28125
TWO_PI_B = 0.0019350051879882812
TWO_PI_C = float(2 * np.pi - TWO_PI_A - TWO_PI_B)
ROUND = 12582912.0

CONST = {}
_at = 0
for _name, _n in (("ident", P), ("ones", P), ("sign", 1), ("before", P), ("causal", P), ("mask", GROUPS * TOK),
                  ("keep", TOK), ("slot", SLOTS), ("lower", EG * EG), ("inv_freq", 1), ("half_pi", 1),
                  ("limits", 3)):
    CONST[_name] = (_at, _at + _n)
    _at += _n
CONST_W = _at


def constant_table():
    t = np.zeros((P, CONST_W), np.float32)
    p = np.arange(P)

    def put(name, v):
        t[:, CONST[name][0]:CONST[name][1]] = v

    put("ident", np.eye(P))
    put("ones", 1.0)
    put("sign", np.where(p % HD < HD // 2, -1.0, 1.0)[:, None])
    put("before", p[:, None] < p[None, :])
    put("causal", (p[:, None] <= p[None, :]) & (p[:, None] // CHUNK == p[None, :] // CHUNK))
    dist = (P + p)[:, None] - np.arange(TOK)[None, :]
    near = [(dist >= 0) & (dist <= 128), (dist >= 0) & (dist % 4 == 0), (dist >= 0) & (dist % 16 == 0)]
    put("mask", np.concatenate([np.where(m, 0.0, NEG) for m in near], axis=1))
    put("keep", (np.arange(TOK) % CHUNK != 0)[None, :])
    put("slot", np.arange(SLOTS)[None, :])
    i = np.arange(EG)
    put("lower", (i[None, :] < i[:, None]).reshape(1, -1))
    put("inv_freq", np.power(np.float32(10000.0), -(2 * (p % (HD // 2))).astype(np.float32) / np.float32(HD))[:, None])
    put("half_pi", np.pi / 2)
    put("limits", (np.arange(1, 4) * SLOTS)[None, :])
    return t


class Plan:

    def __init__(self, steps):
        self.start, self.size, n = {}, {}, 0
        for name, k in steps:
            assert name not in self.start, name
            self.start[name], self.size[name] = n, k
            n += k
        self.total = n

    def of(self, base):
        return lambda name, k=None: base * self.total + (self.start[name] + (self.size[name] if k is None else k))


UNITS = [(qt, h) for qt in range(TT) for h in range(AH)]

LAST_JOB = {"q1": 0, "k1": 1, "v01": 2, "v11": 3, "r1": 4, "r3": 5}
LAST_JOB.update({f"raw{2 * j + 1}": 6 + j for j in range(6)})
LAST_JOB.update({f"vd{g}1": 12 + g for g in range(GROUPS)})
LAST_JOB.update({f"gt{2 * j + 1}": 15 + j for j in range(4)})
LAST_JOB.update({"yg1": 19, "yg3": 20, "ya3": 21, "mo01": 22, "mo11": 23})

VALUES = [f"vd{g}{t}" for g in range(GROUPS) for t in range(TT)]
TURNS = [((0, 1, 2), ["z0", "z1", "a"] + [f"v{c}{t}" for c in range(2) for t in range(TT)]
          + [f"r{j}" for j in range(4)] + ["ks0", "ks1"]),
         ((0, 1, 2), ["raw10", "raw11", "ks0"] + VALUES),
         ((0, 1), VALUES[-3:-1] + [f"pt{u}{j}" for u in range(16) for j in range(UNITS[u][0] + 1)] + ["at0", "at1"]),
         ((2,), VALUES[-1:] + [f"gt{j}" for j in range(8)])]
BANK, BEFORE = {}, {}
for _banks, _turn in TURNS:
    for _i, _name in enumerate(_turn):
        _bank = _banks[_i % len(_banks)]
        assert BANK.setdefault(_name, _bank) == _bank
        if _i >= len(_banks):
            BEFORE[_name] = _turn[_i - len(_banks)]

PE_PLAN = Plan([(name, 0 if name in LAST_JOB else 1) for name in
    [f"xT{t}{c}" for t in range(TT) for c in range(2)] + ["a", "z0", "z1"]
    + [f"{n}{j}" for n in "qk" for j in range(2)] + [f"v{c}{t}" for c in range(2) for t in range(TT)]
    + [f"r{j}" for j in range(4)] + ["ks0", "ks1", "att0", "att1"]
    + [f"upd{n}{j}" for n in range(NCH - 1) for j in range(2)] + [f"o{b}" for b in range(4)]
    + ["raw0", "raw1"] + [f"oT{b}" for b in range(4)] + [f"raw{i}" for i in range(2, 12)]
    + [f"vd{g}{t}" for g in range(GROUPS) for t in range(TT)]
    + [s for i in range(19) for s in
       ([f"S{i}"] if i < 16 else []) + ([f"gt{i // 2}"] if i < 16 and i % 2 else [])
       + (["yg0"] if i == 16 else [])
       + ([f"pt{i - 1}{j}" for j in range(UNITS[i - 1][0] + 1)] if 1 <= i <= 16 else [])
       + ([f"pv{i - 3}"] if i >= 3 else []) + (["yg1"] if i == 17 else [])]
    + ["yg2", "at0", "at1", "yg3"] + [f"ya{j}" for j in range(4)]
    + [f"mo{c}{t}" for c in range(2) for t in range(TT)]
    + [f"x1T{t}{c}" for t in range(TT) for c in range(2)] + ["logits", "rank"]])

ACT_PLAN = Plan(
    [(f"xT{t}{c}", 1) for t in range(TT) for c in range(2)]
    + [("aT", 1), ("z0", 2), ("z1", 2), ("soft", 3), ("decay", 3)]
    + [(f"v{c}{t}", 1) for c in range(2) for t in range(TT)] + [(f"r{j}", 1) for j in range(4)]
    + [("ksn0", 1), ("ksn1", 1)] + [(f"sq{b}", 2) for b in range(4)] + [("rms", 1), ("on0", 4), ("alpha_x", 1)]
    + [(f"raw{i}", 5) for i in range(4)] + [("o_hi", 1)] + [(f"raw{i}", 5) for i in range(4, 12)] + [(f"vd{g}{t}", 1) for g in range(GROUPS) for t in range(TT)]
    + [s for i in range(17) for s in
       ([(f"gt{i // 2}", 1)] if i % 2 else []) + ([(f"pt{i - 1}", UNITS[i - 1][0] + 1)] if i else [])
       + ([(f"ex{i}", 1)] if i < 16 else [])]
    + [("at0", 1), ("at1", 1)]
    + [(f"mix{j}", 1) for j in range(4)] + [("ln1", 1)] + [(f"x1T{t}{c}", 1) for t in range(TT) for c in range(2)]
    + [("router", 1), ("x_hi", 1), ("xacc", 1), ("ln2", 1)])

DVE_PLAN = Plan(
    [("wa", 2)] + [(f"xT{t}{c}", 1) for t in range(TT) for c in range(2)]
    + [("scan", 6), ("last", 1), ("qt0", 1), ("qt1", 1), ("kt0", 2), ("kt1", 2)]
    + [("attm0", 1), ("attm1", 1)] + [("upd00", 1), ("upd01", 1)]
    + [(f"upd{n}{j}", 2) for n in range(1, NCH - 1) for j in range(2)]
    + [("ms", 1), ("rms", 1), ("on1", 4), ("rope0", 3), ("rope1", 3)] + [(f"oT{b}", 2) for b in range(4)]
    + [("rope2", 3), ("rope3", 3), ("o_lo", 1)] + [(f"rope{i}", 3) for i in range(4, 12)]
    + [(f"vd{g}{t}", 1) for g in range(GROUPS) for t in range(TT)]
    + [s for i in range(18) for s in ([(f"pt{i - 2}", UNITS[i - 2][0] + 1)] if i >= 2 else [])
       + ([(f"sc{i}", 2)] if i < 16 else []) + ([("an0", 2)] if i == 10 else [])]
    + [("an1", 2), ("yg0", 1), ("yg1", 1), ("yg2", 1), ("at0", 1), ("at1", 1), ("yg3", 1)]
    + [("ya0", 2), ("ya1", 2), ("mix0", 1), ("ya2", 2), ("mix1", 1), ("ya3", 2)]
    + [("mix2", 1), ("mix3", 1)] + [(f"mo{c}{t}", 2) for c in range(2) for t in range(TT)]
    + [("ln1a", 3), ("ln1r", 1), ("ln1n0", 2), ("ln1n1", 2)] + [(f"x1T{t}{c}", 1) for t in range(TT) for c in range(2)]
    + [("logits", 3), ("gate", 19), ("x_lo", 1), ("rank", 2), ("passes", 4)]
    + [("ln2a", 3), ("ln2r", 1), ("ln2n0", 2), ("ln2n1", 2)])

PE_GATHER = Plan([(f"x{n}", 1) for n in range(4)] + [("gT", 1)])
ACT_GATHER = Plan([("x0", 1), ("x1", 1)])
DVE_GATHER = Plan([("S", 1), ("gated", 1), ("x2", 1), ("x3", 1)])
ACT_PAIR = Plan([("silu0", 1), ("hh0", 1), ("silu1", 1), ("yT0", 1), ("hh1", 1)])
DVE_PAIR = Plan([("h0", 1), ("hl0", 1), ("h1", 1), ("hl1", 1)])
PE_TAIL = Plan([("yT0", 1), ("yT1", 1)] + [(f"y{t}{c}", 1) for t in range(TT) for c in range(2)])
ACT_TAIL = Plan([("yT1", 1), ("yn0", 1), ("yn1", 1)])
DVE_TAIL = Plan([("G", 1)] + [(f"y{t}{c}", 1) for t in range(TT) for c in range(2)])
PRODUCTS = ((0, 0), (0, 1), (1, 0))
PAIR_ORDER = [("gate", 0), ("up", 0), ("gate", 1), ("down", 0), ("up", 1), ("down", 1)]


def build(nc, x, positions, w_in, w_alpha_up, b_alpha, gla_norm, w_gla_o, w_att_o, w_out, ln1_g, ln1_b,
          w_router, b_router, w_e_gate, w_e_up, w_e_down, ln2_g, ln2_b, constants, out):
    with ExitStack() as ctx:
        def sb(name, shape, dt=F32):
            return ctx.enter_context(nc.sbuf_tensor(name, shape, dt))

        def sem(name):
            return ctx.enter_context(nc.semaphore(name))

        ctx.enter_context(nc.allow_non_contiguous_dma("small strided parameter loads"))

        ring = sb("ring", [P, 2 * STAGES, CW])
        x_nat = sb("x_nat", [P, TT, DM])
        xacc = sb("xacc", [P, TT, DM])
        xT = sb("xT", [P, KT, 2, TOK], F16)
        area = sb("area", [P, 16384])
        cst = sb("cst", [P, CONST_W])
        lnp = sb("lnp", [P, 2, DM])
        cos = sb("cos", [P, TOK])
        sin = sb("sin", [P, TOK])
        w_a = sb("w_a", [P, KT, RANK])
        w_a16 = sb("w_a16", [P, 2, KT, RANK], F16)
        w_au = sb("w_au", [RANK, HEADS * DK])
        b_al = sb("b_al", [P, HEADS])
        gnorm = sb("gnorm", [P, 8])
        w_r16 = sb("w_r16", [P, 2, KT, E], F16)
        b_r = sb("b_r", [P, E])
        dec = sb("dec", [P, HEADS, NCH])
        G_pair = sb("G_pair", [P, TOK])
        rms = sb("rms", [P, TT * HEADS])
        stats = sb("stats", [P, TT, 2, 6])
        mv = sb("mv", [P, TT, 2])
        rstd = sb("rstd", [P, TT])
        top = sb("top", [P, 16])
        ntop = sb("ntop", [P, 16])
        psum_l = sb("psum_l", [P, 16])
        rl = sb("rl", [P, 16])
        e_t = sb("e_t", [P, TT, E])
        sel = sb("sel", [P, TT, E])
        comb = sb("comb", [P, TT, E])
        rk = sb("rk", [P, TT, E])
        pm = sb("pm", [P, TT, E])
        g_s = sb("g_s", [P, 8])
        g_r = sb("g_r", [P, 8])
        two = sb("two", [P, 4])
        lim = sb("lim", [1, 4])
        passes_sb = sb("passes_sb", [1, 1], I32)
        bank = ctx.enter_context(nc.psum_tensor("bank", [P, 8, 512], F32))

        def part(a, width, pattern=None, **kw):
            v = area[:, a:a + width]
            return v.rearrange(pattern, **kw) if pattern else v

        zb = part(0, 1024, "p (h t) -> p h t", h=HEADS)
        lb = part(1024, 1024, "p (h t) -> p h t", h=HEADS)
        q_t = part(2048, 1024, "p (h t) -> p h t", h=HEADS)
        k_t = part(3072, 1024, "p (h t) -> p h t", h=HEADS)
        v_g = part(4096, 2048, "p (t c) -> p t c", t=TT)
        ks_n = part(6144, 1024, "p (t h d) -> p t h d", t=TT, h=HEADS)
        attm = part(7168, 1024, "p (t h i) -> p t h i", t=TT, h=HEADS)
        state = part(8192, 3072, "p (n h v) -> p n h v", n=3, h=HEADS)
        oT = part(11264, 2048, "p (m t) -> p m t", m=8)
        o_n = part(14336, 2048, "p (t c) -> p t c", t=TT)
        o16 = part(14336, 2048).bitcast(F16).rearrange("p (k i t) -> p k i t", k=8, i=2)
        aT = area[0:RANK, 11264:11264 + TOK]
        w_r = part(512, KT * E, "p (k e) -> p k e", k=KT)
        qk = part(0, 6144, "p (c t) -> p c t", c=24)
        v_d = part(6144, 3072).bitcast(F16).rearrange("p (t i c) -> p t i c", t=TT, i=2)
        raw = part(9216, 1024, "p (b c t) -> p b c t", b=2, c=2)
        turned = part(13312, 1024, "p (b c t) -> p b c t", b=2, c=2)
        rtmp = part(10240, 512, "p (c t) -> p c t", c=2)
        prob = part(9216, 1536, "p (b c) -> p b c", b=2)
        probT = part(10752, 1536).bitcast(F16).rearrange("p (b c i q) -> p b c i q", b=2, c=6, i=2)
        att_n = part(12288, 1024, "p (t c) -> p t c", t=TT)
        mixT = part(4096, 2048, "p (c t) -> p c t", c=8)
        mtmp = part(6144, 512, "p (c t) -> p c t", c=2)
        att16 = part(9216, 1024).bitcast(F16).rearrange("p (k i t) -> p k i t", k=4, i=2)
        mix16 = part(10240, 2048).bitcast(F16).rearrange("p (k i t) -> p k i t", k=8, i=2)
        gates = [xacc[:, :, :].rearrange("p t d -> p (t d)").rearrange("p (c t) -> p c t", c=8),
                 lnp[:, :, :].rearrange("p i d -> p (i d)").rearrange("p (c t) -> p c t", c=8)]
        cmp_a, cmp_b = part(12288, 128), part(12416, 128)
        x_pair = part(9216, 1024).bitcast(F16).rearrange("p (k i s) -> p k i s", k=KT, i=2)
        S_pair = part(10240, TT * SLOTS).bitcast(F16).rearrange("p (t e s) -> p t e s", t=TT, e=2)
        S_gated = part(10496, TT * 2 * SLOTS, "p (t e s) -> p t e s", t=TT, e=2)
        hid = part(12288, 1024, "p (j c) -> p j c", j=2)
        h16 = part(13312, 1024).bitcast(F16).rearrange("p (j i c) -> p j i c", j=2, i=2)
        yT = part(14336, 1024, "p (m j s) -> p m j s", m=8, j=2)
        yn = part(15360, 1024)

        def gate_tiles(j):
            return gates[j // 4][:, 2 * (j % 4):2 * (j % 4) + 2, :]

        def const(name, rows=P):
            a, b = CONST[name]
            return cst[0:rows, a:b]

        ident, ones = const("ident"), const("ones")
        x16 = xT[:, :, :, :].rearrange("p k i t -> p (k i t)").rearrange("p (i t d) -> p i t d", i=2, t=TT)

        extra = [part(0, CW), part(4096, CW)]

        def staged(c, width=512, depth=STAGES):
            slot = ring[:, c % depth, :] if c % depth < STAGES else extra[0]
            return slot.rearrange("p (k c) -> p k c", c=width)

        def parts(c, width=512, depth=STAGES):
            slot = ring[:, STAGES + c % depth, :] if c % depth < STAGES else extra[1]
            return slot.bitcast(F16).rearrange("p (i k c) -> p i k c", i=2, c=width)

        def halves(b):
            return bank[:, b, :].rearrange("p (c t) -> p c t", c=2)

        tables_landed = sem("tables_landed")
        setup_landed = sem("setup_landed")
        small_landed = sem("small_landed")
        small_ready = sem("small_ready")
        ln1_landed = sem("ln1_landed")
        ln2_landed = sem("ln2_landed")
        landed = [sem(f"chunk_landed{s}") for s in range(DEEP)]
        hi_done = sem("hi_done")
        split_done = sem("split_done")
        chunk_done = sem("chunk_done")
        x_ready = sem("x_ready")
        stats_taken = sem("stats_taken")
        zeroed = sem("zeroed")
        rope_done = sem("rope_tables")
        rope_act = sem("rope_tables_act")
        pe_done, act_done, dve_done = sem("pe_done"), sem("act_done"), sem("dve_done")
        pe_gather, act_gather, dve_gather = sem("pe_gather"), sem("act_gather"), sem("dve_gather")
        pass_over = sem("pass_over")
        act_pair, dve_pair = sem("act_pair"), sem("dve_pair")
        pe_tail, act_tail, dve_tail = sem("pe_tail"), sem("act_tail"), sem("dve_tail")
        w_r_split = sem("w_r_split")
        scaled = sem("scaled")
        out_done = sem("out_done")
        apart_sem = sem("apart")

        block = ctx.enter_context(nc.Block())

        def apart(eng):
            eng.sem_inc(apart_sem, 1)

        def count_passes(eng, layer, passes_reg):
            eng.wait_ge(dve_done, DVE_PLAN.of(layer)("passes"))
            apart(eng)
            n = eng.value_load(passes_sb[0:1, 0:1], min_val=1, max_val=TOK // SLOTS)
            eng.reg_add(passes_reg, passes_reg, n)
            return n

        def pass_loop(eng, layer, body, passes_reg):
            before = eng.snap(passes_reg)
            n = count_passes(eng, layer, passes_reg)
            with eng.Fori(0, n) as p:
                body(before + p, lambda: eng.If(p + 1 < n))

        def stream_place(layer, passes):
            return layer * FRONT_CHUNKS + passes * (PAIRS * PAIR_CHUNKS)

        def pe_steps(layer, before):
            count = PE_PLAN.of(layer)
            return lambda name: ((chunk_done, before + (LAST_JOB[name] + 1 + STAGES)) if name in LAST_JOB
                                 else (pe_done, count(name)))

        def expert_loads(layer, r, c):
            loads = (r * (PAIR_CHUNKS // DEEP) + (c // DEEP + 1)) * 16
            return loads + (layer + 1) * (FRONT_CHUNKS // STAGES * 16) if c % DEEP < STAGES else loads

        def low(dve, before, c, depth=STAGES):
            dve.wait_ge(hi_done, before + (c + 1))
            w = parts(c, depth=depth)
            nc.vector.scalar_tensor_tensor(out=w[:, 1, :, :], in0=staged(c, depth=depth), scalar=W_SCALE,
                                           in1=w[:, 0, :, :], op0=ALU.mult, op1=ALU.subtract).then_inc(split_done, 1)

        w_in_v = w_in.rearrange("l (k p) c -> p l k c", p=P)
        gla_o_v = w_gla_o.rearrange("l (k p) c -> p l k c", p=P)
        att_o_v = w_att_o.rearrange("l (k p) c -> p l k c", p=P)
        out_v = w_out.rearrange("l (k p) c -> p l k c", p=P)
        expert_v = {"gate": w_e_gate.rearrange("l e (k p) c -> p (l e) k c", p=P),
                    "up": w_e_up.rearrange("l e (k p) c -> p (l e) k c", p=P),
                    "down": w_e_down.rearrange("l e (k p) c -> p (l e) k c", p=P)}
        starts = [c * 512 for c in range(A_COL // 512)] + [D_COL + c * 512 for c in range(13)]
        front = [(w_in_v, s, 512) for s in starts] + [(gla_o_v, 0, 512), (gla_o_v, 512, 512), (att_o_v, 0, 1024),
                                                      (out_v, 0, 512), (out_v, 512, 512)]
        assert len(front) == FRONT_CHUNKS

        def small_params(layer):
            return [(w_a[:, :, :], w_in_v[:, bass.ds(layer, 1), :, A_COL:A_COL + RANK]
                     .rearrange("p o k c -> p (o k) c")),
                    (w_au[:, :], w_alpha_up[bass.ds(layer, 1), :, :].rearrange("o r c -> (o r) c")),
                    (b_al[:, :], b_alpha[bass.ds(layer, 1), :].rearrange("o (h p) -> p (o h)", p=P)),
                    (gnorm[:, :], gla_norm[bass.ds(layer, 1), :].rearrange("o (h p) -> p (o h)", p=P))]

        SETUP_LOADS = 2 + len(small_params(0))

        @block.sync
        def _(sp):
            passes_reg = sp.alloc_register("sp_passes")
            sp.reg_mov(passes_reg, 0)
            sp.dma_start(cst[:, :], constants).then_inc(tables_landed, 16)
            sp.dma_start(cos[:, :].bitcast(I32), positions[0:1, :].partition_broadcast(P)
                         .rearrange("a o e -> a (o e)")).then_inc(tables_landed, 16)
            sp.dma_start(w_r, w_router.rearrange("(k p) e -> p k e", p=P)).then_inc(tables_landed, 16)
            sp.dma_start(x_nat[:, :, :], x[0, :, :].rearrange("(t p) d -> p t d", p=P)).then_inc(setup_landed, 16)
            for dst, src in small_params(0):
                sp.dma_start(dst, src).then_inc(setup_landed, 16)
            sp.dma_start(b_r[:, :], b_router.rearrange("(o e) -> o e", o=1).partition_broadcast(P)
                         .rearrange("a o e -> a (o e)")).then_inc(setup_landed, 16)
            with sp.Fori(0, DEPTH) as layer:
                before = sp.snap(stream_place(layer, sp.snap(passes_reg)))
                for c, (w, col, width) in enumerate(front):
                    sp.wait_ge(split_done, before + (c + 1))
                    src = w[:, bass.ds(layer, 1), :, col:col + width].rearrange("p o k c -> p (o k) c")
                    sp.dma_start(staged(c, width), src).then_inc(landed[c % STAGES], 16)

                def expert_chunk(before, pair, c, first=False):
                    kind, j = PAIR_ORDER[c % PAIR_CHUNKS // 2]
                    expert = sp.snap(layer * E + pair * 2 + j)
                    if first and c == STAGES:
                        sp.wait_ge(dve_done, DVE_PLAN.of(layer)("an1"))
                    else:
                        sp.wait_ge(split_done, before + (c + STAGES - (STAGES if first else DEEP) + 1))
                    apart(sp)
                    src = expert_v[kind][:, bass.ds(expert, 1), :,
                                         (c % 2) * 512:(c % 2) * 512 + 512].rearrange("p o k c -> p (o k) c")
                    sp.dma_start(staged(c, depth=DEEP), src).then_inc(landed[c % DEEP], 16)

                for c in (STAGES, 0, 1, 2, 4, 5):
                    expert_chunk(before + FRONT_CHUNKS, 0, c, first=c < DEEP)
                ahead = 6

                def experts(q, more):
                    with sp.Fori(0, PAIRS - 1) as pair:
                        before = sp.snap((layer + 1) * FRONT_CHUNKS + (q * PAIRS + pair) * PAIR_CHUNKS)
                        for c in range(ahead, PAIR_CHUNKS):
                            expert_chunk(before, pair, c)
                        for c in range(PAIR_CHUNKS, PAIR_CHUNKS + ahead):
                            expert_chunk(before, pair + 1, c)
                    before = sp.snap((layer + 1) * FRONT_CHUNKS + (q * PAIRS + (PAIRS - 1)) * PAIR_CHUNKS)
                    for c in range(ahead, PAIR_CHUNKS):
                        expert_chunk(before, PAIRS - 1, c)
                    with more():
                        for c in range(PAIR_CHUNKS, PAIR_CHUNKS + ahead):
                            expert_chunk(before, 0, c)

                pass_loop(sp, layer, experts, passes_reg)
            for t in range(TT):
                sp.wait_ge(dve_done, DVE_PLAN.of(DEPTH - 1)(f"ln2n{t}"))
                sp.dma_start(out[0, t * P:(t + 1) * P, :], x_nat[:, t, :]).then_inc(out_done, 16)
            sp.wait_ge(out_done, TT * 16)

        @block.gpsimd
        def _(pool):
            passes_reg = pool.alloc_register("pool_passes")
            pool.reg_mov(passes_reg, 0)
            pool.wait_ge(setup_landed, SETUP_LOADS * 16)
            pool.sem_inc(small_ready, 1)

            def norm_params(layer, gain, bias, signal):
                for i, w in enumerate((gain, bias)):
                    pool.dma_start(lnp[:, i, :], w[bass.ds(layer, 1), :].partition_broadcast(P)
                                   .rearrange("a o e -> a (o e)")).then_inc(signal, 16)

            def parameters(layer, more):
                pool.wait_ge(x_ready, (layer + 1) * TT)
                apart(pool)
                nc.gpsimd.memset(attm, 0.0).then_inc(zeroed, 1)
                if more:
                    pool.wait_ge(dve_done, DVE_PLAN.of(layer)("oT3"))
                    apart(pool)
                    for dst, src in small_params(layer + 1):
                        pool.dma_start(dst, src).then_inc(small_landed, 16)
                    pool.wait_ge(small_landed, (layer + 1) * (16 * len(small_params(0))))
                    pool.sem_inc(small_ready, 1)
                pool.wait_ge(dve_done, DVE_PLAN.of(layer)("ya3"))
                apart(pool)
                norm_params(layer, ln1_g, ln1_b, ln1_landed)
                passes = pool.snap(passes_reg)
                w, w16 = staged(2, depth=DEEP), parts(2, depth=DEEP)
                pool.wait_ge(landed[2], expert_loads(layer, pool.snap(passes * PAIRS), 2))
                apart(pool)
                nc.gpsimd.tensor_scalar(w, w, W_SCALE, None, ALU.mult).then_inc(scaled, 1)
                pool.wait_ge(hi_done, (layer + 1) * FRONT_CHUNKS + passes * (PAIRS * PAIR_CHUNKS) + 3)
                apart(pool)
                nc.gpsimd.tensor_tensor(w16[:, 1, :, :], w, w16[:, 0, :, :], ALU.subtract).then_inc(split_done, 1)
                pool.wait_ge(dve_done, DVE_PLAN.of(layer)("ln1n1"))
                apart(pool)
                norm_params(layer, ln2_g, ln2_b, ln2_landed)
                if more:
                    count_passes(pool, layer, passes_reg)

            with pool.Fori(0, DEPTH - 1) as layer:
                parameters(layer, True)
            parameters(DEPTH - 1, False)

        @block.tensor
        def _(pe):
            passes_reg = pe.alloc_register("pe_passes")
            pe.reg_mov(passes_reg, 0)
            pe.sem_inc(split_done, STAGES)
            pe.sem_inc(chunk_done, STAGES)
            pe.wait_ge(tables_landed, 48)

            def transposes(b, sources):
                for i, s in enumerate(sources):
                    mm = pe.transpose(bank[:, b, i * P:(i + 1) * P], s, ident)
                return mm

            with pe.Fori(0, DEPTH) as layer:
                before = pe.snap(stream_place(layer, pe.snap(passes_reg)))
                count, A, D = PE_PLAN.of(layer), ACT_PLAN.of(layer), DVE_PLAN.of(layer)

                def ended(name, mm):
                    mm.then_inc(chunk_done if name in LAST_JOB else pe_done, 1)

                def arrived(c):
                    pe.wait_ge(split_done, before + (c + 1 + STAGES))

                def bank_free(name):
                    user = BEFORE[name]
                    if user.startswith(("vd", "at")):
                        pe.wait_ge(dve_done, D(user))
                    elif user.startswith("pt"):
                        pe.wait_ge(dve_done, D(user[:-1], int(user[-1]) + 1))
                    else:
                        pe.wait_ge(act_done, A({"a": "aT", "ks0": "ksn0", "ks1": "ksn1"}.get(user, user)))

                def features(b, half, w, col, rhs, kt=KT):
                    for k in range(kt):
                        for n, (wi, xi) in enumerate(PRODUCTS):
                            mm = pe.matmul(bank[:, b, half * TOK:(half + 1) * TOK], w[:, wi, k, col:col + P],
                                           rhs[:, k, xi, :], start=(k == 0 and n == 0),
                                           stop=(k == kt - 1 and n == 2))
                    return mm

                def two_tiles(b, w, j, rhs, kt=KT):
                    features(b, 0, w, 2 * j * P, rhs, kt)
                    return features(b, 1, w, (2 * j + 1) * P, rhs, kt)

                def tokens(b, t, w, lhs, ready=None):
                    for k in range(KT):
                        if ready and k % 2 == 0:
                            pe.wait_ge(dve_done, D(ready[k // 2]))
                        for n, (wi, xi) in enumerate(PRODUCTS):
                            mm = pe.matmul(bank[:, b, :], lhs[:, k, xi, t * P:(t + 1) * P], w[:, wi, k, :],
                                           start=(k == 0 and n == 0), stop=(k == KT - 1 and n == 2))
                    return mm

                def x_transposed(step):
                    for t in range(TT):
                        if step == "x1T":
                            pe.wait_ge(dve_done, D(f"ln1n{t}"))
                        else:
                            pe.wait_ge(x_ready, layer * TT + (t + 1))
                        for c in range(2):
                            ended(f"{step}{t}{c}", transposes(4 * c + t, [x_nat[:, t, k * P:(k + 1) * P]
                                                                          for k in range(4 * c, 4 * c + 4)]))
                    pe.wait_ge(dve_done, D(f"{step}11"))

                x_transposed("xT")
                pe.wait_ge(dve_done, D("wa"))
                for k in range(KT):
                    for n, (wi, xi) in enumerate(PRODUCTS):
                        mm = pe.matmul(bank[0:RANK, 2, 0:TOK], w_a16[:, wi, k, :], xT[:, k, xi, :],
                                       start=(k == 0 and n == 0), stop=(k == KT - 1 and n == 2))
                ended("a", mm)
                pe.wait_ge(act_done, A("aT"))
                for j in range(2):
                    for i in range(2):
                        h = 2 * j + i
                        mm = pe.matmul(bank[:, j, i * TOK:(i + 1) * TOK], w_au[:, h * DK:(h + 1) * DK], aT,
                                       start=True, stop=True)
                    ended(f"z{j}", mm)
                for c in range(2):
                    arrived(c)
                    for j in range(2):
                        ended(f"{'qk'[c]}{j}", two_tiles(4 + 2 * c + j, parts(c), j, xT))
                for c in range(2, 4):
                    arrived(c)
                    for t in range(TT):
                        name = f"v{c - 2}{t}"
                        bank_free(name)
                        ended(name, tokens(BANK[name], t, parts(c), xT))
                for c in range(4, 6):
                    arrived(c)
                    for j in range(2):
                        name = f"r{2 * (c - 4) + j}"
                        bank_free(name)
                        ended(name, two_tiles(BANK[name], parts(c), j, xT))
                pe.wait_ge(dve_done, D("kt1"))
                for t in range(TT):
                    name = f"ks{t}"
                    bank_free(name)
                    ended(name, transposes(BANK[name], [zb[:, h, t * P:(t + 1) * P] for h in range(HEADS)]))
                for t in range(TT):
                    for h in range(HEADS):
                        mm = pe.matmul(bank[:, 4 + t, h * P:(h + 1) * P], k_t[:, h, t * P:(t + 1) * P],
                                       q_t[:, h, t * P:(t + 1) * P], start=True, stop=True)
                    ended(f"att{t}", mm)
                pe.wait_ge(act_done, A("ksn1"))
                for c in range(NCH - 1):
                    t, rows = c // 2, slice((c % 2) * CHUNK, (c % 2 + 1) * CHUNK)
                    for j in range(2):
                        if c:
                            pe.wait_ge(dve_done, D(f"upd{c - 1}{j}"))
                        for i in range(2):
                            h = 2 * j + i
                            mm = pe.matmul(bank[:, 6 + j, i * DV:(i + 1) * DV], ks_n[rows, t, h, :],
                                           v_g[rows, t, h * DV:(h + 1) * DV], start=True, stop=True)
                        ended(f"upd{c}{j}", mm)
                pe.wait_ge(dve_done, D("upd21"))
                for b in range(4):
                    t = b // 2
                    for i in range(2):
                        h, cols = 2 * (b % 2) + i, slice(i * DV, (i + 1) * DV)
                        values = v_g[:, t, h * DV:(h + 1) * DV]
                        if t == 0:
                            for first in range(2):
                                rows = slice(first * CHUNK, (first + 1) * CHUNK)
                                pe.matmul(bank[rows, 4 + b, cols], attm[:, t, h, rows], values,
                                          start=True, stop=(first == 0))
                        else:
                            pe.matmul(bank[:, 4 + b, cols], attm[:, t, h, :], values, start=True, stop=False)
                        for c in range(max(2 * t, 1), 2 * t + 2):
                            rows = slice((c % 2) * CHUNK, (c % 2 + 1) * CHUNK)
                            mm = pe.matmul(bank[rows, 4 + b, cols], q_t[:, h, c * CHUNK:(c + 1) * CHUNK],
                                           state[:, c - 1, h, :], start=False, stop=True)
                    ended(f"o{b}", mm)

                for i in range(12):
                    if i % 2 == 0:
                        arrived(6 + i // 2)
                    if i >= 2:
                        pe.wait_ge(act_done, A(f"raw{i - 2}"))
                    ended(f"raw{i}", two_tiles(i % 2, parts(6 + i // 2), i % 2, xT))
                    if i == 1:
                        pe.wait_ge(act_done, A("on0"))
                        pe.wait_ge(dve_done, D("on1"))
                        for b in range(4):
                            ended(f"oT{b}", transposes(4 + b, [o_n[:, t, (2 * b + m) * P:(2 * b + m + 1) * P]
                                                               for m in range(2) for t in range(TT)]))
                for g in range(GROUPS):
                    arrived(12 + g)
                    for t in range(TT):
                        name = f"vd{g}{t}"
                        bank_free(name)
                        ended(name, tokens(BANK[name], t, parts(12 + g), xT))
                def y_gla(j):
                    if j % 2 == 0:
                        arrived(19 + j // 2)
                    ended(f"yg{j}", two_tiles(4 + j, parts(19 + j // 2), j % 2, o16))

                pe.wait_ge(dve_done, D("rope11"))
                for i in range(19):
                    if i == 16:
                        pe.wait_ge(dve_done, D("o_lo"))
                        y_gla(0)
                    if i < 16:
                        qt, h = UNITS[i]
                        if i >= 2:
                            pe.wait_ge(dve_done, D(f"sc{i - 2}"))
                        for g in range(GROUPS):
                            hh = g * AH + h
                            rows = slice((hh % 2) * HD, (hh % 2 + 1) * HD)
                            nk = (qt + 1) * P
                            b = 4 + 2 * (i % 2) + g // 2
                            mm = pe.matmul(bank[:, b, (g % 2) * TOK:(g % 2) * TOK + nk],
                                           qk[rows, hh // 2, qt * P:(qt + 1) * P], qk[rows, 12 + hh // 2, 0:nk],
                                           start=True, stop=True)
                        ended(f"S{i}", mm)
                        c, name = 15 + i // 4, f"gt{i // 2}"
                        if i % 4 == 0:
                            arrived(c)
                        if i % 2 == 0:
                            bank_free(name)
                        mm = features(BANK[name], i % 2, parts(c), (i % 4) * P, xT)
                        if i % 2 == 1:
                            ended(name, mm)
                    if 1 <= i <= 16:
                        u = i - 1
                        pe.wait_ge(act_done, A(f"ex{u}"))
                        for j in range(UNITS[u][0] + 1):
                            name = f"pt{u}{j}"
                            bank_free(name)
                            ended(name, transposes(BANK[name], [prob[:, u % 2, (3 * j + s) * P:(3 * j + s + 1) * P]
                                                                for s in range(3)]))
                    if i >= 3:
                        u = i - 3
                        qt, h = UNITS[u]
                        pe.wait_ge(dve_done, D(f"pt{u}"))
                        if u == 8:
                            pe.wait_ge(dve_done, D("an0"))
                        tiles = [(g, kt) for g in range(GROUPS) for kt in range(qt + 1)]
                        for s, (g, kt) in enumerate(tiles):
                            for n, (vi, pi) in enumerate(PRODUCTS):
                                mm = pe.matmul(bank[:, 3, h * HD:(h + 1) * HD], probT[:, u % 2, s, pi, :],
                                               v_d[:, kt, vi, g * 512 + h * HD:g * 512 + (h + 1) * HD],
                                               start=(s == 0 and n == 0), stop=(s == len(tiles) - 1 and n == 2))
                        ended(f"pv{u}", mm)
                    if i == 17:
                        y_gla(1)
                y_gla(2)
                for qt in range(TT):
                    pe.wait_ge(dve_done, D(f"an{qt}"))
                    name = f"at{qt}"
                    bank_free(name)
                    ended(name, transposes(BANK[name], [att_n[:, qt, k * P:(k + 1) * P] for k in range(4)]))
                y_gla(3)
                arrived(21)
                pe.wait_ge(dve_done, D("at1"))
                for j in range(4):
                    pe.wait_ge(dve_done, D(f"yg{j}"))
                    ended(f"ya{j}", two_tiles(4 + j, parts(21, 1024), j, att16, 4))
                merged = [f"mix{j}" for j in range(4)]
                for c in range(2):
                    arrived(22 + c)
                    for t in range(TT):
                        ended(f"mo{c}{t}", tokens(4 + 2 * c + t, t, parts(22 + c), mix16, merged))
                pe.wait_ge(act_done, A("gt7"))
                x_transposed("x1T")
                for t in range(TT):
                    for k in range(KT):
                        for n, (wi, xi) in enumerate(PRODUCTS):
                            mm = pe.matmul(bank[:, 6, t * E:(t + 1) * E], xT[:, k, xi, t * P:(t + 1) * P],
                                           w_r16[:, wi, k, :], start=(k == 0 and n == 0), stop=(k == KT - 1 and n == 2))
                ended("logits", mm)
                pe.wait_ge(dve_done, D("gate", 15))
                pe.matmul(bank[:, 7, 0:E], const("before"), sel[:, 0, :], start=True, stop=True)
                pe.matmul(bank[:, 7, E:2 * E], ones, sel[:, 0, :], start=True, stop=False)
                pe.matmul(bank[:, 7, E:2 * E], const("before"), sel[:, 1, :], start=False, stop=True)
                pe.matmul(bank[:, 7, 2 * E:3 * E], ones, sel[:, 0, :], start=True, stop=False)
                mm = pe.matmul(bank[:, 7, 2 * E:3 * E], ones, sel[:, 1, :], start=False, stop=True)
                ended("rank", mm)

                def experts(q, more):
                    def gather(r):
                        pe.wait_ge(dve_gather, DVE_GATHER.of(r)("S"))
                        for n in range(4):
                            for i in range(4):
                                k, xi = (4 * n + i) // 2, i % 2
                                for t in range(TT):
                                    mm = pe.matmul(bank[:, n, i * P:(i + 1) * P], x16[:, xi, t, k * P:(k + 1) * P],
                                                   S_pair[:, t, :, :].rearrange("p e s -> p (e s)"),
                                                   start=(t == 0), stop=(t == TT - 1))
                            mm.then_inc(pe_gather, 1)

                    def y_to_slots(r):
                        pe.wait_ge(act_tail, ACT_TAIL.of(r)("yT1"))
                        for c in range(2):
                            transposes([7, 0][c], [yT[:, m, :, :].rearrange("p j s -> p (j s)")
                                                   for m in range(4 * c, 4 * c + 4)]).then_inc(pe_tail, 1)

                    def scatter(r):
                        pe.wait_ge(act_tail, ACT_TAIL.of(r)("yn1"))
                        pe.wait_ge(dve_tail, DVE_TAIL.of(r)("G"))
                        for t in range(TT):
                            for c in range(2):
                                pe.matmul(bank[:, [1, 2, 3, 7][2 * t + c], :], G_pair[:, t * P:(t + 1) * P],
                                          yn[:, c * 512:(c + 1) * 512], start=True, stop=True).then_inc(pe_tail, 1)

                    def pair_steps(pair, first=False, last=False):
                        r = q * PAIRS + pair
                        before = pe.snap((layer + 1) * FRONT_CHUNKS + r * PAIR_CHUNKS)
                        AR, DR = ACT_PAIR.of(r), DVE_PAIR.of(r)
                        pe.wait_ge(act_gather, ACT_GATHER.of(r)("x1"))
                        pe.wait_ge(dve_gather, DVE_GATHER.of(r)("x3"))
                        for c in range(PAIR_CHUNKS):
                            kind, j = PAIR_ORDER[c // 2]
                            b = {"gate": 4, "up": 5, "down": 6}[kind]
                            if c % 2 == 0:
                                if kind == "gate" and j == 1:
                                    pe.wait_ge(act_pair, AR("silu0"))
                                if kind == "down":
                                    pe.wait_ge(dve_pair, DR(f"hl{j}"))
                                    if j == 1:
                                        pe.wait_ge(act_pair, AR("yT0"))
                                if kind == "up" and j == 1:
                                    pe.wait_ge(dve_pair, DR("h0"))
                            pe.wait_ge(split_done, before + (c + 1 + STAGES))
                            w = parts(c, depth=DEEP)
                            for m in range(4):
                                mo = (c % 2) * 4 + m
                                for k in range(KT):
                                    for n, (wi, xi) in enumerate(PRODUCTS):
                                        if kind == "down":
                                            rhs = h16[:, j, xi, k * SLOTS:(k + 1) * SLOTS]
                                        else:
                                            rhs = x_pair[:, k, xi, j * SLOTS:(j + 1) * SLOTS]
                                        mm = pe.matmul(bank[:, b, mo * SLOTS:(mo + 1) * SLOTS],
                                                       w[:, wi, k, m * P:(m + 1) * P], rhs,
                                                       start=(k == 0 and n == 0), stop=(k == KT - 1 and n == 2))
                            mm.then_inc(chunk_done, 1)
                            if c == 1 and not first:
                                y_to_slots(r - 1)
                            if c == 2:
                                if not first:
                                    scatter(r - 1)
                                pe.wait_ge(dve_gather, DVE_GATHER.of(r)("gated"))
                                transposes(0, [S_gated[:, t, :, :].rearrange("p e s -> p (e s)") for t in range(TT)])\
                                    .then_inc(pe_gather, 1)
                            if c == 9 and not last:
                                gather(r + 1)

                    gather(q * PAIRS)
                    pair_steps(0, first=True)
                    with pe.Fori(1, PAIRS - 1) as pair:
                        pair_steps(pair)
                    pair_steps(PAIRS - 1, last=True)
                    y_to_slots(q * PAIRS + (PAIRS - 1))
                    scatter(q * PAIRS + (PAIRS - 1))

                pass_loop(pe, layer, experts, passes_reg)

        @block.scalar
        def _(act):
            passes_reg = act.alloc_register("act_passes")
            act.reg_mov(passes_reg, 0)
            turns_left, scratch = xacc[:, 0, 0:TOK], xacc[:, 0, TOK:2 * TOK]
            act.wait_ge(rope_done, 8)
            act.activation(sin[:, :], turns_left, ACT.Sin, scale=const("sign")).then_inc(rope_act, 1)
            act.activation(scratch, turns_left, ACT.Abs).then_inc(rope_act, 1)
            act.wait_ge(rope_act, 2)
            act.activation(cos[:, :], scratch, ACT.Sin, bias=const("half_pi"), scale=-1.0).then_inc(rope_act, 1)

            with act.Fori(0, DEPTH) as layer:
                passes = act.snap(passes_reg)
                before = act.snap(stream_place(layer, passes))
                front_loads = act.snap(layer * (FRONT_CHUNKS // STAGES * 16)
                                       + passes * (PAIRS * PAIR_CHUNKS // DEEP * 16))
                Pn, A, D = pe_steps(layer, before), ACT_PLAN.of(layer), DVE_PLAN.of(layer)

                def high(c):
                    act.wait_ge(landed[c % STAGES], front_loads + (c // STAGES + 1) * 16)
                    act.wait_ge(chunk_done, before + (c + 1))
                    act.activation(parts(c)[:, 0, :, :], staged(c), ACT.Copy, scale=W_SCALE).then_inc(hi_done, 1)

                def expert_high(r, c, first=False):
                    if first and c == 2:
                        act.wait_ge(scaled, layer + 1)
                    else:
                        act.wait_ge(landed[c % DEEP], expert_loads(layer, r, c))
                    done = (layer + 1) * FRONT_CHUNKS + r * PAIR_CHUNKS + (c + 1)
                    act.wait_ge(chunk_done, done if first else done - (DEEP - STAGES))
                    act.activation(parts(c, depth=DEEP)[:, 0, :, :], staged(c, depth=DEEP), ACT.Copy,
                                   scale=1.0 if first and c == 2 else W_SCALE).then_inc(hi_done, 1)

                def quads(b):
                    return bank[:, b, :].rearrange("p (k t) -> p k t", k=4)

                def x_high(step):
                    for t in range(TT):
                        for c in range(2):
                            act.wait_ge(*Pn(f"{step}{t}{c}"))
                            act.activation(xT[:, 4 * c:4 * c + 4, 0, t * P:(t + 1) * P], quads(4 * c + t), ACT.Copy,
                                           scale=X_SCALE).then_inc(act_done, 1)

                x_high("xT")
                high(0)
                act.wait_ge(*Pn("a"))
                act.activation(aT, bank[0:RANK, 2, 0:TOK], ACT.Copy, scale=UNSCALE).then_inc(act_done, 1)
                high(1)
                for h in range(HEADS):
                    act.wait_ge(*Pn(f"z{h // 2}"))
                    act.activation(zb[:, h, :], bank[:, h // 2, (h % 2) * TOK:(h % 2 + 1) * TOK], ACT.Identity,
                                   bias=b_al[:, h:h + 1]).then_inc(act_done, 1)
                act.wait_ge(act_done, A("z1"))
                act.activation(lb, zb, ACT.Abs).then_inc(act_done, 1)
                act.wait_ge(act_done, A("soft", 1))
                act.activation(lb, lb, ACT.Exp, scale=-1.0).then_inc(act_done, 1)
                act.wait_ge(act_done, A("soft", 2))
                act.activation(lb, lb, ACT.Ln, bias=ones[:, 0:1]).then_inc(act_done, 1)
                high(2)
                act.wait_ge(dve_done, D("scan"))
                act.activation(q_t, lb, ACT.Exp, scale=1.0 / TAU).then_inc(act_done, 1)
                act.activation(k_t, lb, ACT.Exp, scale=-1.0 / TAU).then_inc(act_done, 1)
                act.activation(zb, zb, ACT.Exp, scale=1.0 / TAU).then_inc(act_done, 1)
                high(3)
                high(4)
                for c in range(2):
                    for t in range(TT):
                        name = f"v{c}{t}"
                        act.wait_ge(*Pn(name))
                        act.activation(v_g[:, t, c * 512:(c + 1) * 512], bank[:, BANK[name], :], ACT.Copy,
                                       scale=UNSCALE).then_inc(act_done, 1)
                    high(5 + c)
                for j in range(4):
                    act.wait_ge(*Pn(f"r{j}"))
                    act.activation(oT[:, 2 * j:2 * j + 2, :], halves(BANK[f"r{j}"]), ACT.Silu, scale=UNSCALE)\
                        .then_inc(act_done, 1)
                    if j == 1:
                        high(7)
                for t in range(TT):
                    act.wait_ge(*Pn(f"ks{t}"))
                    act.activation(ks_n[:, t, :, :], quads(BANK[f"ks{t}"]), ACT.Copy).then_inc(act_done, 1)
                high(8)
                for b in range(4):
                    act.wait_ge(*Pn(f"o{b}"))
                    for i in range(2):
                        act.activation(o_n[:, b // 2, (2 * (b % 2) + i) * DV:(2 * (b % 2) + i + 1) * DV], bank[:, 4 + b, i * DV:(i + 1) * DV], ACT.Square,
                                       accum_out=rms[:, 2 * b + i:2 * b + i + 1]).then_inc(act_done, 1)
                act.wait_ge(dve_done, D("ms"))
                act.activation(rms[:, :], rms[:, :], ACT.Sqrt).then_inc(act_done, 1)
                act.wait_ge(dve_done, D("rms"))
                for h in range(HEADS):
                    act.activation(o_n[:, 0, h * DV:(h + 1) * DV], bank[:, 4 + h // 2, (h % 2) * DV:(h % 2 + 1) * DV],
                                   ACT.Copy, scale=rms[:, h:h + 1]).then_inc(act_done, 1)
                act.activation(x_nat[:, :, :], x_nat[:, :, :], ACT.Copy, scale=ALPHA).then_inc(act_done, 1)
                for i in range(12):
                    act.wait_ge(*Pn(f"raw{i}"))
                    if i >= 2:
                        act.wait_ge(dve_done, D(f"rope{i - 2}"))
                    act.activation(raw[:, i % 2, :, :], halves(i % 2), ACT.Copy, scale=UNSCALE).then_inc(act_done, 1)
                    for to, of in ((0, 1), (1, 0), (2, 3), (3, 2)):
                        act.activation(turned[to * 32:(to + 1) * 32, i % 2, :, :],
                                       halves(i % 2)[of * 32:(of + 1) * 32], ACT.Copy, scale=UNSCALE).then_inc(act_done, 1)
                    if i % 2 == 1:
                        high(9 + i // 2)
                    if i == 3:
                        act.wait_ge(dve_done, D("oT3"))
                        act.activation(o16[:, :, 0, :], oT, ACT.Copy, scale=X_SCALE).then_inc(act_done, 1)
                for g in range(GROUPS):
                    for t in range(TT):
                        name = f"vd{g}{t}"
                        act.wait_ge(*Pn(name))
                        act.activation(v_d[:, t, 0, g * 512:(g + 1) * 512], bank[:, BANK[name], :], ACT.Copy,
                                       scale=X_SCALE * UNSCALE).then_inc(act_done, 1)
                    high(15 + g)
                for i in range(17):
                    if i % 2 == 1:
                        j = i // 2
                        act.wait_ge(*Pn(f"gt{j}"))
                        act.activation(gate_tiles(j), halves(BANK[f"gt{j}"]), ACT.Sigmoid, scale=UNSCALE)\
                            .then_inc(act_done, 1)
                    if i >= 1:
                        u = i - 1
                        for j in range(UNITS[u][0] + 1):
                            act.wait_ge(*Pn(f"pt{u}{j}"))
                            if j == 0 and u >= 2:
                                act.wait_ge(*Pn(f"pv{u - 2}"))
                            act.activation(probT[:, u % 2, 3 * j:3 * j + 3, 0, :], quads(BANK[f"pt{u}{j}"])[:, 0:3, :],
                                           ACT.Copy, scale=X_SCALE).then_inc(act_done, 1)
                    if i < 16:
                        w = 3 * (UNITS[i][0] + 1) * P
                        act.wait_ge(dve_done, D(f"sc{i}"))
                        act.activation(prob[:, i % 2, 0:w], prob[:, i % 2, 0:w], ACT.Exp, bias=ntop[:, i:i + 1],
                                       scale=HD ** -0.5, accum_out=psum_l[:, i:i + 1]).then_inc(act_done, 1)
                    if i in (4, 8, 12, 16):
                        high(17 + i // 4)
                high(22)
                for qt in range(TT):
                    act.wait_ge(*Pn(f"at{qt}"))
                    act.activation(att16[:, :, 0, qt * P:(qt + 1) * P], quads(BANK[f"at{qt}"]), ACT.Copy,
                                   scale=1.0 / X_SCALE).then_inc(act_done, 1)
                high(23)
                for j in range(4):
                    act.wait_ge(dve_done, D(f"ya{j}"))
                    act.activation(mix16[:, 2 * j:2 * j + 2, 0, :], mixT[:, 2 * j:2 * j + 2, :], ACT.Copy,
                                   scale=X_SCALE).then_inc(act_done, 1)
                first_pair = act.snap(passes * PAIRS)
                expert_high(first_pair, 0, first=True)
                expert_high(first_pair, 1, first=True)
                act.wait_ge(dve_done, D("ln1a"))
                act.activation(rstd[:, :], rstd[:, :], ACT.Sqrt).then_inc(act_done, 1)
                expert_high(first_pair, 2, first=True)
                x_high("x1T")
                act.wait_ge(dve_done, D("logits"))
                act.activation(e_t[:, :, :], e_t[:, :, :], ACT.Exp).then_inc(act_done, 1)
                act.activation(x16[:, 0, :, :], x_nat[:, :, :], ACT.Copy, scale=X_SCALE).then_inc(act_done, 1)
                act.activation(xacc[:, :, :], x_nat[:, :, :], ACT.Copy, scale=ALPHA).then_inc(act_done, 1)
                act.wait_ge(dve_done, D("mix3"))
                expert_high(first_pair, 3)

                def experts(q, more):
                    def x_out(r):
                        for n in range(2):
                            act.wait_ge(pe_gather, PE_GATHER.of(r)(f"x{n}"))
                            act.activation(x_pair[:, 2 * n:2 * n + 2, :, :].rearrange("p k i s -> p (k i s)"),
                                           bank[:, n, :], ACT.Copy).then_inc(act_gather, 1)

                    def y_out(done, j, signal):
                        act.wait_ge(chunk_done, done)
                        act.activation(yT[:, :, j, :], bank[:, 6, :].rearrange("p (m s) -> p m s", m=8), ACT.Copy,
                                       scale=UNSCALE).then_inc(signal, 1)

                    def slots_out(r):
                        for c in range(2):
                            act.wait_ge(pe_tail, PE_TAIL.of(r)(f"yT{c}"))
                            act.activation(yn[:, c * 512:(c + 1) * 512], bank[:, [7, 0][c], :], ACT.Copy)\
                                .then_inc(act_tail, 1)

                    def pair_steps(pair, first=False, last=False):
                        r = q * PAIRS + pair
                        before = act.snap((layer + 1) * FRONT_CHUNKS + r * PAIR_CHUNKS)
                        DR = DVE_PAIR.of(r)

                        def used(kind, j):
                            return before + (2 * PAIR_ORDER.index((kind, j)) + 2 + STAGES)

                        def silu(j):
                            act.wait_ge(chunk_done, used("gate", j))
                            act.activation(hid[:, j, :], bank[:, 4, :], ACT.Silu, scale=UNSCALE).then_inc(act_pair, 1)

                        def high_h(j):
                            act.wait_ge(dve_pair, DR(f"h{j}"))
                            act.activation(h16[:, j, 0, :], hid[:, j, :], ACT.Copy).then_inc(act_pair, 1)

                        if first:
                            expert_high(r, 4)
                            expert_high(r, 5)
                            silu(0)
                            expert_high(r, 6)
                        else:
                            y_out(before + STAGES, 1, act_tail)
                            expert_high(r, 4)
                            slots_out(r - 1)
                            silu(0)
                            expert_high(r, 5)
                        high_h(0)
                        if not first:
                            expert_high(r, 6)
                        expert_high(r, 7)
                        silu(1)
                        expert_high(r, 8)
                        expert_high(r, 9)
                        y_out(used("down", 0), 0, act_pair)
                        expert_high(r, 10)
                        expert_high(r, 11)
                        high_h(1)
                        if not last:
                            x_out(r + 1)
                            next_chunks(r)

                    def next_chunks(r):
                        for c in range(PAIR_CHUNKS, PAIR_CHUNKS + 4):
                            expert_high(r, c)

                    x_out(q * PAIRS)
                    pair_steps(0, first=True)
                    with act.Fori(1, PAIRS - 1) as pair:
                        pair_steps(pair)
                    pair_steps(PAIRS - 1, last=True)
                    y_out((layer + 1) * FRONT_CHUNKS + (q * PAIRS + PAIRS) * PAIR_CHUNKS + STAGES, 1, act_tail)
                    slots_out(q * PAIRS + (PAIRS - 1))
                    with more():
                        next_chunks(act.snap(q * PAIRS + (PAIRS - 1)))

                pass_loop(act, layer, experts, passes_reg)
                act.wait_ge(dve_done, D("ln2a"))
                act.activation(rstd[:, :], rstd[:, :], ACT.Sqrt).then_inc(act_done, 1)

        @block.vector
        def _(dve):
            V = nc.vector
            passes_reg = dve.alloc_register("dve_passes")
            dve.reg_mov(passes_reg, 0)
            dve.wait_ge(tables_landed, 48)
            ang, turns = xacc[:, 0, 0:TOK], xacc[:, 0, TOK:2 * TOK]
            V.tensor_copy(turns, cos[:, :].bitcast(I32)).then_inc(rope_done, 1)
            dve.wait_ge(rope_done, 1)
            V.tensor_scalar(ang, turns, const("inv_freq"), None, ALU.mult).then_inc(rope_done, 1)
            dve.wait_ge(rope_done, 2)
            V.tensor_scalar(turns, ang, float(1 / (2 * np.pi)), ROUND, ALU.mult, ALU.add).then_inc(rope_done, 1)
            dve.wait_ge(rope_done, 3)
            V.tensor_scalar(turns, turns, -ROUND, None, ALU.add).then_inc(rope_done, 1)
            for i, c in enumerate((TWO_PI_A, TWO_PI_B, TWO_PI_C)):
                dve.wait_ge(rope_done, 4 + i)
                V.scalar_tensor_tensor(out=ang, in0=turns, scalar=-c, in1=ang, op0=ALU.mult, op1=ALU.add)\
                    .then_inc(rope_done, 1)
            dve.wait_ge(rope_done, 7)
            V.tensor_scalar(ang, ang, 3.1415925, -3.1415925, ALU.min, ALU.max).then_inc(rope_done, 1)
            V.tensor_scalar(w_r16[:, 0, :, :], w_r, W_SCALE, None, ALU.mult).then_inc(w_r_split, 1)
            dve.wait_ge(w_r_split, 1)
            V.scalar_tensor_tensor(out=w_r16[:, 1, :, :], in0=w_r, scalar=W_SCALE, in1=w_r16[:, 0, :, :],
                                   op0=ALU.mult, op1=ALU.subtract).then_inc(w_r_split, 1)
            dve.wait_ge(setup_landed, SETUP_LOADS * 16)
            dve.sem_inc(x_ready, TT)

            with dve.Fori(0, DEPTH) as layer:
                before = dve.snap(stream_place(layer, dve.snap(passes_reg)))
                Pn, A, D = pe_steps(layer, before), ACT_PLAN.of(layer), DVE_PLAN.of(layer)

                def quads(b):
                    return bank[:, b, :].rearrange("p (k t) -> p k t", k=4)

                def own(step, n=None):
                    dve.wait_ge(dve_done, D(step, n))

                def low_part(out, src, scale):
                    hi, lo = out
                    V.scalar_tensor_tensor(out=lo, in0=src, scalar=scale, in1=hi, op0=ALU.mult, op1=ALU.subtract)\
                        .then_inc(dve_done, 1)

                def x_low(step):
                    for t in range(TT):
                        for c in range(2):
                            dve.wait_ge(act_done, A(f"{step}{t}{c}"))
                            xv = xT[:, 4 * c:4 * c + 4, :, t * P:(t + 1) * P]
                            low_part((xv[:, :, 0, :], xv[:, :, 1, :]), quads(4 * c + t), X_SCALE)

                dve.wait_ge(small_ready, layer + 1)
                V.tensor_scalar(w_a16[:, 0, :, :], w_a[:, :, :], W_SCALE, None, ALU.mult).then_inc(dve_done, 1)
                own("wa", 1)
                low_part((w_a16[:, 0, :, :], w_a16[:, 1, :, :]), w_a[:, :, :], W_SCALE)
                x_low("xT")
                low(dve, before, 0)
                low(dve, before, 1)
                dve.wait_ge(act_done, A("soft"))
                V.scalar_tensor_tensor(out=zb, in0=zb, scalar=0.0, in1=lb, op0=ALU.min, op1=ALU.subtract)\
                    .then_inc(dve_done, 1)
                own("scan", 1)
                for h in range(HEADS):
                    V.tensor_tensor_scan(lb[:, h, :], const("keep"), zb[:, h, :], 0.0, ALU.mult, ALU.add)\
                        .then_inc(dve_done, 1)
                own("scan", 5)
                lb_c = lb.rearrange("p h (n c) -> p (h n) c", c=CHUNK)
                V.tensor_tensor(zb.rearrange("p h (n c) -> p (h n) c", c=CHUNK),
                                lb_c[:, :, CHUNK - 1:CHUNK].to_broadcast([P, HEADS * NCH, CHUNK]), lb_c, ALU.subtract)\
                    .then_inc(dve_done, 1)
                dve.wait_ge(act_done, A("decay"))
                V.tensor_copy(dec[:, :, :], q_t.rearrange("p h (n c) -> p h n c", c=CHUNK)[:, :, :, CHUNK - 1])\
                    .then_inc(dve_done, 1)
                low(dve, before, 2)
                own("last")
                for j in range(2):
                    dve.wait_ge(*Pn(f"q{j}"))
                    qv = q_t[:, 2 * j:2 * j + 2, :]
                    V.scalar_tensor_tensor(out=qv, in0=halves(4 + j), scalar=DK ** -0.5 * UNSCALE, in1=qv, op0=ALU.mult,
                                           op1=ALU.mult).then_inc(dve_done, 1)
                low(dve, before, 3)
                for j in range(2):
                    dve.wait_ge(*Pn(f"k{j}"))
                    for dst in (k_t, zb):
                        kv = dst[:, 2 * j:2 * j + 2, :]
                        V.scalar_tensor_tensor(out=kv, in0=halves(6 + j), scalar=UNSCALE, in1=kv, op0=ALU.mult,
                                               op1=ALU.mult).then_inc(dve_done, 1)
                for c in range(4, 8):
                    low(dve, before, c)
                dve.wait_ge(zeroed, layer + 1)
                for t in range(TT):
                    dve.wait_ge(*Pn(f"att{t}"))
                    apart(dve)
                    V.copy_predicated(attm[:, t, :, :], const("causal").bitcast(U32).unsqueeze(1)
                                      .to_broadcast([P, HEADS, P]), quads(4 + t)).then_inc(dve_done, 1)
                for c in range(NCH - 1):
                    for j in range(2):
                        dve.wait_ge(*Pn(f"upd{c}{j}"))
                        if c == 0:
                            V.tensor_copy(state[:, 0, 2 * j:2 * j + 2, :], halves(6 + j)).then_inc(dve_done, 1)
                        else:
                            own(f"upd{c - 1}{j}")
                            for i in range(2):
                                h = 2 * j + i
                                V.scalar_tensor_tensor(out=state[:, c, h, :], in0=state[:, c - 1, h, :],
                                                       scalar=dec[:, h, c:c + 1], in1=bank[:, 6 + j, i * DV:(i + 1) * DV],
                                                       op0=ALU.mult, op1=ALU.add).then_inc(dve_done, 1)
                dve.wait_ge(act_done, A("sq3"))
                V.tensor_scalar(rms[:, :], rms[:, :], 1.0 / DV, RMS_EPS, ALU.mult, ALU.add).then_inc(dve_done, 1)
                dve.wait_ge(act_done, A("rms"))
                V.reciprocal(rms[:, :], rms[:, :]).then_inc(dve_done, 1)
                own("rms")
                for h in range(HEADS):
                    V.tensor_scalar(o_n[:, 1, h * DV:(h + 1) * DV], bank[:, 6 + h // 2, (h % 2) * DV:(h % 2 + 1) * DV],
                                    rms[:, HEADS + h:HEADS + h + 1], None, ALU.mult).then_inc(dve_done, 1)
                cosb = cos[:, :].unsqueeze(1).to_broadcast([P, 2, TOK])
                sinb = sin[:, :].unsqueeze(1).to_broadcast([P, 2, TOK])
                for i in range(12):
                    dst = qk[:, 2 * i:2 * i + 2, :]
                    dve.wait_ge(act_done, A(f"raw{i}"))
                    if i:
                        own(f"rope{i - 1}")
                    V.tensor_tensor(dst, raw[:, i % 2, :, :], cosb, ALU.mult).then_inc(dve_done, 1)
                    V.tensor_tensor(rtmp, turned[:, i % 2, :, :], sinb, ALU.mult).then_inc(dve_done, 1)
                    own(f"rope{i}", 2)
                    V.tensor_tensor(dst, dst, rtmp, ALU.add).then_inc(dve_done, 1)
                    if i == 0:
                        low(dve, before, 8)
                    if i % 2 == 1:
                        low(dve, before, 9 + i // 2)
                    if i == 1:
                        dve.wait_ge(act_done, A("r3"))
                        for b in range(4):
                            dve.wait_ge(*Pn(f"oT{b}"))
                            for m in range(2 * b, 2 * b + 2):
                                V.scalar_tensor_tensor(out=oT[:, m, :], in0=bank[:, 4 + b, (m % 2) * TOK:(m % 2 + 1) * TOK],
                                                       scalar=gnorm[:, m:m + 1], in1=oT[:, m, :],
                                                       op0=ALU.mult, op1=ALU.mult).then_inc(dve_done, 1)
                    if i == 3:
                        dve.wait_ge(act_done, A("o_hi"))
                        low_part((o16[:, :, 0, :], o16[:, :, 1, :]), oT, X_SCALE)
                for g in range(GROUPS):
                    for t in range(TT):
                        name = f"vd{g}{t}"
                        dve.wait_ge(act_done, A(name))
                        vv = v_d[:, t, :, g * 512:(g + 1) * 512]
                        low_part((vv[:, 0, :], vv[:, 1, :]), bank[:, BANK[name], :], X_SCALE * UNSCALE)
                    if g < 2:
                        low(dve, before, 15 + g)
                own("rope11")

                def attention_out(qt):
                    dve.wait_ge(act_done, A(f"ex{8 * qt + 7}"))
                    V.reciprocal(rl[:, 8 * qt:8 * qt + 8], psum_l[:, 8 * qt:8 * qt + 8]).then_inc(dve_done, 1)
                    dve.wait_ge(*Pn(f"pv{8 * qt + 7}"))
                    own(f"an{qt}", 1)
                    V.tensor_tensor(att_n[:, qt, :].rearrange("p (h e) -> p h e", h=AH),
                                    bank[:, 3, :].rearrange("p (h e) -> p h e", h=AH),
                                    rl[:, 8 * qt:8 * qt + 8].unsqueeze(2).to_broadcast([P, AH, HD]), ALU.mult)\
                        .then_inc(dve_done, 1)

                def probabilities_low(u):
                    for j in range(UNITS[u][0] + 1):
                        dve.wait_ge(act_done, A(f"pt{u}", j + 1))
                        pv = probT[:, u % 2, 3 * j:3 * j + 3, :, :]
                        low_part((pv[:, :, 0, :], pv[:, :, 1, :]), quads(BANK[f"pt{u}{j}"])[:, 0:3, :], X_SCALE)

                for i, (qt, h) in enumerate(UNITS):
                    if i >= 2:
                        probabilities_low(i - 2)
                    nk = (qt + 1) * P
                    b = 4 + 2 * (i % 2)
                    dve.wait_ge(*Pn(f"S{i}"))
                    if i >= 2:
                        dve.wait_ge(*Pn(f"pt{i - 2}{UNITS[i - 2][0]}"))
                    apart(dve)
                    scores = bank[:, b:b + 2, :].rearrange("p b (g k) -> p (b g) k", g=2)[:, 0:3, 0:nk]
                    mask = const("mask").rearrange("p (g k) -> p g k", g=3)[:, :, TOK - nk:TOK]
                    V.tensor_tensor_reduce(prob[:, i % 2, 0:3 * nk].rearrange("p (g k) -> p g k", g=3), scores, mask,
                                           1.0, -3e38, ALU.add, ALU.max, top[:, i:i + 1]).then_inc(dve_done, 1)
                    own(f"sc{i}", 1)
                    V.tensor_scalar(ntop[:, i:i + 1], top[:, i:i + 1], -(HD ** -0.5), None, ALU.mult)\
                        .then_inc(dve_done, 1)
                    if i in (1, 5, 9, 13):
                        low(dve, before, 17 + i // 4)
                    if i == 10:
                        attention_out(0)
                probabilities_low(14)
                probabilities_low(15)
                attention_out(1)
                low(dve, before, 21)
                for j in range(4):
                    dve.wait_ge(*Pn(f"yg{j}"))
                    dve.wait_ge(act_done, A(f"gt{j}"))
                    V.scalar_tensor_tensor(out=mixT[:, 2 * j:2 * j + 2, :], in0=halves(4 + j), scalar=UNSCALE,
                                           in1=gate_tiles(j), op0=ALU.mult, op1=ALU.mult).then_inc(dve_done, 1)
                    if j == 2:
                        for qt in range(TT):
                            dve.wait_ge(act_done, A(f"at{qt}"))
                            av = att16[:, :, :, qt * P:(qt + 1) * P]
                            low_part((av[:, :, 0, :], av[:, :, 1, :]), quads(BANK[f"at{qt}"]), 1.0 / X_SCALE)
                    if j % 2 == 1:
                        low(dve, before, 22 + j // 2)

                def attention_branch(j):
                    dve.wait_ge(*Pn(f"ya{j}"))
                    dve.wait_ge(act_done, A(f"gt{4 + j}"))
                    own("yg3") if j == 0 else own(f"ya{j - 1}")
                    V.scalar_tensor_tensor(out=mtmp, in0=halves(4 + j), scalar=UNSCALE,
                                           in1=gate_tiles(4 + j), op0=ALU.mult, op1=ALU.mult).then_inc(dve_done, 1)
                    own(f"ya{j}", 1)
                    V.tensor_tensor(mixT[:, 2 * j:2 * j + 2, :], mixT[:, 2 * j:2 * j + 2, :], mtmp, ALU.add)\
                        .then_inc(dve_done, 1)

                def mix_low(j):
                    dve.wait_ge(act_done, A(f"mix{j}"))
                    mv_ = mix16[:, 2 * j:2 * j + 2, :, :]
                    low_part((mv_[:, :, 0, :], mv_[:, :, 1, :]), mixT[:, 2 * j:2 * j + 2, :], X_SCALE)

                attention_branch(0)
                attention_branch(1)
                mix_low(0)
                attention_branch(2)
                mix_low(1)
                attention_branch(3)
                mix_low(2)
                mix_low(3)
                experts_before = dve.snap(before + FRONT_CHUNKS)
                low(dve, experts_before, 0, DEEP)
                dve.wait_ge(act_done, A("alpha_x"))
                for c in range(2):
                    for t in range(TT):
                        dve.wait_ge(*Pn(f"mo{c}{t}"))
                        xv = x_nat[:, t, c * 512:(c + 1) * 512]
                        V.scalar_tensor_tensor(out=xv, in0=bank[:, 4 + 2 * c + t, :], scalar=UNSCALE, in1=xv,
                                               op0=ALU.mult, op1=ALU.add).then_inc(dve_done, 1)
                        own(f"mo{c}{t}", 1)
                        V.bn_stats(stats[:, t, c, :], xv).then_inc(dve_done, 1)
                    if c == 0:
                        low(dve, experts_before, 1, DEEP)

                def layer_norm(w, src, params_landed):
                    if w == "ln1":
                        own(w + "a", 0)
                    else:
                        dve.wait_ge(stats_taken, dve.snap(passes_reg) * (2 * TT))
                    apart(dve)
                    for t in range(TT):
                        V.bn_aggr(mv[:, t, :], stats[:, t, :, :].rearrange("p c s -> p (c s)")).then_inc(dve_done, 1)
                    own(w + "a", 2)
                    V.tensor_scalar(rstd[:, :], mv[:, :, 1], LN_EPS, None, ALU.add).then_inc(dve_done, 1)
                    dve.wait_ge(act_done, A(w))
                    V.reciprocal(rstd[:, :], rstd[:, :]).then_inc(dve_done, 1)
                    own(w + "r")
                    dve.wait_ge(params_landed, (layer + 1) * 32)
                    for t in range(TT):
                        xv = x_nat[:, t, :]
                        V.scalar_tensor_tensor(out=xv, in0=src[:, t, :], scalar=mv[:, t, 0:1], in1=lnp[:, 0, :],
                                               op0=ALU.subtract, op1=ALU.mult).then_inc(dve_done, 1)
                        own(f"{w}n{t}", 1)
                        V.scalar_tensor_tensor(out=xv, in0=xv, scalar=rstd[:, t:t + 1], in1=lnp[:, 1, :],
                                               op0=ALU.mult, op1=ALU.add).then_inc(dve_done, 1)
                        if w == "ln2":
                            own(f"{w}n{t}")
                            dve.sem_inc(x_ready, 1)

                layer_norm("ln1", x_nat, ln1_landed)
                x_low("x1T")

                two_b = two[:, 0:2].unsqueeze(2).to_broadcast([P, TT, E])
                dve.wait_ge(*Pn("logits"))
                V.scalar_tensor_tensor(out=e_t[:, :, :], in0=bank[:, 6, 0:TT * E].rearrange("p (t e) -> p t e", t=TT),
                                       scalar=UNSCALE, in1=b_r[:, :].unsqueeze(1).to_broadcast([P, TT, E]),
                                       op0=ALU.mult, op1=ALU.add).then_inc(dve_done, 1)
                own("logits", 1)
                V.tensor_reduce(two[:, 0:2], e_t[:, :, :], AX.X, ALU.max).then_inc(dve_done, 1)
                own("logits", 2)
                V.tensor_tensor(e_t[:, :, :], e_t[:, :, :], two_b, ALU.subtract).then_inc(dve_done, 1)
                dve.wait_ge(act_done, A("router"))
                e_f = e_t[:, :, :].rearrange("p t e -> p (t e)")
                n = 0

                def gate_step(ins):
                    ins.then_inc(dve_done, 1)

                def places(v, groups):
                    v4 = v.rearrange("p (g i) -> p g i", i=EG)
                    first = v4.unsqueeze(3).to_broadcast([P, groups, EG, EG])
                    other = v4.unsqueeze(2).to_broadcast([P, groups, EG, EG])
                    a = cmp_a[:, 0:groups * 16].rearrange("p (g i j) -> p g i j", i=EG, j=EG)
                    b = cmp_b[:, 0:groups * 16].rearrange("p (g i j) -> p g i j", i=EG, j=EG)
                    return first, other, a, b

                sel_f = sel[:, :, :].rearrange("p t e -> p (t e)")
                rk_f = rk[:, :, :].rearrange("p t e -> p (t e)")
                for v, groups, dst, limit, base in ((e_f, 8, rk_f, 1.5, 0), (g_s[:, :], 2, g_r[:, :], 0.5, 8)):
                    first, other, a, b = places(v, groups)
                    if base:
                        own("gate", base)
                    V.tensor_tensor(a, other, first, ALU.is_gt).then_inc(dve_done, 1)
                    V.tensor_tensor(b, other, first, ALU.is_equal).then_inc(dve_done, 1)
                    own("gate", base + 2)
                    bf = cmp_b[:, 0:groups * 16].rearrange("p (g c) -> p g c", g=groups)
                    V.tensor_tensor(bf, bf, const("lower").unsqueeze(1).to_broadcast([P, groups, 16]), ALU.mult)\
                        .then_inc(dve_done, 1)
                    own("gate", base + 3)
                    af = cmp_a[:, 0:groups * 16]
                    V.tensor_tensor(af, af, cmp_b[:, 0:groups * 16], ALU.add).then_inc(dve_done, 1)
                    own("gate", base + 4)
                    V.tensor_reduce(dst, af.rearrange("p (c j) -> p c j", j=EG), AX.X, ALU.add).then_inc(dve_done, 1)
                    own("gate", base + 5)
                    V.tensor_scalar(dst, dst, limit, None, ALU.is_lt).then_inc(dve_done, 1)
                    own("gate", base + 6)
                    if base == 0:
                        V.tensor_tensor(e_f, e_f, rk_f, ALU.mult).then_inc(dve_done, 1)
                        own("gate", 7)
                        V.tensor_reduce(g_s[:, :], e_f.rearrange("p (g i) -> p g i", i=EG), AX.X, ALU.add)\
                            .then_inc(dve_done, 1)
                in_group = g_r[:, :].unsqueeze(2).to_broadcast([P, 8, EG])
                g4 = dict(i=EG)
                V.tensor_tensor(sel_f.rearrange("p (g i) -> p g i", **g4), rk_f.rearrange("p (g i) -> p g i", **g4),
                                in_group, ALU.mult).then_inc(dve_done, 1)
                V.tensor_tensor(e_f.rearrange("p (g i) -> p g i", **g4), e_f.rearrange("p (g i) -> p g i", **g4),
                                in_group, ALU.mult).then_inc(dve_done, 1)
                own("gate", 16)
                V.tensor_reduce(two[:, 2:4], e_t[:, :, :], AX.X, ALU.add).then_inc(dve_done, 1)
                own("gate", 17)
                V.reciprocal(two[:, 0:2], two[:, 2:4]).then_inc(dve_done, 1)
                own("gate", 18)
                V.tensor_tensor(comb[:, :, :], e_t[:, :, :], two_b, ALU.mult).then_inc(dve_done, 1)
                dve.wait_ge(act_done, A("x_hi"))
                low_part((x16[:, 0, :, :], x16[:, 1, :, :]), x_nat[:, :, :], X_SCALE)
                dve.wait_ge(*Pn("rank"))
                V.scalar_tensor_tensor(out=pm[:, :, :], in0=bank[:, 7, 0:TT * E].rearrange("p (t e) -> p t e", t=TT),
                                       scalar=1.0, in1=sel[:, :, :], op0=ALU.add, op1=ALU.mult).then_inc(dve_done, 1)
                own("rank", 1)
                V.tensor_scalar(pm[:, :, :], pm[:, :, :], -1.0, None, ALU.add).then_inc(dve_done, 1)
                V.tensor_reduce(lim[:, 0:1], bank[0:1, 7, 2 * E:3 * E], AX.X, ALU.max).then_inc(dve_done, 1)
                own("passes", 1)
                V.tensor_scalar(lim[:, 1:4], const("limits", 1), lim[:, 0:1], None, ALU.is_lt).then_inc(dve_done, 1)
                own("passes", 2)
                V.tensor_reduce(lim[:, 0:1], lim[:, 1:4], AX.X, ALU.add).then_inc(dve_done, 1)
                own("passes", 3)
                V.tensor_scalar(passes_sb[:, :], lim[:, 0:1], 1.0, None, ALU.add).then_inc(dve_done, 1)
                def experts(q, more):
                    def add_y(r, last=False):
                        for t in range(TT):
                            for c in range(2):
                                dve.wait_ge(pe_tail, PE_TAIL.of(r)(f"y{t}{c}"))
                                xv = xacc[:, t, c * 512:(c + 1) * 512]
                                V.tensor_tensor(xv, xv, bank[:, [1, 2, 3, 7][2 * t + c], :], ALU.add)\
                                    .then_inc(dve_tail, 1)
                                if last:
                                    dve.wait_ge(dve_tail, DVE_TAIL.of(r)(f"y{t}{c}"))
                                    V.bn_stats(stats[:, t, c, :], xv).then_inc(stats_taken, 1)

                    def select(pair):
                        shape = [P, TT, 2, SLOTS]
                        of_pair = (slice(None), slice(None), bass.ds(pair * 2, 2))
                        V.tensor_tensor(S_pair, const("slot").unsqueeze(1).unsqueeze(1).to_broadcast(shape),
                                        pm[of_pair].unsqueeze(3).to_broadcast(shape), ALU.is_equal)\
                            .then_inc(dve_gather, 1)
                        dve.wait_ge(dve_gather, DVE_GATHER.of(q * PAIRS + pair)("S"))
                        V.tensor_tensor(S_gated, S_pair, comb[of_pair].unsqueeze(3).to_broadcast(shape), ALU.mult)\
                            .then_inc(dve_gather, 1)

                    def x_out(r):
                        for n in range(2, 4):
                            dve.wait_ge(pe_gather, PE_GATHER.of(r)(f"x{n}"))
                            V.tensor_copy(x_pair[:, 2 * n:2 * n + 2, :, :].rearrange("p k i s -> p (k i s)"),
                                          bank[:, n, :]).then_inc(dve_gather, 1)

                    def pair_steps(pair, first=False, last=False):
                        r = q * PAIRS + pair
                        before = dve.snap((layer + 1) * FRONT_CHUNKS + r * PAIR_CHUNKS)
                        AR = ACT_PAIR.of(r)

                        def hidden(j):
                            dve.wait_ge(chunk_done, before + (2 * PAIR_ORDER.index(("up", j)) + 2 + STAGES))
                            dve.wait_ge(act_pair, AR(f"silu{j}"))
                            V.scalar_tensor_tensor(out=hid[:, j, :], in0=bank[:, 5, :], scalar=UNSCALE * X_SCALE,
                                                   in1=hid[:, j, :], op0=ALU.mult, op1=ALU.mult).then_inc(dve_pair, 1)

                        def low_h(j):
                            dve.wait_ge(act_pair, AR(f"hh{j}"))
                            V.tensor_tensor(h16[:, j, 1, :], hid[:, j, :], h16[:, j, 0, :], ALU.subtract)\
                                .then_inc(dve_pair, 1)

                        for c in range(3, 5):
                            low(dve, before, c, DEEP)
                        low(dve, before, 5, DEEP)
                        hidden(0)
                        low_h(0)
                        if not first:
                            add_y(r - 1)
                        dve.wait_ge(pe_gather, PE_GATHER.of(r)("gT"))
                        V.tensor_copy(G_pair[:, :], bank[:, 0, 0:TOK]).then_inc(dve_tail, 1)
                        for c in range(6, 9):
                            low(dve, before, c, DEEP)
                        if not last:
                            select(pair + 1)
                        low(dve, before, 9, DEEP)
                        low(dve, before, 10, DEEP)
                        hidden(1)
                        if not last:
                            x_out(r + 1)
                        low_h(1)
                        low(dve, before, 11, DEEP)
                        if not last:
                            next_chunks(before)

                    def next_chunks(before):
                        for c in range(PAIR_CHUNKS, PAIR_CHUNKS + 3):
                            low(dve, before, c, DEEP)

                    dve.wait_ge(split_done, (layer + 1) * FRONT_CHUNKS + q * (PAIRS * PAIR_CHUNKS) + (3 + STAGES))
                    own("rank")
                    dve.wait_ge(act_done, A("xacc"))
                    select(0)
                    x_out(q * PAIRS)
                    pair_steps(0, first=True)
                    with dve.Fori(1, PAIRS - 1) as pair:
                        pair_steps(pair)
                    pair_steps(PAIRS - 1, last=True)
                    last = q * PAIRS + (PAIRS - 1)
                    add_y(last, last=True)
                    V.tensor_scalar(pm[:, :, :], pm[:, :, :], float(-SLOTS), None, ALU.add).then_inc(pass_over, 1)
                    dve.wait_ge(dve_tail, DVE_TAIL.of(last)("y11"))
                    apart(dve)
                    dve.wait_ge(pass_over, q + 1)
                    apart(dve)
                    with more():
                        next_chunks(dve.snap((layer + 1) * FRONT_CHUNKS + (q * PAIRS + (PAIRS - 1)) * PAIR_CHUNKS))

                pass_loop(dve, layer, experts, passes_reg)
                layer_norm("ln2", xacc, ln2_landed)


_INS = ["x", "positions", "w_in", "w_alpha_up", "b_alpha", "gla_norm", "w_gla_o", "w_att_o", "w_out", "ln1_g", "ln1_b",
        "w_router", "b_router", "w_e_gate", "w_e_up", "w_e_down", "ln2_g", "ln2_b"]


def kernel(**inputs):
    import concourse.bacc as bacc
    from concourse.bass_utils import run_bass_kernel_spmd as run

    nc = bacc.Bacc("TRN2", target_bir_lowering=False, num_devices=1)
    arrays, args = {}, []
    for name in _INS + ["constants"]:
        a = constant_table() if name == "constants" else np.ascontiguousarray(inputs[name])
        arrays[f"in_{name}"] = a
        args.append(nc.dram_tensor(f"in_{name}", a.shape, mybir.dt.from_np(a.dtype), kind="ExternalInput").ap())
    out = nc.dram_tensor("out_0", (1, TOK, DM), F32, kind="ExternalOutput").ap()
    build(nc, *args, out)
    r = run(nc, [arrays], core_ids=[0])
    return r.results[0]["out_0"]
```
